# Optimizing a Trainium2 kernel written in Bass

```python
import jax, jax.numpy as jnp
from jax import lax
import numpy as np

D_MODEL = 1024
BATCH = 1
SEQ = 512
DEPTH = 1

CTX_LEN = 256
GRID_W = 64
N_HEADS = 8
HEAD_DIM = 64
D_ATT = N_HEADS * HEAD_DIM
WIN_ROWS_MAX = 8
WIN_COLS = 16
D_CONV = 512
CONV_WIDTH = 31
N_GROUPS = 4
EXPERTS_PER_GROUP = 8
N_EXPERTS = N_GROUPS * EXPERTS_PER_GROUP
TOP_K_IN_GROUP = 2
D_EXPERT = 512
MOE_BLOCK = 128
NORM_EPS = 1e-6
NEG_INF = -1e30

Q0 = 0
K0 = Q0 + D_ATT
V0 = K0 + D_ATT
GLU0 = V0 + D_ATT
GA0 = GLU0 + 2 * D_CONV
GB0 = GA0 + D_MODEL
D_IN = GB0 + D_MODEL


def rmsnorm(x, g):
    xf = x.astype(jnp.float32)
    y = xf * lax.rsqrt(jnp.mean(xf * xf, axis=-1, keepdims=True) + NORM_EPS)
    return (y * g.astype(jnp.float32)).astype(x.dtype)

def layernorm(x, g, b):
    xf = x.astype(jnp.float32)
    mu = jnp.mean(xf, axis=-1, keepdims=True)
    var = jnp.mean(jnp.square(xf - mu), axis=-1, keepdims=True)
    y = (xf - mu) * lax.rsqrt(var + NORM_EPS)
    return (y * g.astype(jnp.float32) + b.astype(jnp.float32)).astype(x.dtype)

def modulate(h, shift, scale):
    return h * (1 + scale) + shift

def split_heads(t):
    return t.reshape(t.shape[0], t.shape[1], N_HEADS, HEAD_DIM)

def latent_neighbourhood_attention(q, k, v, k_ctx, v_ctx, rpb):
    B, N, H, hd = q.shape
    rows = N // GRID_W
    kh = min(WIN_ROWS_MAX, rows)
    scale = hd ** -0.5
    q_rows = q.reshape(B, rows, GRID_W, H, hd).transpose(1, 0, 3, 2, 4)
    k_grid = k.reshape(B, rows, GRID_W, H, hd).transpose(0, 3, 1, 2, 4)
    v_grid = v.reshape(B, rows, GRID_W, H, hd).transpose(0, 3, 1, 2, 4)
    cq = jnp.arange(GRID_W)[:, None]
    ck = jnp.arange(GRID_W)[None, :]
    c_start = jnp.clip(cq - WIN_COLS // 2, 0, GRID_W - WIN_COLS)
    col_mask = (ck >= c_start) & (ck < c_start + WIN_COLS)
    band_mask = jnp.broadcast_to(col_mask[:, None, :], (GRID_W, kh, GRID_W)).reshape(GRID_W, kh * GRID_W)
    dc_idx = jnp.clip(ck - cq + WIN_COLS - 1, 0, 2 * WIN_COLS - 2)
    rpb_cols = rpb[:, :, dc_idx]

    def row_block(args):
        q_r, r = args
        r_start = jnp.clip(r - kh // 2, 0, rows - kh)
        k_blk = lax.dynamic_slice_in_dim(k_grid, r_start, kh, axis=2).reshape(B, H, kh * GRID_W, hd)
        v_blk = lax.dynamic_slice_in_dim(v_grid, r_start, kh, axis=2).reshape(B, H, kh * GRID_W, hd)
        dr_idx = r_start + jnp.arange(kh) - r + WIN_ROWS_MAX - 1
        bias = jnp.take(rpb_cols, dr_idx, axis=1)
        bias = bias.transpose(0, 2, 1, 3).reshape(H, GRID_W, kh * GRID_W).astype(jnp.float32)
        s_loc = jnp.einsum('bhqd,bhkd->bhqk', q_r, k_blk, preferred_element_type=jnp.float32) * scale + bias
        s_loc = jnp.where(band_mask, s_loc, NEG_INF)
        s_ctx = jnp.einsum('bhqd,bhkd->bhqk', q_r, k_ctx, preferred_element_type=jnp.float32) * scale
        p = jax.nn.softmax(jnp.concatenate([s_loc, s_ctx], axis=-1), axis=-1).astype(v.dtype)
        n_loc = kh * GRID_W
        return (jnp.einsum('bhqk,bhkd->bhqd', p[..., :n_loc], v_blk)
                + jnp.einsum('bhqk,bhkd->bhqd', p[..., n_loc:], v_ctx))

    o = lax.map(row_block, (q_rows, jnp.arange(rows)))
    return o.transpose(1, 0, 3, 2, 4).reshape(B, N, H * hd)

def context_attention(q_c, k_c, v_c):
    s = jnp.einsum('bhqd,bhkd->bhqk', q_c, k_c, preferred_element_type=jnp.float32) * (HEAD_DIM ** -0.5)
    p = jax.nn.softmax(s, axis=-1).astype(v_c.dtype)
    o = jnp.einsum('bhqk,bhkd->bhqd', p, v_c)
    return o.transpose(0, 2, 1, 3).reshape(q_c.shape[0], q_c.shape[2], D_ATT)

def conformer_conv(glu_in, conv_w, conv_b, ln_g, ln_b, w_out):
    a, g = jnp.split(glu_in, 2, axis=-1)
    u = a * jax.nn.sigmoid(g)
    y = lax.conv_general_dilated(u, conv_w[:, None, :].astype(u.dtype), window_strides=(1,),
                                 padding=[(CONV_WIDTH // 2, CONV_WIDTH // 2)],
                                 dimension_numbers=('NWC', 'WIO', 'NWC'),
                                 feature_group_count=D_CONV) + conv_b
    y = jax.nn.silu(layernorm(y, ln_g, ln_b))
    return y @ w_out

def merge_branches(proj, att, conv_w, conv_b, ln_g, ln_b, w_att_out, w_conv_out, w_o):
    y_att = att @ w_att_out
    y_conv = conformer_conv(proj[..., GLU0:GA0], conv_w, conv_b, ln_g, ln_b, w_conv_out)
    gate_att = jax.nn.sigmoid(proj[..., GA0:GB0])
    gate_conv = jax.nn.sigmoid(proj[..., GB0:D_IN])
    return (gate_att * y_att + gate_conv * y_conv) @ w_o

def hierarchical_moe(h, w_rg, b_rg, w_re, b_re, w_g, w_u, w_d):
    T, D = h.shape
    hf = h.astype(jnp.float32)
    g_logits = hf @ w_rg.astype(jnp.float32) + b_rg.astype(jnp.float32)
    g_idx = jnp.argmax(g_logits, axis=-1)
    p_group = jnp.take_along_axis(jax.nn.softmax(g_logits, axis=-1), g_idx[:, None], axis=-1)
    e_logits = (hf @ w_re.astype(jnp.float32) + b_re.astype(jnp.float32)).reshape(T, N_GROUPS, EXPERTS_PER_GROUP)
    e_sel = jnp.take_along_axis(e_logits, g_idx[:, None, None], axis=1)[:, 0]
    top_v, top_i = lax.top_k(e_sel, TOP_K_IN_GROUP)
    gate = p_group * jax.nn.softmax(top_v, axis=-1)
    flat_e = (g_idx[:, None] * EXPERTS_PER_GROUP + top_i).reshape(-1)
    flat_tok = jnp.repeat(jnp.arange(T), TOP_K_IN_GROUP)
    flat_w = gate.reshape(-1)
    A = T * TOP_K_IN_GROUP
    order = jnp.argsort(flat_e)
    e_s, tok_s, w_s = flat_e[order], flat_tok[order], flat_w[order]
    counts = jnp.bincount(flat_e, length=N_EXPERTS)
    padded = (counts + MOE_BLOCK - 1) // MOE_BLOCK * MOE_BLOCK
    pad_end = jnp.cumsum(padded)
    pad_start = pad_end - padded
    start = jnp.cumsum(counts) - counts
    dest = pad_start[e_s] + (jnp.arange(A) - start[e_s])
    n_blocks = -(-A // MOE_BLOCK) + N_EXPERTS
    P = n_blocks * MOE_BLOCK
    row_tok = jnp.zeros((P,), jnp.int32).at[dest].set(tok_s.astype(jnp.int32))
    row_w = jnp.zeros((P,), jnp.float32).at[dest].set(w_s)
    block_e = jnp.clip(jnp.searchsorted(pad_end, jnp.arange(n_blocks) * MOE_BLOCK, side='right'), 0, N_EXPERTS - 1)

    def run_block(args):
        tok, e, wt = args
        xb = h[tok]
        y = (jax.nn.silu(xb @ w_g[e]) * (xb @ w_u[e])) @ w_d[e]
        return y.astype(jnp.float32) * wt[:, None]

    ys = lax.map(run_block, (row_tok.reshape(n_blocks, MOE_BLOCK), block_e, row_w.reshape(n_blocks, MOE_BLOCK)))
    out = jnp.zeros((T, D), jnp.float32).at[row_tok].add(ys.reshape(P, D))
    return out.astype(h.dtype)

def first_inputs(seed: int = 0) -> dict:
    key = jax.random.key(seed)
    ks = jax.random.split(key, 25)
    L, D = DEPTH, D_MODEL

    def nrm(k, shape, s):
        return jax.random.normal(k, shape, jnp.float32) * s

    return {
        "x": nrm(ks[0], (BATCH, SEQ, D), 1.0),
        "c": nrm(ks[1], (BATCH, D), 1.0),
        "ctx": nrm(ks[2], (BATCH, CTX_LEN, D), 1.0),
        "c_ctx": nrm(ks[3], (D,), 1.0),
        "w_mod": nrm(ks[4], (L, D, 6 * D), 0.5 * D ** -0.5),
        "b_mod": nrm(ks[5], (L, 6 * D), 0.01),
        "norm_mix": 1.0 + nrm(ks[6], (L, D), 0.02),
        "w_in": nrm(ks[7], (L, D, D_IN), D ** -0.5),
        "rpb": nrm(ks[8], (L, N_HEADS, 2 * WIN_ROWS_MAX - 1, 2 * WIN_COLS - 1), 0.1),
        "w_att_out": nrm(ks[9], (L, D_ATT, D), D_ATT ** -0.5),
        "conv_w": nrm(ks[10], (L, CONV_WIDTH, D_CONV), CONV_WIDTH ** -0.5),
        "conv_b": nrm(ks[11], (L, D_CONV), 0.01),
        "conv_ln_g": 1.0 + nrm(ks[12], (L, D_CONV), 0.02),
        "conv_ln_b": nrm(ks[13], (L, D_CONV), 0.01),
        "w_conv_out": nrm(ks[14], (L, D_CONV, D), D_CONV ** -0.5),
        "w_o": nrm(ks[15], (L, D, D), D ** -0.5),
        "norm_ffn": 1.0 + nrm(ks[16], (L, D), 0.02),
        "w_router_group": nrm(ks[17], (L, D, N_GROUPS), D ** -0.5),
        "b_router_group": nrm(ks[18], (L, N_GROUPS), 0.01),
        "w_router_expert": nrm(ks[19], (L, D, N_EXPERTS), D ** -0.5),
        "b_router_expert": nrm(ks[20], (L, N_EXPERTS), 0.01),
        "w_exp_gate": nrm(ks[21], (L, N_EXPERTS, D, D_EXPERT), D ** -0.5),
        "w_exp_up": nrm(ks[22], (L, N_EXPERTS, D, D_EXPERT), D ** -0.5),
        "w_exp_down": nrm(ks[23], (L, N_EXPERTS, D_EXPERT, D), D_EXPERT ** -0.5),
        "final_norm": 1.0 + nrm(ks[24], (D,), 0.02),
    }

def first_block(x, c, ctx, c_ctx, w_mod, b_mod, norm_mix, w_in, rpb, w_att_out, conv_w, conv_b,
              conv_ln_g, conv_ln_b, w_conv_out, w_o, norm_ffn, w_router_group, b_router_group,
              w_router_expert, b_router_expert, w_exp_gate, w_exp_up, w_exp_down, final_norm):
    B, N, D = x.shape
    n_ctx = ctx.shape[1]
    for l in range(DEPTH):
        last = l == DEPTH - 1
        m_lat = jax.nn.silu(c) @ w_mod[l] + b_mod[l]
        sh1, sc1, g1, sh2, sc2, g2 = jnp.split(m_lat[:, None, :], 6, axis=-1)
        m_ctx = jax.nn.silu(c_ctx) @ w_mod[l] + b_mod[l]
        sh1c, sc1c, g1c, sh2c, sc2c, g2c = jnp.split(m_ctx, 6, axis=-1)

        h = modulate(rmsnorm(x, norm_mix[l]), sh1, sc1)
        hc = modulate(rmsnorm(ctx, norm_mix[l]), sh1c, sc1c)
        proj = h @ w_in[l]
        q = split_heads(proj[..., Q0:K0])
        k = split_heads(proj[..., K0:V0])
        v = split_heads(proj[..., V0:GLU0])
        if last:
            kv_c = hc @ w_in[l][:, K0:GLU0]
            proj_c = None
        else:
            proj_c = hc @ w_in[l]
            kv_c = proj_c[..., K0:GLU0]
        k_c = split_heads(kv_c[..., :D_ATT]).transpose(0, 2, 1, 3)
        v_c = split_heads(kv_c[..., D_ATT:]).transpose(0, 2, 1, 3)
        att = latent_neighbourhood_attention(q, k, v, k_c, v_c, rpb[l])
        y = merge_branches(proj, att, conv_w[l], conv_b[l], conv_ln_g[l], conv_ln_b[l],
                           w_att_out[l], w_conv_out[l], w_o[l])
        x_mid = x + g1 * y
        h2 = modulate(rmsnorm(x_mid, norm_ffn[l]), sh2, sc2)

        if last:
            tokens = h2.reshape(B * N, D)
        else:
            q_c = split_heads(proj_c[..., Q0:K0]).transpose(0, 2, 1, 3)
            att_c = context_attention(q_c, k_c, v_c)
            y_c = merge_branches(proj_c, att_c, conv_w[l], conv_b[l], conv_ln_g[l], conv_ln_b[l],
                                 w_att_out[l], w_conv_out[l], w_o[l])
            ctx_mid = ctx + g1c * y_c
            h2c = modulate(rmsnorm(ctx_mid, norm_ffn[l]), sh2c, sc2c)
            tokens = jnp.concatenate([h2.reshape(B * N, D), h2c.reshape(B * n_ctx, D)], axis=0)
        f = hierarchical_moe(tokens, w_router_group[l], b_router_group[l], w_router_expert[l],
                             b_router_expert[l], w_exp_gate[l], w_exp_up[l], w_exp_down[l])
        x = x_mid + g2 * f[:B * N].reshape(B, N, D)
        if not last:
            ctx = ctx_mid + g2c * f[B * N:].reshape(B, n_ctx, D)
    return rmsnorm(x, final_norm)


CHUNK = 64
Q_BLOCK = 2 * CHUNK
N_FOX_HEADS = 8
N_SB_HEADS = 8
FOX_WIDTH = N_FOX_HEADS * HEAD_DIM
SB_WIDTH = N_SB_HEADS * HEAD_DIM
MIX_WIDTH = FOX_WIDTH + SB_WIDTH
IN_COLS = 3 * FOX_WIDTH + N_FOX_HEADS + 3 * SB_WIDTH
PEER_HEADS = 8
PEER_N_KEYS = 128
PEER_N_EXPERTS = PEER_N_KEYS * PEER_N_KEYS
PEER_TOPK = 16
PEER_D_KEY = 256
PEER_HALF = PEER_D_KEY // 2
PEER_TOKEN_BLOCK = 128
N_MOD = 6
EPS = 1e-6


def rms_norm(x, g):
    xf = x.astype(jnp.float32)
    inv = lax.rsqrt(jnp.mean(xf * xf, axis=-1, keepdims=True) + EPS)
    return (xf * inv).astype(x.dtype) * g

def split_heads_2(t, n_heads):
    b, s, _ = t.shape
    return t.reshape(b, s, n_heads, HEAD_DIM).transpose(0, 2, 1, 3)

def merge_blocks(o):
    nb, b, h, qb, dh = o.shape
    return o.transpose(1, 0, 3, 2, 4).reshape(b, nb * qb, h, dh)

def forgetting_attention(q, k, v, log_fcum):
    seq = q.shape[2]
    n_blocks = seq // Q_BLOCK
    scale = HEAD_DIM ** -0.5
    k_pos = jnp.arange(seq)

    def block(i):
        start = i * Q_BLOCK
        qb = lax.dynamic_slice_in_dim(q, start, Q_BLOCK, axis=2)
        fq = lax.dynamic_slice_in_dim(log_fcum, start, Q_BLOCK, axis=2)
        q_pos = start + jnp.arange(Q_BLOCK)
        logits = jnp.einsum('bhqd,bhkd->bhqk', qb, k, preferred_element_type=jnp.float32) * scale
        logits = logits + fq[..., :, None] - log_fcum[..., None, :]
        mask = k_pos[None, :] <= q_pos[:, None]
        logits = jnp.where(mask, logits, -jnp.inf)
        p = jax.nn.softmax(logits, axis=-1)
        return jnp.einsum('bhqk,bhkd->bhqd', p.astype(v.dtype), v)

    return merge_blocks(lax.map(block, jnp.arange(n_blocks)))

def stick_breaking_attention(q, k, v):
    seq = q.shape[2]
    n_blocks = seq // Q_BLOCK
    scale = HEAD_DIM ** -0.5
    k_pos = jnp.arange(seq)

    def block(i):
        start = i * Q_BLOCK
        qb = lax.dynamic_slice_in_dim(q, start, Q_BLOCK, axis=2)
        q_pos = start + jnp.arange(Q_BLOCK)
        z = jnp.einsum('bhqd,bhkd->bhqk', qb, k, preferred_element_type=jnp.float32) * scale
        mask = k_pos[None, :] < q_pos[:, None]
        log_beta = jax.nn.log_sigmoid(z)
        log_one_minus = jnp.where(mask, jax.nn.log_sigmoid(-z), 0.0)
        rest = lax.cumsum(log_one_minus, axis=3, reverse=True) - log_one_minus
        a = jnp.where(mask, jnp.exp(log_beta + rest), 0.0)
        return jnp.einsum('bhqk,bhkd->bhqd', a.astype(v.dtype), v)

    return merge_blocks(lax.map(block, jnp.arange(n_blocks)))

def peer_layer(h, w_query, sub_keys, expert_down, expert_up):
    b, s, d = h.shape
    t = b * s
    ht = h.reshape(t, d)
    query = (ht @ w_query).reshape(t, PEER_HEADS, 2, PEER_HALF)
    sub_scores = jnp.einsum('thpd,hpkd->thpk', query, sub_keys,
                            preferred_element_type=jnp.float32)
    half_vals, half_idx = lax.top_k(sub_scores, PEER_TOPK)
    cand = (half_vals[:, :, 0, :, None] + half_vals[:, :, 1, None, :]
            ).reshape(t, PEER_HEADS, PEER_TOPK * PEER_TOPK)
    top_vals, top_pos = lax.top_k(cand, PEER_TOPK)
    i1 = jnp.take_along_axis(half_idx[:, :, 0, :], top_pos // PEER_TOPK, axis=-1)
    i2 = jnp.take_along_axis(half_idx[:, :, 1, :], top_pos % PEER_TOPK, axis=-1)
    experts = i1 * PEER_N_KEYS + i2
    gates = jax.nn.softmax(top_vals, axis=-1).astype(h.dtype)

    n_blk = t // PEER_TOKEN_BLOCK
    xs = (ht.reshape(n_blk, PEER_TOKEN_BLOCK, d),
          experts.reshape(n_blk, PEER_TOKEN_BLOCK, PEER_HEADS, PEER_TOPK),
          gates.reshape(n_blk, PEER_TOKEN_BLOCK, PEER_HEADS, PEER_TOPK))

    def block(args):
        xb, eb, gb = args
        u = expert_down[eb]
        act = jax.nn.gelu(jnp.einsum('td,thkd->thk', xb, u), approximate=False) * gb
        vv = expert_up[eb]
        return jnp.einsum('thk,thkd->td', act, vv)

    return lax.map(block, xs).reshape(b, s, d)

def second_inputs(seed: int = 0) -> dict:
    key = jax.random.key(seed)
    ks = jax.random.split(key, 17)
    nrm = jax.random.normal
    L, D = DEPTH, D_MODEL
    return {
        "x": nrm(ks[0], (BATCH, SEQ, D), jnp.float32),
        "c": nrm(ks[1], (BATCH, D), jnp.float32),
        "w_ada": nrm(ks[2], (L, D, N_MOD * D), jnp.float32) * D ** -0.5,
        "b_ada": 0.02 * nrm(ks[3], (L, N_MOD * D), jnp.float32),
        "g_norm_mix": 1.0 + 0.05 * nrm(ks[4], (L, D), jnp.float32),
        "w_in": nrm(ks[5], (L, D, IN_COLS), jnp.float32) * D ** -0.5,
        "b_forget": 1.5 + 0.5 * nrm(ks[6], (L, N_FOX_HEADS), jnp.float32),
        "g_out_fox": 1.0 + 0.05 * nrm(ks[7], (L, HEAD_DIM), jnp.float32),
        "g_out_sb": 1.0 + 0.05 * nrm(ks[8], (L, HEAD_DIM), jnp.float32),
        "w_out": nrm(ks[9], (L, MIX_WIDTH, D), jnp.float32) * MIX_WIDTH ** -0.5,
        "g_norm_ffn": 1.0 + 0.05 * nrm(ks[10], (L, D), jnp.float32),
        "w_query": nrm(ks[11], (L, D, PEER_HEADS * PEER_D_KEY), jnp.float32) * D ** -0.5,
        "sub_keys": nrm(ks[12], (L, PEER_HEADS, 2, PEER_N_KEYS, PEER_HALF), jnp.float32) * PEER_HALF ** -0.5,
        "expert_down": nrm(ks[13], (L, PEER_N_EXPERTS, D), jnp.float32) * D ** -0.5,
        "expert_up": nrm(ks[14], (L, PEER_N_EXPERTS, D), jnp.float32) * PEER_HEADS ** -0.5,
        "g_final": 1.0 + 0.05 * nrm(ks[15], (D,), jnp.float32),
    }

def second_block(x, c, w_ada, b_ada, g_norm_mix, w_in, b_forget, g_out_fox, g_out_sb,
              w_out, g_norm_ffn, w_query, sub_keys, expert_down, expert_up, g_final):
    b, s, d = x.shape
    c_act = jax.nn.silu(c)
    for l in range(DEPTH):
        mod = c_act @ w_ada[l] + b_ada[l]
        sh1, sc1, gt1, sh2, sc2, gt2 = [m[:, None, :] for m in jnp.split(mod, N_MOD, axis=-1)]

        h = rms_norm(x, g_norm_mix[l]) * (1.0 + sc1) + sh1
        proj = h @ w_in[l]
        o1 = 3 * FOX_WIDTH
        o2 = o1 + N_FOX_HEADS
        fq, fk, fv = jnp.split(proj[..., :o1], 3, axis=-1)
        f_logit = proj[..., o1:o2]
        sq, sk, sv = jnp.split(proj[..., o2:], 3, axis=-1)

        log_f = jax.nn.log_sigmoid((f_logit + b_forget[l]).astype(jnp.float32))
        log_fcum = lax.cumsum(log_f, axis=1).transpose(0, 2, 1)
        fox_out = forgetting_attention(split_heads_2(fq, N_FOX_HEADS), split_heads_2(fk, N_FOX_HEADS),
                                       split_heads_2(fv, N_FOX_HEADS), log_fcum)
        sb_out = stick_breaking_attention(split_heads_2(sq, N_SB_HEADS), split_heads_2(sk, N_SB_HEADS),
                                          split_heads_2(sv, N_SB_HEADS))
        mixed = jnp.concatenate([rms_norm(fox_out, g_out_fox[l]).reshape(b, s, FOX_WIDTH),
                                 rms_norm(sb_out, g_out_sb[l]).reshape(b, s, SB_WIDTH)], axis=-1)
        x = x + gt1 * (mixed @ w_out[l])

        h2 = rms_norm(x, g_norm_ffn[l]) * (1.0 + sc2) + sh2
        x = x + gt2 * peer_layer(h2, w_query[l], sub_keys[l], expert_down[l], expert_up[l])
    return rms_norm(x, g_final)


def setup_inputs(seed=0):
    out = dict(first_inputs(seed))
    for name, value in second_inputs(seed + 1).items():
        if name != "x":
            out[name + "_2"] = value
    return out


def reference(
    x, c, ctx, c_ctx, w_mod, b_mod, norm_mix, w_in, rpb, w_att_out, conv_w, conv_b, conv_ln_g,
    conv_ln_b, w_conv_out, w_o, norm_ffn, w_router_group, b_router_group, w_router_expert,
    b_router_expert, w_exp_gate, w_exp_up, w_exp_down, final_norm, c_2, w_ada_2, b_ada_2,
    g_norm_mix_2, w_in_2, b_forget_2, g_out_fox_2, g_out_sb_2, w_out_2, g_norm_ffn_2, w_query_2,
    sub_keys_2, expert_down_2, expert_up_2, g_final_2,
):
    x = first_block(
        x, c, ctx, c_ctx, w_mod, b_mod, norm_mix, w_in, rpb, w_att_out, conv_w, conv_b,
        conv_ln_g, conv_ln_b, w_conv_out, w_o, norm_ffn, w_router_group, b_router_group,
        w_router_expert, b_router_expert, w_exp_gate, w_exp_up, w_exp_down, final_norm,
    )
    return second_block(
        x, c_2, w_ada_2, b_ada_2, g_norm_mix_2, w_in_2, b_forget_2, g_out_fox_2, g_out_sb_2,
        w_out_2, g_norm_ffn_2, w_query_2, sub_keys_2, expert_down_2, expert_up_2, g_final_2,
    )


_drawn_inputs = setup_inputs


def setup_inputs(seed=0):
    import zlib

    import numpy as np

    out = dict(_drawn_inputs(seed))
    spreads = {}
    factors = {'b_mod': 3.417,
     'norm_mix': 6.575,
     'rpb': 8.0,
     'conv_b': 7.935,
     'conv_ln_g': 7.16,
     'conv_ln_b': 8.0,
     'norm_ffn': 3.116,
     'b_router_group': 6.872,
     'b_router_expert': 8.0}
    for name, (base, spread) in spreads.items():
        noise = np.random.default_rng([zlib.crc32(name.encode()), seed]).standard_normal(out[name].shape)
        drawn = base * np.exp(spread * noise) if base else spread * noise
        out[name] = __import__('jax').numpy.asarray(drawn.astype(out[name].dtype))
    for name, factor in factors.items():
        out[name] = (out[name] * factor).astype(out[name].dtype)
    return out
```

```python
from contextlib import ExitStack

import numpy as np
import concourse.bass as bass
from concourse import mybir

F32 = mybir.dt.float32
I32 = mybir.dt.int32
U32 = mybir.dt.uint32
ALU = mybir.AluOpType
ACT = mybir.ActivationFunctionType
AX = mybir.AxisListType.X

P = 128
T = 512
TT = T // P
D = 1024
DC = D // P
CTX = 256
CT = CTX // P
H = 8
HD = 64
DA = H * HD
AC = DA // P
GRID_W, WIN = 64, 16
ROWS = T // GRID_W
RPB_R, RPB_C = 2 * ROWS - 1, 2 * WIN - 1
SKEW = 128
CONV_W = 31
PADC = CONV_W // 2
CC = 512 // P
UW = T + 2 * PADC
NG, NE, EPG = 4, 32, 8
F = 512
CAP = 64
OVER = (2 * T) // (CAP + 1)
SLOTS = (NE + OVER) * CAP
EPS = 1e-6
NEG = -1e30
RING = 6
SLAB = 4096
KEYS = T + CTX
K16 = 16
G4 = 4
DOWN_SETS = 2
UP_SETS = K16 // G4


class Link:

    def __init__(self, eng, own):
        self.eng, self.own, self.count = eng, own, {}

    def __call__(self, ins, sem=None):
        sem = self.own if sem is None else sem
        n = self.count.get(id(sem), 0) + 1
        self.count[id(sem)] = n
        ins.then_inc(sem, 1)
        self.eng.wait_ge(sem, n)
        return n


def build(nc, A, out):
    with ExitStack() as ctx:
        def sb(name, shape, dt=F32):
            return ctx.enter_context(nc.sbuf_tensor(name, shape, dt))

        def sem(name):
            return ctx.enter_context(nc.semaphore(name))

        def dram(name, shape, dt=F32):
            return nc.dram_tensor(name, shape, dt, kind="Internal")

        bank = [ctx.enter_context(nc.psum_tensor(f"bank{i}", [P, 512], F32)) for i in range(8)]
        ring = sb("ring", [P, RING, SLAB])
        arena_x = sb("arena_x", [P, 4224])
        arena_h = sb("arena_h", [P, 4096])
        arena_q = sb("arena_q", [P, 4096])
        arena_v = sb("arena_v", [P, 8192])
        arena_w = sb("arena_w", [P, 4864])

        def view(arena, at, *shape):
            n = int(np.prod(shape))
            ap = arena[:, at:at + n]
            if len(shape) == 1:
                return ap
            names = "abcd"[:len(shape)]
            return ap.rearrange(f"p ({' '.join(names)}) -> p {' '.join(names)}",
                                **{k: v for k, v in zip(names[1:], shape[1:])})

        def slot(s, *shape):
            ap = ring[:, s, :]
            names = "abcd"[:len(shape)]
            return ap.rearrange(f"p ({' '.join(names)}) -> p {' '.join(names)}",
                                **{k: v for k, v in zip(names[1:], shape[1:])})

        ident = sb("ident", [P, P])
        before = sb("before", [P, P])
        ones = sb("ones", [P, P])
        later_neg = sb("later_neg", [P, P])
        ones_neg = sb("ones_neg", [P, P])
        causal = sb("causal", [P, P])
        mean_w = sb("mean_w", [P, P])
        iota_i = sb("iota_i", [P, 64], I32)
        iota = sb("iota", [P, 64])
        part_i = sb("part_i", [P, 1], I32)
        band = sb("band", [P, 64])
        band_t = sb("band_t", [P, 2, 64])
        wstart = sb("wstart", [P, 4])

        cvec = sb("cvec", [P, 3, DC])
        mcol = sb("mcol", [P, 2, DC])
        mcol_c = sb("mcol_c", [P, 2, DC])
        mcol_2 = sb("mcol_2", [P, 2, DC])
        gcol = sb("gcol", [P, 2, DC])
        acol = sb("acol", [P, 3, DC])
        convc = sb("convc", [P, CC, 34])
        ssq = sb("ssq", [P, 8])
        rms = sb("rms", [P, 8])
        rms_t = sb("rms_t", [P, 8])
        smx = sb("smx", [P, 2, 4])
        ssum = sb("ssum", [P, 2, 32])
        rinv = sb("rinv", [P, 8])

        xr = view(arena_x, 0, TT, D)
        u_pad = view(arena_x, 0, CC, UW)
        conv = view(arena_x, CC * UW, CC, T)
        hT = view(arena_h, 0, DC, T)
        modr = view(arena_q, 0, 3, T)
        modb = view(arena_q, 3 * T, 3, T)
        junk = view(arena_q, 6 * T, D)
        kT = view(arena_q, 0, AC, T)
        qT = view(arena_q, AC * T, AC, T)
        mixT = view(arena_q, 0, DC, T)
        vrow = view(arena_v, 0, TT, DA)
        kcT = view(arena_v, 2048, AC, CTX)
        vcrow = view(arena_v, 3072, CT, DA)
        hcT = view(arena_v, 4096, DC, CTX)
        cr = view(arena_v, 6144, CT, D)
        attT = view(arena_v, 4096, AC, T)
        att = view(arena_v, 6144, TT, DA)
        bias = [view(arena_w, 896 * i, 14, 64) for i in range(2)]
        prob = [view(arena_w, 1792 + KEYS * i, KEYS) for i in range(2)]
        probT = [view(arena_w, 3328 + KEYS * i, KEYS // P, P) for i in range(2)]
        sig = [prob[i][:, 0:T] for i in range(2)]
        convw_in = view(arena_w, 4096, T)
        rpb_pad = view(arena_w, 4608, SKEW)
        conv_sq = view(arena_w, 1792, CC, T)
        conv_r = view(arena_w, 3840, T)
        conv_t = view(arena_w, 4352, T)
        gate_a = [view(arena_w, T * i, T) for i in range(2)]
        gate_c = [view(arena_w, 1024 + T * i, T) for i in range(2)]
        tmp = view(arena_w, 2048, D)
        tmp2 = view(arena_w, 3072, D)
        g1_b = view(arena_v, 0, D)
        a2_b = view(arena_v, D, D)
        sh2_b = view(arena_v, 2 * D, D)
        g2_b = view(arena_v, 3 * D, D)
        h2r = view(arena_v, 4096, TT, D)

        def route(at, *shape):
            return view(arena_w, at, *shape)
        junk2 = view(arena_w, 0, D)
        h2T = view(arena_h, 0, DC, T)
        lg = route(1024, TT, NG + NE)
        lgp = route(1168, TT, 8)
        gval, eval_ = route(1200, TT, 8), route(1232, TT, 8)
        gexp, oneh, pen = route(1264, TT, NG), route(1280, TT, NG), route(1296, TT, NG)
        gif, psum_, eif = route(1312, TT), route(1316, TT), route(1320, TT, 2)
        dval, dexp, dden = route(1328, TT), route(1332, TT), route(1336, TT)
        emask = route(1344, TT, NE)
        pick = route(1472, 2, TT, NE)
        both = route(1728, TT, NE)
        rank = route(1856, TT, NE)
        cnt, nblk, incl, incl2, delta, e64 = (route(1984 + 32 * i, NE) for i in range(6))
        over_at = route(2176, TT, NE)
        sel = route(2304, TT, NE)
        slot_f = route(2432, 2, TT)
        tab = route(2440, OVER, NE)
        tab_e = route(2920, OVER)
        ridx = sb("ridx", [P, 2, TT, 8], U32)
        slot_i = sb("slot_i", [P, 2, TT], I32)
        gw = sb("gw", [P, 2, TT])
        over_i = sb("over_i", [P, 16], I32)
        wr = sb("wr", [P, DC, NG + NE])
        br = sb("br", [P, NG + NE])
        zeros = sb("zeros", [P, P])
        xblk = [arena_h[0:CAP, D * i:D * i + D] for i in range(2)]
        xbT = [view(arena_h, 2048 + 512 * i, DC, CAP) for i in range(2)]
        yblk = [view(arena_h, 3072 + 512 * i, 512) for i in range(2)]
        silu_g = [view(arena_q, 256 * i, 256) for i in range(2)]
        hid = [view(arena_q, 512 + 256 * i, 256) for i in range(2)]
        hidT = [view(arena_q, 1024 + 256 * i, 2, P) for i in range(2)]
        ygat = [[view(arena_v, 4096 + 2048 * i + 1024 * s, D) for s in range(2)] for i in range(2)]
        fn_b = g1_b
        xnb = view(arena_q, 0, TT, D)

        wf = sb("wf", [P, DC, H])
        bf = sb("bf", [P, H])
        gob = sb("gob", [P, 2])
        sqT, skT_ = view(arena_v, 0, AC, T), view(arena_v, 2048, AC, T)
        svr, fvr = view(arena_v, 4096, TT, DA), view(arena_v, 6144, TT, DA)
        fqT, fkT = view(arena_q, 0, AC, T), view(arena_q, 2048, AC, T)
        mixed = view(arena_h, 0, TT, D)
        flog = route(4096, TT, H)
        fabs = route(4128, TT, H)
        fcumT = arena_w[0:H, 4160:4160 + T]
        fcum = route(4672, TT, H)
        stick_a = [ring[:, s, 0:1536].rearrange("p (a b) -> p a b", b=512) for s in (5, 0)]
        stick_b = [ring[:, s, 1536:3072].rearrange("p (a b) -> p a b", b=512) for s in (5, 0)]
        fprob = [ring[:, 5, 3072 + 512 * i:3584 + 512 * i] for i in range(2)]
        fprobT = [ring[:, 0, 3072 + 512 * i:3584 + 512 * i] for i in range(2)]
        msq = [view(arena_q, D * i, D) for i in range(2)]
        mss, mrt, msc = (view(arena_q, 2048 + 64 * i, TT, 2 * H) for i in range(3))
        mixT2 = view(arena_v, 0, DC, T)
        gt1_2, a2_2, sh2_2, nf_2 = (route(D * i, D) for i in range(4))
        tmp_2 = route(4096, 512)
        h2r_2 = view(arena_q, 0, TT, D)
        qT2 = view(arena_v, 0, TT * H, 2 * P)
        sk_in = view(ring[:, 1, :], 0, 2 * H, P)
        skT = route(0, H + 1, 2 * P)
        gt2_2, gfin = route(2304, D), route(3328, D)
        tmp_p = route(4352, 512)

        def small(at, *shape):
            return view(arena_h, at, *shape)
        diag = small(0, K16, P)
        qh = small(2048, 2, P)
        work = small(2304, 2, P)
        cand = small(2560, K16 * K16)
        cand2 = small(2816, K16 * K16)
        onehot = small(3072, K16, K16)
        hval = small(3328, 2, K16)
        hidx_f = small(3360, 2, K16)
        pos_f = small(3392, 2, K16)
        top = small(3424, K16)
        half_i = small(3440, 2, K16)
        id_f = small(3472, K16)
        gsub, gex = small(3488, K16), small(3504, K16)
        gate_p = [small(3520 + K16 * i, K16) for i in range(2)]
        dots, gel, coef = small(3552, K16), small(3568, K16), small(3584, K16)
        gsum = small(3600, 1)
        hidx = sb("hidx", [P, 2, K16], U32)
        pos = sb("pos", [P, K16], U32)
        pos_hl = sb("pos_hl", [P, 2, K16], U32)
        ids = [sb(f"ids{i}", [P, K16], I32) for i in range(2)]
        gbuf = [ring[:, i // 4, D * (i % 4):D * (i % 4) + D] for i in range(4 * RING)]
        down, up = gbuf[0:8], gbuf[8:24]

        mod_d = dram("mod_d", [2, 6 * D])
        mod2_d = dram("mod2_d", [1, 6 * D])
        skew_d = dram("skew_d", [H * RPB_R, GRID_W, SKEW])
        xs_d = dram("xs_d", [SLOTS, D])
        ys_d = dram("ys_d", [SLOTS, D])

        slab_in = [sem(f"slab_in{s}") for s in range(RING)]
        vec_in = sem("vec_in")
        x_in = sem("x_in")
        modb_in = sem("modb_in")
        cw_in = sem("cw_in")
        modb2_in = sem("modb2_in")
        rpb_in = sem("rpb_in")
        skew_out = sem("skew_out")
        bias_in = [sem("bias_in0"), sem("bias_in1")]
        mod_out = sem("mod_out")
        mod2_out = sem("mod2_out")
        convc_done = sem("convc_done")
        mcol2_in = sem("mcol2_in")
        mod_out_rest = sem("mod_out_rest")
        mcol_in = sem("mcol_in")
        xres_in = sem("xres_in")
        rows_in = sem("rows_in")
        xs_zero = sem("xs_zero")
        ys_zero = sem("ys_zero")
        out_dma = sem("out_dma")
        const_step = sem("const_step")
        consts = sem("consts")
        pe_mod = sem("pe_mod")
        mod_rows = sem("mod_rows")
        dve_step = sem("dve_step")
        act_step = sem("act_step")
        silu_c = sem("silu_c")
        ssq_done = sem("ssq_done")
        ms_done = sem("ms_done")
        root_done = sem("root_done")
        xn_done = sem("xn_done")
        acol_done = sem("acol_done")
        xT_done = sem("xT_done")
        hT_done = sem("hT_done")
        convw_T = sem("convw_T")
        glu_done = sem("glu_done")
        sig_done = sem("sig_done")
        u_done = sem("u_done")
        conv_done = sem("conv_done")
        proj_done = sem("proj_done")
        proj_out = sem("proj_out")
        cmean_done = sem("cmean_done")
        ccen_done = sem("ccen_done")
        csq_done = sem("csq_done")
        cvar_done = sem("cvar_done")
        cms_done = sem("cms_done")
        croot_done = sem("croot_done")
        cnorm_done = sem("cnorm_done")
        convy_done = sem("convy_done")
        s_done = sem("s_done")
        nmax_done = sem("nmax_done")
        p_done = sem("p_done")
        pT_done = sem("pT_done")
        pTa_out = sem("pTa_out")
        pTb_out = sem("pTb_out")
        o_done = sem("o_done")
        att_done = sem("att_done")
        attT_pe = sem("attT_pe")
        attT_done = sem("attT_done")
        merge_pe = sem("merge_pe")
        gates_done = sem("gates_done")
        mix_done = sem("mix_done")
        wo_pe = sem("wo_pe")
        res_done = sem("res_done")

        h2_done = sem("h2_done")
        h2T_pe = sem("h2T_pe")
        h2T_done = sem("h2T_done")
        logit_pe = sem("logit_pe")
        gsub_done = sem("gsub_done")
        gexp_done = sem("gexp_done")
        both_done = sem("both_done")
        rank_pe = sem("rank_pe")
        route_done = sem("route_done")
        wr_in = sem("wr_in")
        fn_in = sem("fn_in")
        scat = sem("scat")
        xbT_done = sem("xbT_done")
        xbT_out = sem("xbT_out")
        gu_done = sem("gu_done")
        silu_done = sem("silu_done")
        hid_done = sem("hid_done")
        hidT_pe = sem("hidT_pe")
        hidT_done = sem("hidT_done")
        dn_done = sem("dn_done")
        yv_done = sem("yv_done")
        over_done = sem("over_done")
        ov_xin = sem("ov_xin")
        ov_slab = sem("ov_slab")
        ov_ydma = sem("ov_ydma")
        comb_done = sem("comb_done")
        x2_done = sem("x2_done")
        xnb_done = sem("xnb_done")
        mark = sem("mark")
        xb_in = [sem("xb_in0"), sem("xb_in1")]
        y_dma = [sem("y_dma0"), sem("y_dma1")]
        acol2_done = sem("acol2_done")
        f_pe = sem("f_pe")
        f_dve = sem("f_dve")
        f_act = sem("f_act")
        sbz_pe = sem("sbz_pe")
        sba_done = sem("sba_done")
        sbl_done = sem("sbl_done")
        sbb_done = sem("sbb_done")
        mask_done = sem("mask_done")
        sbr_pe = sem("sbr_pe")
        sbc_done = sem("sbc_done")
        sbe_done = sem("sbe_done")
        sbo_pe = sem("sbo_pe")
        sbo_done = sem("sbo_done")
        msq_done = sem("msq_done")
        mms_done = sem("mms_done")
        mroot_done = sem("mroot_done")
        mixed_done = sem("mixed_done")
        sk_dma = sem("sk_dma")
        skT_pe = sem("skT_pe")
        skT_done = sem("skT_done")
        q_pe = sem("q_pe")
        q_done = sem("q_done")
        qh_done = sem("qh_done")
        sc_pe = sem("sc_pe")
        topk_step = sem("topk_step")
        gsub2_done = sem("gsub2_done")
        gex_done = sem("gex_done")
        ids_done = sem("ids_done")
        down_free = sem("down_free")
        up_free = sem("up_free")
        gelu_done = sem("gelu_done")
        coef_done = sem("coef_done")
        diag_done = sem("diag_done")
        peer_done = sem("peer_done")
        fin_add = sem("fin_add")
        fin_done = sem("fin_done")
        rows2_in = sem("rows2_in")
        down_in = [sem(f"down_in{i}") for i in range(DOWN_SETS)]
        up_in = [sem(f"up_in{i}") for i in range(UP_SETS)]
        yg_in = [sem(f"yg_in{t}") for t in range(TT)]

        def cols_pc(w, j):
            return w[:, j * 512:(j + 1) * 512].rearrange("(p c) n -> p c n", c=DC)

        def cols_cp(w, j):
            return w[:, j * 512:(j + 1) * 512].rearrange("(c p) n -> p c n", p=P)

        def rows_kp(w):
            return w.rearrange("(k p) n -> p k n", p=P)

        w_in = A["w_in"]
        QKV, GLU, GA, GB = 0, 3, 5, 7
        slabs = []
        slabs += [(cols_pc(A["w_mod"], j), (DC, 512), pe_mod, j // 4 + 1) for j in range(12)]
        slabs += [(cols_pc(w_in, GLU), (DC, 512), glu_done, CC), (cols_pc(w_in, GLU + 1), (DC, 512), glu_done, CC)]
        slabs += [(cols_pc(w_in, QKV + 1), (DC, 512), proj_done, 12), (cols_pc(w_in, QKV), (DC, 512), proj_done, 8),
                  (cols_pc(w_in, QKV + 2), (DC, 512), proj_done, 18)]
        slabs += [(cols_pc(A["w_ada_2"], j), (DC, 512), pe_mod, 3 + j // 4 + 1) for j in range(12)]
        slabs += [(cols_pc(w_in, GA), (DC, 512), merge_pe, 4), (cols_pc(w_in, GB), (DC, 512), merge_pe, 4),
                  (rows_kp(A["w_att_out"]), (AC, D), merge_pe, 8), (rows_kp(A["w_conv_out"]), (CC, D), merge_pe, 8),
                  (cols_pc(w_in, GA + 1), (DC, 512), merge_pe, 8), (cols_pc(w_in, GB + 1), (DC, 512), merge_pe, 8)]
        slabs += [(cols_cp(A["w_o"], j), (DC, 512), wo_pe, 8) for j in range(2)]
        N_MOD, N_GLU, N_K, N_Q, N_V, N_ADA, N_GA, N_WO = 0, 12, 14, 15, 16, 17, 29, 35

        def w_gu(w, e):
            return w[e, :, :].rearrange("(p c) n -> p c n", c=DC)

        def w_dn(w, e):
            return w[e, :, :].rearrange("(h p k) n -> p h k n", h=2, k=2)

        N_EXP = len(slabs)
        for e in range(2):
            slabs += [(w_gu(A["w_exp_gate"], e), (DC, F), gu_done, 2 * NE), (w_gu(A["w_exp_up"], e), (DC, F), gu_done, 2 * NE),
                      (w_dn(A["w_exp_down"], e), (2, 2, D), dn_done, 2 * NE)]

        SQ_2ND, SQ_FINAL, SQ_1ST, SQ_LAST = (CT + TT, CT + 4 * TT), CT + 2 * TT, CT + 3 * TT, CT + 5 * TT
        MS_2ND, MS_FINAL, MS_1ST, MS_LAST = (1, TT + 3), TT + 1, TT + 2, 2 * TT + 3

        N2 = N_EXP + 3 * NE
        FOX_W, STICK_W = 3 * DA, 3 * DA + H
        slabs2 = [cols_pc(A["w_in_2"], j) for j in range(3)]
        slabs2 += [A["w_in_2"][:, STICK_W + j * 512:STICK_W + (j + 1) * 512].rearrange("(p c) n -> p c n", c=DC) for j in range(3)]
        slabs2 += [cols_cp(A["w_out_2"], j) for j in range(2)]
        slabs2 += [cols_pc(A["w_query_2"], j) for j in range(4)]
        S_FOX, S_STICK, S_WO, S_WQ = 0, 3, 6, 8

        def slab2(k):
            return slot((N2 + k) % RING, DC, 512)

        def slab2_ready(eng, k):
            eng.wait_ge(slab_in[(N2 + k) % RING], 16 * ((N2 + k) // RING + 1))

        PIECES = (512, 512, 256)

        def stick_cols(j, q):
            return (0, 1, 2, 1)[j], (0, 0, 0, 384)[j] + (q - j) * P

        def at_head(n, per, extra):
            i, off = n
            return per * off + extra if i is None else i * (2 * per) + (per * off + extra)

        def unless_first(eng, s, value):
            if not isinstance(value, int) or value > 0:
                eng.wait_ge(s, value)

        def slab(n):
            return slot(n % RING, *slabs[n][1])

        def slab_ready(eng, n):
            eng.wait_ge(slab_in[n % RING], 16 * (n // RING + 1))

        block = ctx.enter_context(nc.Block())

        @block.sync
        def _(sp):
            sp.dma_start(cr, A["ctx"].rearrange("(t p) d -> p t d", p=P)).then_inc(x_in, 16)
            sp.dma_start(xr, A["x"].rearrange("(t p) d -> p t d", p=P)).then_inc(x_in, 16)
            for n, (src, shape, _, _) in enumerate(slabs):
                if n >= RING:
                    _, _, free, value = slabs[n - RING]
                    sp.wait_ge(free, value)
                sp.dma_start(slab(n), src).then_inc(slab_in[n % RING], 16)
                if n == N_V:
                    sp.wait_ge(consts, 1)
                    sp.dma_start(xs_d[:, :].rearrange("(p r) (a b) -> p (r a) b", p=CAP, b=P),
                                 zeros[0:CAP, :].unsqueeze(1).broadcast_to([CAP, SLOTS // CAP * DC, P])).then_inc(xs_zero, 16)
                    sp.dma_start(ys_d[NE * CAP:SLOTS, :].rearrange("(p r) (a b) -> p (r a) b", p=CAP, b=P),
                                 zeros[0:CAP, :].unsqueeze(1).broadcast_to([CAP, OVER * DC, P])).then_inc(ys_zero, 16)

            def rows(e, b):
                unless_first(sp, xbT_done, e - 1)
                sp.dma_start(xblk[b], xs_d[bass.ds(e * CAP, CAP), :]).then_inc(xb_in[b], 16)

            sp.wait_ge(scat, 16 * 2 * TT)
            for b in range(2):
                rows(b, b)
            with sp.Fori(1, NE // 2) as i:
                for b in range(2):
                    e = i * 2 + b
                    n = N_EXP + 3 * b
                    rows(e, b)
                    for w, k in (("w_exp_gate", 0), ("w_exp_up", 1)):
                        if k == 0:
                            sp.wait_ge(gu_done, e - 1)
                        sp.dma_start(slab(n + k), A[w][bass.ds(e, 1), :, :].rearrange("o (p c) n -> p (o c) n", c=DC))\
                            .then_inc(slab_in[(n + k) % RING], 16)
                    sp.wait_ge(dn_done, e - 1)
                    sp.dma_start(slab(n + 2), A["w_exp_down"][bass.ds(e, 1), :, :].rearrange("o (h p k) n -> p (o h) k n", h=2, k=2))\
                        .then_inc(slab_in[(n + 2) % RING], 16)
            def load2(k):
                sp.dma_start(slab2(k), slabs2[k]).then_inc(slab_in[(N2 + k) % RING], 16)

            sp.wait_ge(dn_done, NE)
            for k in range(S_STICK, S_STICK + 3):
                load2(k)
            sp.wait_ge(route_done, 1)
            sp.wait_ge(ys_zero, 16)
            n_over = sp.value_load(over_i[0:1, 0:1], min_val=0, max_val=OVER)
            with sp.Fori(0, OVER) as i:
                with sp.If(i < n_over):
                    sp.wait_ge(dn_done, NE)
                    sp.wait_ge(yv_done, NE)
                    e = sp.value_load(over_i[0:1, bass.ds(i + 1, 1)], min_val=0, max_val=NE - 1)
                    sp.dma_start(xblk[0], xs_d[bass.ds(i * CAP + NE * CAP, CAP), :]).then_inc(ov_xin, 16)
                    for w, k in (("w_exp_gate", 0), ("w_exp_up", 1)):
                        sp.dma_start(slab(N_EXP + k), A[w][bass.ds(e, 1), :, :].rearrange("o (p c) n -> p (o c) n", c=DC))\
                            .then_inc(ov_slab, 16)
                    sp.dma_start(slab(N_EXP + 2), A["w_exp_down"][bass.ds(e, 1), :, :].rearrange("o (h p k) n -> p (o h) k n", h=2, k=2))\
                        .then_inc(ov_slab, 16)
                    sp.wait_ge(yv_done, i + (NE + 1))
                    for half in range(2):
                        sp.dma_start(ys_d[bass.ds(i * CAP + NE * CAP, CAP), 512 * half:512 * half + 512],
                                     yblk[0][CAP * half:CAP * half + CAP, :]).then_inc(ov_ydma, 16)
                    sp.wait_ge(ov_ydma, i * 32 + 32)
                    sp.sem_inc(mark, 1)
            sp.sem_inc(over_done, 1)
            for k in range(S_FOX, S_FOX + 3):
                load2(k)
            sp.wait_ge(proj_done, 18 + 24)
            for k in range(S_WO, S_WO + 4):
                load2(k)
            sp.wait_ge(att_done, 2 * H)
            sp.wait_ge(sbo_done, H)
            for k in range(S_WO + 4, S_WO + 6):
                load2(k)
            sp.wait_ge(wo_pe, 4 * TT)
            sp.dma_start(sk_in, A["sub_keys_2"].rearrange("h p k d -> k (h p) d")).then_inc(sk_dma, 16)
            for t in range(TT):
                sp.wait_ge(fin_done, t + 1)
                sp.dma_start(out[t * P:(t + 1) * P, :], xr[:, t, :]).then_inc(out_dma, 16)
            sp.wait_ge(out_dma, 16 * TT)
            sp.wait_ge(skew_out, 16)
            sp.wait_ge(mod_out_rest, 16 * 8)
            sp.wait_ge(mod2_out, 16 * 12)

        @block.gpsimd
        def _(pool):
            link = Link(pool, const_step)
            for t, v in ((ident, 0.0), (before, 1.0), (ones, 1.0), (later_neg, -1.0), (ones_neg, -1.0),
                         (causal, 0.0), (mean_w, 1.0 / 512), (zeros, 0.0)):
                link(pool.memset(t[:, :], v))
            link(pool.memset(rpb_pad, 0.0))
            link(pool.affine_select(out=ident[:, :], in_=ident[:, :], compare_op=ALU.not_equal, fill=1.0, base=0,
                                    pattern=[[-1, P]], channel_multiplier=1))
            link(pool.affine_select(out=before[:, :], in_=before[:, :], compare_op=ALU.is_gt, fill=0.0, base=0,
                                    pattern=[[1, P]], channel_multiplier=-1))
            link(pool.affine_select(out=later_neg[:, :], in_=later_neg[:, :], compare_op=ALU.is_gt, fill=0.0, base=0,
                                    pattern=[[-1, P]], channel_multiplier=1))
            link(pool.affine_select(out=causal[:, :], in_=causal[:, :], compare_op=ALU.is_ge, fill=NEG, base=0,
                                    pattern=[[-1, P]], channel_multiplier=1))
            link(pool.iota(iota_i[:, :], pattern=[[1, 64]], base=0, channel_multiplier=0))
            link(pool.iota(part_i[:, :], pattern=[[0, 1]], base=0, channel_multiplier=1), consts)
            pool.dma_start(rpb_pad[0:H * RPB_R, GRID_W - WIN:GRID_W - WIN + RPB_C],
                           A["rpb"].rearrange("h r c -> (h r) c")).then_inc(rpb_in, 16)
            pool.wait_ge(rpb_in, 16)
            pool.dma_start(skew_d[:, :, :], rpb_pad[0:H * RPB_R, :].unsqueeze(1).broadcast_to([H * RPB_R, GRID_W, SKEW]))\
                .then_inc(skew_out, 16)
            for j in range(12):
                pool.wait_ge(mod_rows, j + 1)
                pool.dma_start(mod_d[:, j * 512:(j + 1) * 512], modr[32 * (j % 4):32 * (j % 4) + 2, j // 4, :])\
                    .then_inc(mod_out if j < 4 else mod_out_rest, 16)
                if j == 3:
                    pool.wait_ge(mod_out, 16 * 4)
                    for r, dst in ((0, mcol), (1, mcol_c)):
                        pool.dma_start(dst[:, :, :], mod_d[r, 0:2 * D].rearrange("(k p c) -> p k c", k=2, c=DC))\
                            .then_inc(mcol_in, 16)
            pool.wait_ge(skew_out, 16)
            skew = skew_d[:, :, :]
            for h in range(H):
                if h >= 2:
                    pool.wait_ge(nmax_done, 4 * (h - 1))
                for half in range(2):
                    src = bass.AP(skew.tensor, skew.offset + (h * RPB_R + 1 - half) * GRID_W * SKEW + GRID_W - 1,
                                  [[SKEW - 1, GRID_W], [GRID_W * SKEW, 14], [1, GRID_W]])
                    pool.dma_start(bias[h % 2][64 * half:64 * half + 64, :, :], src).then_inc(bias_in[h % 2], 16)
            for j in range(12):
                pool.wait_ge(mod_rows, 12 + j + 1)
                pool.dma_start(mod2_d[:, j * 512:(j + 1) * 512], modr[32 * (j % 4):32 * (j % 4) + 1, j // 4, :])\
                    .then_inc(mod2_out, 16)
            pool.wait_ge(mod_out_rest, 16 * 8)
            pool.wait_ge(o_done, 32)
            for dst, src in ((g1_b, mod_d[0, 2 * D:3 * D]), (sh2_b, mod_d[0, 3 * D:4 * D]), (a2_b, mod_d[0, 4 * D:5 * D]),
                             (g2_b, mod_d[0, 5 * D:6 * D])):
                pool.dma_start(dst, src.partition_broadcast(P)).then_inc(rows_in, 16)
            pool.wait_ge(merge_pe, DC)
            pool.dma_start(xr, A["x"].rearrange("(t p) d -> p t d", p=P)).then_inc(xres_in, 16)
            pool.dma_start(tmp2, A["norm_ffn"].partition_broadcast(P)).then_inc(rows_in, 16)
            pool.wait_ge(mod2_out, 16 * 12)
            pool.dma_start(mcol_2[:, :, :], mod2_d[0, 0:2 * D].rearrange("(k p c) -> p k c", k=2, c=DC)).then_inc(mcol2_in, 16)
            pool.wait_ge(h2_done, TT)
            pool.wait_ge(route_done, 1)
            pool.wait_ge(xs_zero, 16)
            for t in range(TT):
                for s in range(2):
                    pool.indirect_dma_start(xs_d[:, :], bass.IndirectOffsetOnAxis(ap=slot_i[:, s, t:t + 1], axis=0),
                                            h2r[:, t, :], None).then_inc(scat, 16)
            pool.wait_ge(res_done, 2 * TT)
            pool.dma_start(fn_b, A["final_norm"].partition_broadcast(P)).then_inc(fn_in, 16)
            for b in range(2):
                pool.wait_ge(y_dma[b], 32 * (NE // 2))
            pool.wait_ge(over_done, 1)
            pool.wait_ge(ys_zero, 16)
            pool.wait_ge(scat, 16 * 2 * TT)
            for t in range(TT):
                if t >= 2:
                    pool.wait_ge(comb_done, t - 1)
                for s in range(2):
                    pool.indirect_dma_start(ygat[t % 2][s], None, ys_d[:, :],
                                            bass.IndirectOffsetOnAxis(ap=slot_i[:, s, t:t + 1], axis=0)).then_inc(yg_in[t], 16)
            pool.wait_ge(ssq_done, SQ_1ST + TT)
            pool.wait_ge(wo_pe, 2 * TT)
            for dst, src in ((gt1_2, mod2_d[0, 2 * D:3 * D]), (sh2_2, mod2_d[0, 3 * D:4 * D]), (a2_2, mod2_d[0, 4 * D:5 * D]),
                             (nf_2, A["g_norm_ffn_2"])):
                pool.dma_start(dst, src.partition_broadcast(P)).then_inc(rows2_in, 16)

            def mask(x, done):
                link(pool.tensor_tensor(x[:, :, 0:P], x[:, :, 0:P], before[:, :].unsqueeze(1).broadcast_to([P, 3, P]), ALU.mult))
                link(pool.tensor_tensor(x[:, 1, 384:512], x[:, 1, 384:512], before[:, :], ALU.mult), done)

            for h in range(H):
                pool.wait_ge(sbb_done, h + 1)
                mask(stick_a[h % 2], mask_done)
                pool.wait_ge(sbe_done, h + 1)
                mask(stick_b[h % 2], mask_done)
            pool.wait_ge(h2_done, 2 * TT)
            pool.wait_ge(ssq_done, SQ_2ND[1] + TT)
            for dst, src in ((gt2_2, mod2_d[0, 5 * D:6 * D]), (gfin, A["g_final_2"])):
                pool.dma_start(dst, src.partition_broadcast(P)).then_inc(rows2_in, 16)
            pool.wait_ge(q_pe, 4 * TT)
            pool.wait_ge(skT_pe, 4)
            pool.sem_inc(down_free, DOWN_SETS)
            pool.sem_inc(up_free, UP_SETS)

            def gathers(n, b):
                def down_rows(g):
                    pool.wait_ge(down_free, at_head(n, UP_SETS, g + 1))
                    pool.sem_inc(mark, 1)
                    for k in range(G4):
                        r = G4 * g + k
                        pool.indirect_dma_start(down[r % (G4 * DOWN_SETS)], None, A["expert_down_2"],
                                                bass.IndirectOffsetOnAxis(ap=ids[b][:, r:r + 1], axis=0)).then_inc(down_in[g % DOWN_SETS], 16)

                def up_rows(g):
                    pool.wait_ge(up_free, at_head(n, UP_SETS, g + 1))
                    pool.sem_inc(mark, 1)
                    for k in range(G4):
                        r = G4 * g + k
                        pool.indirect_dma_start(up[r], None, A["expert_up_2"],
                                                bass.IndirectOffsetOnAxis(ap=ids[b][:, r:r + 1], axis=0)).then_inc(up_in[g], 16)

                pool.wait_ge(ids_done, at_head(n, 1, 1))
                pool.sem_inc(mark, 1)
                down_rows(0)
                for g in range(1, UP_SETS):
                    down_rows(g)
                    up_rows(g - 1)
                up_rows(UP_SETS - 1)

            for t in range(TT):
                with pool.Fori(0, H // 2) as i:
                    for b in range(2):
                        gathers((i, t * H + b), b)

        @block.scalar
        def _(act):
            link = Link(act, act_step)
            for i, n in enumerate(("c", "c_ctx", "c_2")):
                act.dma_start(cvec[:, i, :], A[n].rearrange("(p c) -> p c", c=DC)).then_inc(vec_in, 16)
            for i, n in enumerate(("norm_mix", "g_norm_mix_2")):
                act.dma_start(gcol[:, i, :], A[n].rearrange("(p c) -> p c", c=DC)).then_inc(vec_in, 16)
            for r in range(2):
                act.dma_start(modb[r:P:32, :, :], A["b_mod"].rearrange("(g j n) -> j g n", j=4, n=512)).then_inc(modb_in, 16)
            act.dma_start(convw_in[0:CONV_W, :], A["conv_w"]).then_inc(cw_in, 16)
            for i, n in enumerate(("conv_b", "conv_ln_g", "conv_ln_b")):
                act.dma_start(convw_in[CONV_W + i:CONV_W + i + 1, :], A[n].rearrange("(a n) -> a n", a=1)).then_inc(cw_in, 16)
            act.dma_start(wr[:, :, 0:NG], A["w_router_group"].rearrange("(p c) e -> p c e", c=DC)).then_inc(wr_in, 16)
            act.dma_start(wr[:, :, NG:NG + NE], A["w_router_expert"].rearrange("(p c) e -> p c e", c=DC)).then_inc(wr_in, 16)
            act.dma_start(br[:, 0:NG], A["b_router_group"].partition_broadcast(P)).then_inc(wr_in, 16)
            act.dma_start(br[:, NG:NG + NE], A["b_router_expert"].partition_broadcast(P)).then_inc(wr_in, 16)
            act.dma_start(wf[:, :, :], A["w_in_2"][:, FOX_W:FOX_W + H].rearrange("(p c) e -> p c e", c=DC)).then_inc(wr_in, 16)
            act.dma_start(bf[:, :], A["b_forget_2"].partition_broadcast(P)).then_inc(wr_in, 16)
            for i, n in enumerate(("g_out_fox_2", "g_out_sb_2")):
                for half in range(2):
                    act.dma_start(gob[HD * half:HD * half + HD, i:i + 1], A[n].rearrange("(d a) -> d a", a=1)).then_inc(wr_in, 16)
            act.wait_ge(vec_in, 16 * 5)
            link(act.activation(cvec[:, :, :], cvec[:, :, :], ACT.Silu), silu_c)
            act.wait_ge(x_in, 32)
            for i in range(CT + TT):
                row = cr[:, i, :] if i < CT else xr[:, i - CT, :]
                link(act.activation(junk, row, ACT.Square, accum_out=ssq[:, i:i + 1]), ssq_done)
            act.wait_ge(ms_done, 1)
            link(act.activation(rms[:, 0:6], rms_t[:, 0:6], ACT.Sqrt), root_done)
            act.wait_ge(acol_done, 2)
            for g in range(2 * DC):
                act.wait_ge(xT_done, g + 1)
                c = g % DC
                if g < DC:
                    link(act.activation(hcT[:, c, :], bank[4 + g % 4][:, 0:CTX], ACT.Identity,
                                        scale=acol[:, 1, c:c + 1], bias=mcol_c[:, 0, c:c + 1]), hT_done)
                else:
                    link(act.activation(hT[:, c, :], bank[4 + g % 4][:, :], ACT.Identity,
                                        scale=acol[:, 0, c:c + 1], bias=mcol[:, 0, c:c + 1]), hT_done)
            for cc in range(CC):
                act.wait_ge(glu_done, cc + 1)
                if cc >= 2:
                    act.wait_ge(u_done, cc - 1)
                link(act.activation(sig[cc % 2], bank[2 * (cc % 2) + 1][:, :], ACT.Sigmoid), sig_done)
            act.wait_ge(mod_out, 16 * 4)
            act.wait_ge(mod_out_rest, 16 * 8)
            for m in range(18):
                act.wait_ge(proj_done, m + 1)
                src = bank[4 + m % 4]
                if m < 4:
                    link(act.activation(kT[:, m, :], src[:, :], ACT.Copy), proj_out)
                elif m < 8:
                    link(act.activation(qT[:, m - 4, :], src[:, :], ACT.Copy, scale=HD ** -0.5), proj_out)
                elif m < 12:
                    link(act.activation(kcT[:, m - 8, :], src[:, 0:CTX], ACT.Copy), proj_out)
                elif m < 16:
                    link(act.activation(vrow[:, m - 12, :], src[:, :], ACT.Copy), proj_out)
                else:
                    link(act.activation(vcrow[:, m - 16, :], src[:, :], ACT.Copy), proj_out)
            act.wait_ge(ccen_done, CC)
            for cc in range(CC):
                link(act.activation(conv_sq[:, cc, :], conv[:, cc, :], ACT.Square), csq_done)
            act.wait_ge(cms_done, 1)
            link(act.activation(conv_r, conv_t, ACT.Sqrt), croot_done)
            for cc in range(CC):
                act.wait_ge(cnorm_done, cc + 1)
                link(act.activation(conv[:, cc, :], conv[:, cc, :], ACT.Silu, scale=convc[:, cc, CONV_W + 1:CONV_W + 2],
                                    bias=convc[:, cc, CONV_W + 2:CONV_W + 3]), convy_done)

            def probs_out(n):
                act.wait_ge(pT_done, n + 1)
                if n >= 2:
                    act.wait_ge(o_done, n - 1)
                link(act.activation(probT[n % 2][:, 0:4, :], bank[4][:, :].rearrange("p (a b) -> p a b", b=P), ACT.Copy), pTa_out)

            for n in range(H * TT):
                act.wait_ge(nmax_done, n + 1)
                link(act.activation(prob[n % 2][:, 0:T], prob[n % 2][:, 0:T], ACT.Exp, bias=smx[:, n % 2, 2:3],
                                    accum_out=ssum[:, 0, n:n + 1]))
                link(act.activation(prob[n % 2][:, T:KEYS], bank[2 + n % 2][:, 0:CTX], ACT.Exp, bias=smx[:, n % 2, 2:3],
                                    accum_out=ssum[:, 1, n:n + 1]), p_done)
                if n >= 1:
                    probs_out(n - 1)
            probs_out(H * TT - 1)
            for k in range(AC):
                act.wait_ge(attT_pe, k + 1)
                link(act.activation(attT[:, k, :], bank[k][:, :], ACT.Copy), attT_done)
            act.wait_ge(s_done, H * TT)
            act.dma_start(modb[0:P:32, :, :], A["b_ada_2"].rearrange("(g j n) -> j g n", j=4, n=512)).then_inc(modb2_in, 16)
            for c in range(DC):
                act.wait_ge(merge_pe, c + 1)
                if c >= 2:
                    act.wait_ge(mix_done, c - 1)
                link(act.activation(gate_a[c % 2], bank[4 * (c % 2)][:, :], ACT.Sigmoid))
                link(act.activation(gate_c[c % 2], bank[4 * (c % 2) + 1][:, :], ACT.Sigmoid), gates_done)
            def second_norm(t, block, junk):
                n = block * TT + t
                act.wait_ge(res_done, 2 * n + 2)
                link(act.activation(junk, xr[:, t, :], ACT.Square, accum_out=ssq[:, t:t + 1]), ssq_done)
                act.wait_ge(ms_done, MS_2ND[block] + t + 1)
                link(act.activation(rms[:, t:t + 1], rms_t[:, t:t + 1], ACT.Sqrt), root_done)
                act.wait_ge(h2T_pe, n + 1)
                for i in range(2):
                    link(act.activation(h2T[:, 4 * i:4 * i + 4, t * P:(t + 1) * P],
                                        bank[2 * t + i][:, :].rearrange("p (a b) -> p a b", b=P), ACT.Copy), h2T_done)

            for t in range(TT):
                second_norm(t, 0, junk2)
            act.wait_ge(gsub_done, 1)
            link(act.activation(gexp, gexp, ACT.Exp), gexp_done)
            act.wait_ge(gsub_done, 2)
            link(act.activation(dexp, dval, ACT.Exp), gexp_done)

            def expert(e, b, i):
                act.wait_ge(xbT_done, e + 1)
                unless_first(act, gu_done, e - 1)
                act.activation(xbT[b], bank[b][:, :].rearrange("p (a c) -> p a c", c=CAP), ACT.Copy).then_inc(xbT_out, 1)
                act.wait_ge(gu_done, e + 1)
                unless_first(act, hid_done, e - 1)
                act.activation(silu_g[b], bank[2 + b][:, 0:256], ACT.Silu).then_inc(silu_done, 1)
                act.wait_ge(dn_done, e + 1)
                unless_first(act, y_dma[b], i * 32)
                act.activation(yblk[b], bank[6 + b][:, :], ACT.Copy).then_inc(yv_done, 1)
                act.wait_ge(yv_done, e + 1)
                for half in range(2):
                    act.dma_start(ys_d[bass.ds(e * CAP, CAP), 512 * half:512 * half + 512],
                                  yblk[b][CAP * half:CAP * half + CAP, :]).then_inc(y_dma[b], 16)

            for b in range(2):
                expert(b, b, 0)
            with act.Fori(1, NE // 2) as i:
                for b in range(2):
                    expert(i * 2 + b, b, i)
            act.wait_ge(route_done, 1)
            n_over = act.value_load(over_i[0:1, 0:1], min_val=0, max_val=OVER)
            with act.Fori(0, OVER) as i:
                with act.If(i < n_over):
                    act.wait_ge(xbT_done, i + (NE + 1))
                    act.activation(xbT[0], bank[0][:, :].rearrange("p (a c) -> p a c", c=CAP), ACT.Copy).then_inc(xbT_out, 1)
                    act.wait_ge(gu_done, i + (NE + 1))
                    act.activation(silu_g[0], bank[2][:, 0:256], ACT.Silu).then_inc(silu_done, 1)
                    act.wait_ge(y_dma[0], 32 * (NE // 2))
                    act.wait_ge(dn_done, i + (NE + 1))
                    act.activation(yblk[0], bank[6][:, :], ACT.Copy).then_inc(yv_done, 1)
            for t in range(TT):
                act.wait_ge(comb_done, t + 1)
                link(act.activation(junk2, xr[:, t, :], ACT.Square, accum_out=ssq[:, t:t + 1]), ssq_done)
            act.wait_ge(ms_done, MS_FINAL + 1)
            link(act.activation(rms[:, 0:TT], rms_t[:, 0:TT], ACT.Sqrt), root_done)
            for t in range(TT):
                act.wait_ge(x2_done, t + 1)
                link(act.activation(junk2, xr[:, t, :], ACT.Square, accum_out=ssq[:, t:t + 1]), ssq_done)
            act.wait_ge(ms_done, MS_1ST + 1)
            link(act.activation(rms[:, 0:TT], rms_t[:, 0:TT], ACT.Sqrt), root_done)
            act.wait_ge(acol2_done, 1)
            for c in range(DC):
                act.wait_ge(xT_done, 2 * DC + c + 1)
                link(act.activation(hT[:, c, :], bank[c][:, :], ACT.Identity, scale=acol[:, 2, c:c + 1], bias=mcol_2[:, 0, c:c + 1]), hT_done)
            def soft(x, done):
                link(act.activation(x, x, ACT.Exp))
                link(act.activation(x, x, ACT.Ln, bias=ones[:, 0:1]), done)

            act.wait_ge(f_dve, 1)
            soft(fabs, f_act)
            for m in range(24):
                act.wait_ge(proj_done, 18 + m + 1)
                dst, scale = ((sqT, HD ** -0.5), (skT_, 1.0), (svr, 1.0), (fqT, HD ** -0.5), (fkT, 1.0), (fvr, 1.0))[m // 4]
                link(act.activation(dst[:, m % 4, :], bank[m % 8][:, :], ACT.Copy, scale=scale), proj_out)
            act.wait_ge(f_pe, 3)
            link(act.activation(fcumT, bank[1][0:H, :], ACT.Copy, scale=-1.0), f_act)

            def stick_soft(h):
                x = stick_a[h % 2]
                act.wait_ge(sba_done, h + 1)
                for i, w in ((slice(0, 2), 512), (2, 256)):
                    link(act.activation(x[:, i, 0:w], x[:, i, 0:w], ACT.Exp))
                    link(act.activation(x[:, i, 0:w], x[:, i, 0:w], ACT.Ln, bias=ones[:, 0:1]), sbl_done)

            def stick_exp(h):
                x = stick_b[h % 2]
                act.wait_ge(sbc_done, h + 1)
                link(act.activation(x[:, 0:2, :], x[:, 0:2, :], ACT.Exp))
                link(act.activation(x[:, 2, 0:256], x[:, 2, 0:256], ACT.Exp), sbe_done)

            def stick_out(h):
                act.wait_ge(sbo_pe, h + 1)
                link(act.activation(mixed[:, :, DA + h * HD:DA + h * HD + HD], bank[6][:, 0:256].rearrange("p (t d) -> p t d", d=HD),
                                    ACT.Copy), sbo_done)

            def fox_exp(n):
                w = (n % TT + 1) * P
                act.wait_ge(nmax_done, H * TT + n + 1)
                if n >= 2:
                    act.wait_ge(pT_done, H * TT + n - 1)
                link(act.activation(fprob[n % 2][:, 0:w], bank[3 + n % 2][:, 0:w], ACT.Exp, bias=smx[:, n % 2, 2:3],
                                    accum_out=ssum[:, 0, n:n + 1]), p_done)

            def fox_T(n):
                w = (n % TT + 1) * P
                act.wait_ge(pT_done, H * TT + n + 1)
                if n >= 2:
                    act.wait_ge(o_done, H * TT + n - 1)
                link(act.activation(fprobT[n % 2][:, 0:w], bank[5][:, 0:w], ACT.Copy), pTa_out)

            for h in range(H):
                stick_soft(h)
                if h >= 1:
                    stick_out(h - 1)
                for t in range(TT):
                    n = h * TT + t
                    fox_exp(n)
                    if n >= 1:
                        fox_T(n - 1)
                    if t == 2:
                        stick_exp(h)
            stick_out(H - 1)
            fox_T(H * TT - 1)
            act.wait_ge(att_done, 2 * H)
            for t in range(TT):
                if t >= 2:
                    act.wait_ge(mms_done, t - 1)
                link(act.activation(msq[t % 2], mixed[:, t, :], ACT.Square), msq_done)
            act.wait_ge(mms_done, TT + 1)
            link(act.activation(mrt, mss, ACT.Sqrt), mroot_done)
            act.wait_ge(wr_in, 16 * 10)
            for k in range(DC):
                act.wait_ge(attT_pe, AC + k + 1)
                link(act.activation(mixT2[:, k, :], bank[k][:, :], ACT.Copy, scale=gob[:, k // AC:k // AC + 1]), attT_done)
            for t in range(TT):
                second_norm(t, 1, nf_2)
            for m in range(4 * TT):
                act.wait_ge(q_pe, m + 1)
                at = (m // 4) * H + 2 * (m % 4)
                link(act.activation(qT2[:, at:at + 2, :], bank[m % 8][:, :].rearrange("p (a b) -> p a b", a=2), ACT.Copy), q_done)
            for m in range(4):
                act.wait_ge(skT_pe, m + 1)
                link(act.activation(skT[:, 2 * m:2 * m + 2, :], bank[m][:, :].rearrange("p (a b) -> p a b", a=2), ACT.Copy), skT_done)
            link(act.activation(skT[:, H, :], bank[0][:, 0:2 * P], ACT.Copy), skT_done)

            def queries(n):
                i, off = n
                if off > 0:
                    act.wait_ge(sc_pe, at_head(n, 1, 0))
                    act.sem_inc(mark, 1)
                src = qT2[:, off, :] if i is None else qT2[:, bass.ds(i * 2 + off, 1), :].rearrange("p a b -> p (a b)")
                act.activation(qh.rearrange("p a b -> p (a b)"), src, ACT.Copy).then_inc(qh_done, 1)

            def gate_exp(n):
                act.wait_ge(gsub2_done, at_head(n, 1, 1))
                act.activation(gex, gsub, ACT.Exp, accum_out=gsum).then_inc(gex_done, 1)

            def peer_head(n, more):
                nxt = (n[0], n[1] + 1)

                def gelu(g):
                    act.wait_ge(down_free, at_head(n, UP_SETS, DOWN_SETS + g + 1))
                    act.activation(gel[:, G4 * g:G4 * g + G4], dots[:, G4 * g:G4 * g + G4], ACT.Gelu).then_inc(gelu_done, 1)

                def diagonals(g):
                    act.wait_ge(up_free, at_head(n, UP_SETS, g + 1))
                    act.wait_ge(coef_done, at_head(n, UP_SETS, g + 1))
                    for r in range(G4 * g, G4 * g + G4):
                        d = act.activation(diag[:, r, :], ident[:, :], ACT.Copy, scale=coef[:, r:r + 1])
                    d.then_inc(diag_done, 1)

                if more:
                    queries(nxt)
                gelu(0)
                gelu(1)
                diagonals(0)
                if more:
                    gate_exp(nxt)
                gelu(2)
                diagonals(1)
                gelu(3)
                diagonals(2)
                diagonals(3)

            def last_norm(t):
                act.wait_ge(fin_add, t + 1)
                link(act.activation(h2r_2[:, t, :], xr[:, t, :], ACT.Square, accum_out=ssq[:, t:t + 1]), ssq_done)
                act.wait_ge(ms_done, MS_LAST + t + 1)
                link(act.activation(rms[:, t:t + 1], rms_t[:, t:t + 1], ACT.Sqrt), root_done)

            queries((None, 0))
            gate_exp((None, 0))
            for t in range(TT):
                last = t == TT - 1
                with act.Fori(0, H // 2 - last) as i:
                    for b in range(2):
                        peer_head((i, t * H + b), True)
                if last:
                    peer_head((None, TT * H - 2), True)
                    peer_head((None, TT * H - 1), False)
                if t >= 1:
                    last_norm(t - 1)
            last_norm(TT - 1)

        @block.vector
        def _(dve):
            link = Link(dve, dve_step)

            def inv_root(n, root, last=None):
                dve.wait_ge(*root)
                r, v, s = n
                link(dve.reciprocal(r, r))
                link(dve.tensor_tensor(s, r, r, ALU.mult))
                link(dve.tensor_tensor(s, s, v, ALU.mult))
                link(dve.tensor_scalar(s, s, -0.5, 1.5, ALU.mult, ALU.add))
                link(dve.tensor_tensor(r, r, s, ALU.mult), last)

            dve.wait_ge(consts, 1)
            link(dve.tensor_copy(iota[:, :], iota_i[:, :]))
            link(dve.tensor_copy(wstart[:, 0:1], part_i[:, :]))
            link(dve.tensor_scalar(wstart[:, 1:2], wstart[:, 0:1], float(GRID_W), -float(GRID_W), ALU.is_ge, ALU.mult))
            link(dve.tensor_tensor(wstart[:, 0:1], wstart[:, 0:1], wstart[:, 1:2], ALU.add))
            link(dve.tensor_scalar(wstart[:, 2:3], wstart[:, 0:1], -float(WIN // 2), 0.0, ALU.add, ALU.max))
            link(dve.tensor_scalar(wstart[:, 2:3], wstart[:, 2:3], float(GRID_W - WIN), None, ALU.min))
            link(dve.tensor_scalar(wstart[:, 3:4], wstart[:, 2:3], float(WIN), None, ALU.add))
            link(dve.tensor_scalar(band_t[:, 0, :], iota[:, :], wstart[:, 2:3], None, ALU.is_ge))
            link(dve.tensor_scalar(band_t[:, 1, :], iota[:, :], wstart[:, 3:4], None, ALU.is_lt))
            link(dve.tensor_tensor(band[:, :], band_t[:, 0, :], band_t[:, 1, :], ALU.mult))
            link(dve.tensor_scalar(band[:, :], band[:, :], -NEG, NEG, ALU.mult, ALU.add))

            dve.wait_ge(ssq_done, CT + TT)
            link(dve.tensor_scalar(rms_t[:, 0:6], ssq[:, 0:6], 1.0 / D, EPS, ALU.mult, ALU.add), ms_done)
            inv_root((rms[:, 0:6], rms_t[:, 0:6], ssq[:, 0:6]), (root_done, 1))
            for i in range(CT + TT):
                row = cr[:, i, :] if i < CT else xr[:, i - CT, :]
                link(dve.tensor_scalar(row, row, rms[:, i:i + 1], None, ALU.mult), xn_done)

            def mod_row(j, rows):
                at = slice(32 * (j % 4), 32 * (j % 4) + rows)
                link(dve.tensor_tensor(modr[at, j // 4, :], bank[j // 4][at, :], modb[at, j // 4, :], ALU.add), mod_rows)

            dve.wait_ge(modb_in, 32)
            for j in range(12):
                dve.wait_ge(pe_mod, j // 4 + 1)
                mod_row(j, 2)
                if j == 3:
                    dve.wait_ge(mcol_in, 32)
                    link(dve.scalar_tensor_tensor(out=acol[:, 0, :], in0=mcol[:, 1, :], scalar=1.0, in1=gcol[:, 0, :],
                                                  op0=ALU.add, op1=ALU.mult), acol_done)
                    link(dve.scalar_tensor_tensor(out=acol[:, 1, :], in0=mcol_c[:, 1, :], scalar=1.0, in1=gcol[:, 0, :],
                                                  op0=ALU.add, op1=ALU.mult), acol_done)
            dve.wait_ge(convw_T, CC)
            link(dve.tensor_copy(convc[:, :, :], bank[3][:, 0:CC * 34].rearrange("p (a b) -> p a b", b=34)), convc_done)
            dve.wait_ge(xT_done, 2 * DC)
            link(dve.memset(u_pad[:, :, 0:PADC], 0.0))
            link(dve.memset(u_pad[:, :, PADC + T:UW], 0.0))
            for cc in range(CC):
                dve.wait_ge(sig_done, cc + 1)
                link(dve.tensor_tensor(u_pad[:, cc, PADC:PADC + T], bank[2 * (cc % 2)][:, :], sig[cc % 2], ALU.mult), u_done)
            for cc in range(CC):
                link(dve.tensor_scalar(conv[:, cc, :], u_pad[:, cc, 0:T], convc[:, cc, 0:1], convc[:, cc, CONV_W:CONV_W + 1],
                                       ALU.mult, ALU.add))
                for k in range(1, CONV_W):
                    link(dve.scalar_tensor_tensor(out=conv[:, cc, :], in0=u_pad[:, cc, k:k + T], scalar=convc[:, cc, k:k + 1],
                                                  in1=conv[:, cc, :], op0=ALU.mult, op1=ALU.add),
                         conv_done if k == CONV_W - 1 else None)
            dve.wait_ge(cmean_done, 1)
            for cc in range(CC):
                link(dve.tensor_tensor(conv[:, cc, :], conv[:, cc, :], bank[0][:, :], ALU.subtract), ccen_done)
            dve.wait_ge(cvar_done, 1)
            dve.wait_ge(skew_out, 16)
            link(dve.tensor_scalar(conv_t, bank[1][:, :], EPS, None, ALU.add), cms_done)
            inv_root((conv_r, conv_t, conv_sq[:, 0, :]), (croot_done, 1))
            for cc in range(CC):
                link(dve.tensor_tensor(conv[:, cc, :], conv[:, cc, :], conv_r, ALU.mult), cnorm_done)

            def probs_out(n):
                dve.wait_ge(pT_done, n + 1)
                if n >= 2:
                    dve.wait_ge(o_done, n - 1)
                link(dve.tensor_copy(probT[n % 2][:, 4:6, :], bank[5][:, 0:2 * P].rearrange("p (a b) -> p a b", b=P)), pTb_out)

            def head_out(h):
                dve.wait_ge(o_done, TT * (h + 1))
                at = slice(TT * h, TT * h + TT)
                link(dve.tensor_tensor(rinv[:, 0:TT], ssum[:, 0, at], ssum[:, 1, at], ALU.add))
                link(dve.reciprocal(rinv[:, 0:TT], rinv[:, 0:TT]))
                link(dve.tensor_tensor(att[:, :, h * HD:(h + 1) * HD],
                                       bank[6 + h % 2][:, 0:TT * HD].rearrange("p (t d) -> p t d", d=HD),
                                       rinv[:, 0:TT].unsqueeze(2).broadcast_to([P, TT, HD]), ALU.mult), att_done)

            for n in range(H * TT):
                h, t = n // TT, n % TT
                if t == 0:
                    dve.wait_ge(bias_in[h % 2], 32 * (h // 2 + 1))
                    link(dve.tensor_tensor(bias[h % 2], bias[h % 2], band[:, :].unsqueeze(1).broadcast_to([P, 14, 64]), ALU.add))
                dve.wait_ge(s_done, n + 1)
                if n >= 2:
                    dve.wait_ge(pT_done, n - 1)
                at = 6 - 2 * t
                link(dve.tensor_tensor(prob[n % 2][:, 0:T], bank[n % 2][:, :],
                                       bias[h % 2][:, at:at + ROWS, :].rearrange("p a b -> p (a b)"), ALU.add))
                link(dve.tensor_reduce(smx[:, n % 2, 0:1], prob[n % 2][:, 0:T], AX, ALU.max))
                link(dve.tensor_reduce(smx[:, n % 2, 1:2], bank[2 + n % 2][:, 0:CTX], AX, ALU.max))
                link(dve.tensor_scalar(smx[:, n % 2, 2:3], smx[:, n % 2, 0:1], smx[:, n % 2, 1:2], -1.0, ALU.max, ALU.mult), nmax_done)
                if n >= 1:
                    probs_out(n - 1)
                if n >= 2 and (n - 2) % TT == TT - 1:
                    head_out((n - 2) // TT)
            probs_out(H * TT - 1)
            head_out(H - 1)
            dve.wait_ge(modb2_in, 16)
            for j in range(12):
                dve.wait_ge(pe_mod, 3 + j // 4 + 1)
                mod_row(j, 1)
            dve.wait_ge(mod2_out, 16 * 12)
            for c in range(DC):
                dve.wait_ge(gates_done, c + 1)
                b = 4 * (c % 2)
                link(dve.tensor_tensor(gate_a[c % 2], bank[b + 2][:, :], gate_a[c % 2], ALU.mult))
                link(dve.tensor_tensor(gate_c[c % 2], bank[b + 3][:, :], gate_c[c % 2], ALU.mult))
                link(dve.tensor_tensor(mixT[:, c, :], gate_a[c % 2], gate_c[c % 2], ALU.add), mix_done)
            dve.wait_ge(rows_in, 16 * 5)
            link(dve.scalar_tensor_tensor(out=a2_b, in0=a2_b, scalar=1.0, in1=tmp2, op0=ALU.add, op1=ALU.mult))
            def second_norm(t, block, g1, a2, sh2, h2, tmp):
                n = block * TT + t
                for j in range(2):
                    at = slice(j * 512, j * 512 + 512)
                    dve.wait_ge(wo_pe, 2 * n + j + 1)
                    link(dve.tensor_tensor(tmp, bank[2 * t + j][:, :], g1[:, at], ALU.mult))
                    link(dve.tensor_tensor(xr[:, t, at], xr[:, t, at], tmp, ALU.add), res_done)
                dve.wait_ge(ssq_done, SQ_2ND[block] + t + 1)
                one = slice(t, t + 1)
                link(dve.tensor_scalar(rms_t[:, one], ssq[:, one], 1.0 / D, EPS, ALU.mult, ALU.add), ms_done)
                inv_root((rms[:, one], rms_t[:, one], ssq[:, one]), (root_done, MS_2ND[block] + t + 1))
                link(dve.tensor_scalar(h2[:, t, :], xr[:, t, :], rms[:, one], None, ALU.mult))
                link(dve.tensor_tensor(h2[:, t, :], h2[:, t, :], a2, ALU.mult))
                link(dve.tensor_tensor(h2[:, t, :], h2[:, t, :], sh2, ALU.add), h2_done)

            dve.wait_ge(xres_in, 16)
            for t in range(TT):
                second_norm(t, 0, g1_b, a2_b, sh2_b, h2r, tmp[:, 0:512])
            link(dve.memset(lgp, NEG))
            for t in range(TT):
                dve.wait_ge(logit_pe, t + 1)
                link(dve.tensor_tensor(lg[:, t, :], bank[2 * t][:, 0:NG + NE], br[:, :], ALU.add))
            link(dve.tensor_copy(lgp[:, :, 0:NG], lg[:, :, 0:NG]))
            for t in range(TT):
                link(dve.max(gval[:, t, :], lgp[:, t, :]))
                link(dve.max_index(ridx[:, 0, t, :], gval[:, t, :], lgp[:, t, :]))
            link(dve.tensor_tensor(gexp, lg[:, :, 0:NG], gval[:, :, 0:1].broadcast_to([P, TT, NG]), ALU.subtract), gsub_done)
            link(dve.tensor_copy(gif, ridx[:, 0, :, 0]))
            link(dve.tensor_tensor(oneh, iota[:, 0:NG].unsqueeze(1).broadcast_to([P, TT, NG]),
                                   gif.unsqueeze(2).broadcast_to([P, TT, NG]), ALU.is_equal))
            link(dve.tensor_scalar(pen, oneh, 1.0, -NEG, ALU.subtract, ALU.mult))
            em = emask.rearrange("p t (g e) -> p t g e", e=EPG)
            link(dve.tensor_tensor(em, lg[:, :, NG:NG + NE].rearrange("p t (g e) -> p t g e", e=EPG),
                                   oneh.unsqueeze(3).broadcast_to([P, TT, NG, EPG]), ALU.mult))
            link(dve.tensor_tensor(em, em, pen.unsqueeze(3).broadcast_to([P, TT, NG, EPG]), ALU.add))
            for t in range(TT):
                link(dve.max(eval_[:, t, :], emask[:, t, :]))
                link(dve.max_index(ridx[:, 1, t, :], eval_[:, t, :], emask[:, t, :]))
            link(dve.tensor_tensor(dval, eval_[:, :, 1], eval_[:, :, 0], ALU.subtract), gsub_done)
            link(dve.tensor_copy(eif, ridx[:, 1, :, 0:2]))
            for s in range(2):
                link(dve.tensor_tensor(pick[:, s, :, :], iota[:, 0:NE].unsqueeze(1).broadcast_to([P, TT, NE]),
                                       eif[:, :, s:s + 1].broadcast_to([P, TT, NE]), ALU.is_equal))
            link(dve.tensor_tensor(both, pick[:, 0, :, :], pick[:, 1, :, :], ALU.add), both_done)
            dve.wait_ge(gexp_done, 1)
            link(dve.tensor_reduce(psum_, gexp, AX, ALU.add))
            link(dve.reciprocal(psum_, psum_))
            dve.wait_ge(gexp_done, 2)
            link(dve.tensor_scalar(dden, dexp, 1.0, None, ALU.add))
            link(dve.reciprocal(dden, dden))
            link(dve.tensor_tensor(gw[:, 0, :], dden, psum_, ALU.mult))
            link(dve.tensor_tensor(gw[:, 1, :], gw[:, 0, :], dexp, ALU.mult))
            dve.wait_ge(rank_pe, 1)
            link(dve.tensor_copy(rank, bank[1][:, 0:TT * NE].rearrange("p (t e) -> p t e", e=NE)))
            link(dve.tensor_copy(cnt, bank[1][:, TT * NE:TT * NE + NE]))
            link(dve.tensor_scalar(nblk, cnt, float(CAP), None, ALU.is_gt))
            for k in range(2, T // CAP):
                link(dve.scalar_tensor_tensor(out=nblk, in0=cnt, scalar=float(CAP * k), in1=nblk, op0=ALU.is_gt, op1=ALU.add))
            a, b = incl, incl2
            link(dve.tensor_copy(a, nblk))
            for sh in (1, 2, 4, 8, 16):
                link(dve.tensor_copy(b[:, 0:sh], a[:, 0:sh]))
                link(dve.tensor_tensor(b[:, sh:NE], a[:, sh:NE], a[:, 0:NE - sh], ALU.add))
                a, b = b, a
            total = a
            link(dve.tensor_scalar(e64, iota[:, 0:NE], float(CAP), None, ALU.mult))
            link(dve.tensor_tensor(delta, total, nblk, ALU.subtract))
            link(dve.tensor_scalar(delta, delta, float(CAP), float(NE * CAP - CAP), ALU.mult, ALU.add))
            link(dve.tensor_tensor(delta, delta, e64, ALU.subtract))
            link(dve.tensor_scalar(over_at, rank, float(CAP), None, ALU.is_ge))
            link(dve.tensor_tensor(over_at, over_at, delta.unsqueeze(1).broadcast_to([P, TT, NE]), ALU.mult))
            link(dve.tensor_tensor(over_at, over_at, rank, ALU.add))
            link(dve.tensor_tensor(over_at, over_at, e64.unsqueeze(1).broadcast_to([P, TT, NE]), ALU.add))
            for s in range(2):
                link(dve.tensor_tensor(sel, pick[:, s, :, :], over_at, ALU.mult))
                link(dve.tensor_reduce(slot_f[:, s, :], sel, AX, ALU.add))
            link(dve.tensor_copy(slot_i[:, :, :], slot_f))
            link(dve.tensor_tensor(tab, total.unsqueeze(1).broadcast_to([P, OVER, NE]),
                                   iota[:, 0:OVER].unsqueeze(2).broadcast_to([P, OVER, NE]), ALU.is_le))
            link(dve.tensor_reduce(tab_e, tab, AX, ALU.add))
            link(dve.tensor_scalar(tab_e, tab_e, float(NE - 1), None, ALU.min))
            link(dve.tensor_copy(over_i[:, 1:1 + OVER], tab_e))
            link(dve.tensor_copy(over_i[:, 0:1], total[:, NE - 1:NE]), route_done)

            def expert(e, b):
                dve.wait_ge(silu_done, e + 1)
                unless_first(dve, hidT_pe, e - 1)
                dve.tensor_tensor(hid[b], silu_g[b], bank[2 + b][:, 256:512], ALU.mult).then_inc(hid_done, 1)
                dve.wait_ge(hidT_pe, e + 1)
                unless_first(dve, dn_done, e - 1)
                dve.tensor_copy(hidT[b], bank[4 + b][:, 0:256].rearrange("p (k r) -> p k r", k=2)).then_inc(hidT_done, 1)

            for b in range(2):
                expert(b, b)
            with dve.Fori(1, NE // 2) as i:
                for b in range(2):
                    expert(i * 2 + b, b)
            n_over = dve.value_load(over_i[0:1, 0:1], min_val=0, max_val=OVER)
            with dve.Fori(0, OVER) as i:
                with dve.If(i < n_over):
                    dve.wait_ge(silu_done, i + (NE + 1))
                    dve.tensor_tensor(hid[0], silu_g[0], bank[2][:, 256:512], ALU.mult).then_inc(hid_done, 1)
                    dve.wait_ge(hidT_pe, i + (NE + 1))
                    dve.tensor_copy(hidT[0], bank[4][:, 0:256].rearrange("p (k r) -> p k r", k=2)).then_inc(hidT_done, 1)
            for t in range(TT):
                dve.wait_ge(yg_in[t], 32)
                y0, y1 = ygat[t % 2]
                link(dve.tensor_scalar(y0, y0, gw[:, 0, t:t + 1], None, ALU.mult))
                link(dve.scalar_tensor_tensor(out=y0, in0=y1, scalar=gw[:, 1, t:t + 1], in1=y0, op0=ALU.mult, op1=ALU.add))
                link(dve.tensor_tensor(y0, y0, g2_b, ALU.mult))
                link(dve.tensor_tensor(xr[:, t, :], xr[:, t, :], y0, ALU.add), comb_done)
            allt = slice(0, TT)
            dve.wait_ge(ssq_done, SQ_FINAL + TT)
            link(dve.tensor_scalar(rms_t[:, allt], ssq[:, allt], 1.0 / D, EPS, ALU.mult, ALU.add), ms_done)
            inv_root((rms[:, allt], rms_t[:, allt], ssq[:, allt]), (root_done, MS_FINAL + 1))
            dve.wait_ge(fn_in, 16)
            for t in range(TT):
                link(dve.scalar_tensor_tensor(out=xr[:, t, :], in0=xr[:, t, :], scalar=rms[:, t:t + 1], in1=fn_b,
                                              op0=ALU.mult, op1=ALU.mult), x2_done)
            dve.wait_ge(ssq_done, SQ_1ST + TT)
            link(dve.tensor_scalar(rms_t[:, allt], ssq[:, allt], 1.0 / D, EPS, ALU.mult, ALU.add), ms_done)
            inv_root((rms[:, allt], rms_t[:, allt], ssq[:, allt]), (root_done, MS_1ST + 1))
            for t in range(TT):
                link(dve.tensor_scalar(xnb[:, t, :], xr[:, t, :], rms[:, t:t + 1], None, ALU.mult), xnb_done)
            dve.wait_ge(mcol2_in, 16)
            link(dve.scalar_tensor_tensor(out=acol[:, 2, :], in0=mcol_2[:, 1, :], scalar=1.0, in1=gcol[:, 1, :],
                                          op0=ALU.add, op1=ALU.mult), acol2_done)
            dve.wait_ge(f_pe, 1)
            dve.wait_ge(wr_in, 16 * 10)
            link(dve.tensor_tensor(flog, bank[0][:, 0:TT * H].rearrange("p (t h) -> p t h", h=H),
                                   bf[:, :].unsqueeze(1).broadcast_to([P, TT, H]), ALU.add))
            link(dve.scalar_tensor_tensor(out=fabs, in0=flog, scalar=-1.0, in1=flog, op0=ALU.mult, op1=ALU.min), f_dve)
            dve.wait_ge(f_act, 1)
            link(dve.scalar_tensor_tensor(out=flog, in0=flog, scalar=0.0, in1=fabs, op0=ALU.min, op1=ALU.subtract), f_dve)
            dve.wait_ge(f_pe, 2)
            link(dve.tensor_copy(fcum, bank[0][:, 0:TT * H].rearrange("p (t h) -> p t h", h=H)), f_dve)

            def stick_abs(h):
                x = stick_a[h % 2]
                dve.wait_ge(sbz_pe, h + 1)
                for i, w in enumerate(PIECES):
                    z = bank[i][:, 0:w]
                    link(dve.tensor_copy(x[:, i, 0:w], z))
                    link(dve.scalar_tensor_tensor(out=x[:, i, 0:w], in0=x[:, i, 0:w], scalar=-1.0, in1=x[:, i, 0:w], op0=ALU.mult, op1=ALU.min),
                         sba_done if i == 2 else None)

            def stick_beta(h):
                x, y = stick_a[h % 2], stick_b[h % 2]
                dve.wait_ge(sbl_done, 2 * h + 2)
                if h >= 2:
                    dve.wait_ge(sbo_pe, h - 1)
                for i, w in enumerate(PIECES):
                    link(dve.scalar_tensor_tensor(out=x[:, i, 0:w], in0=bank[i][:, 0:w], scalar=0.0, in1=x[:, i, 0:w], op0=ALU.max, op1=ALU.add))
                for i, w in enumerate(PIECES):
                    link(dve.tensor_tensor(y[:, i, 0:w], bank[i][:, 0:w], x[:, i, 0:w], ALU.subtract), sbb_done if i == 2 else None)

            def stick_rest(h):
                y = stick_b[h % 2]
                dve.wait_ge(sbr_pe, h + 1)
                for i, w in enumerate(PIECES):
                    link(dve.tensor_tensor(y[:, i, 0:w], bank[i][:, 0:w], y[:, i, 0:w], ALU.add), sbc_done if i == 2 else None)

            def fox_max(n):
                w = (n % TT + 1) * P
                dve.wait_ge(s_done, H * TT + n + 1)
                if n >= 2:
                    dve.wait_ge(p_done, H * TT + n - 1)
                link(dve.tensor_reduce(smx[:, n % 2, 0:1], bank[3 + n % 2][:, 0:w], AX, ALU.max))
                link(dve.tensor_scalar(smx[:, n % 2, 2:3], smx[:, n % 2, 0:1], -1.0, None, ALU.mult), nmax_done)

            def fox_out(h):
                dve.wait_ge(o_done, H * TT + TT * (h + 1))
                link(dve.reciprocal(rinv[:, 0:TT], ssum[:, 0, TT * h:TT * h + TT]))
                link(dve.tensor_tensor(mixed[:, :, h * HD:(h + 1) * HD], bank[7][:, 0:256].rearrange("p (t d) -> p t d", d=HD),
                                       rinv[:, 0:TT].unsqueeze(2).broadcast_to([P, TT, HD]), ALU.mult), att_done)

            for h in range(H):
                stick_abs(h)
                fox_max(h * TT)
                fox_max(h * TT + 1)
                stick_beta(h)
                fox_max(h * TT + 2)
                if h >= 1:
                    fox_out(h - 1)
                stick_rest(h)
                fox_max(h * TT + 3)
            fox_out(H - 1)
            for t in range(TT):
                dve.wait_ge(msq_done, t + 1)
                link(dve.tensor_reduce(mss[:, t, :], msq[t % 2].rearrange("p (h d) -> p h d", d=HD), AX, ALU.add), mms_done)
            link(dve.tensor_scalar(mss, mss, 1.0 / HD, EPS, ALU.mult, ALU.add), mms_done)
            inv_root((mrt, mss, msc), (mroot_done, 1))
            for t in range(TT):
                m = mixed[:, t, :].rearrange("p (h d) -> p h d", d=HD)
                link(dve.tensor_tensor(m, m, mrt[:, t, :].unsqueeze(2).broadcast_to([P, 2 * H, HD]), ALU.mult), mixed_done)
            dve.wait_ge(rows2_in, 16 * 4)
            link(dve.scalar_tensor_tensor(out=a2_2, in0=a2_2, scalar=1.0, in1=nf_2, op0=ALU.add, op1=ALU.mult))
            for t in range(TT):
                second_norm(t, 1, gt1_2, a2_2, sh2_2, h2r_2, tmp_2)

            TOPK_STEPS = 33

            def topk(n, b):
                k = 0

                def step(ins, hold=False):
                    nonlocal k
                    k += 1
                    ins.then_inc(topk_step, 1)
                    dve.wait_ge(topk_step, at_head(n, TOPK_STEPS, k))
                    if hold:
                        dve.sem_inc(mark, 1)

                def top16(val, idx, src, rest):
                    step(dve.max(val[:, 0:8], src), True)
                    step(dve.max_index(idx[:, 0:8], val[:, 0:8], src), True)
                    step(dve.match_replace(rest, val[:, 0:8], src, NEG), True)
                    step(dve.max(val[:, 8:16], rest), True)
                    step(dve.max_index(idx[:, 8:16], val[:, 8:16], rest), True)

                dve.wait_ge(sc_pe, at_head(n, 1, 1))
                dve.sem_inc(mark, 1)
                for p in range(2):
                    top16(hval[:, p, :], hidx[:, p, :], bank[0][:, p * P:(p + 1) * P], work[:, p, :])
                step(dve.tensor_copy(hidx_f, hidx[:, :, :]))
                step(dve.tensor_tensor(cand.rearrange("p (a b) -> p a b", b=K16), hval[:, 0, :].unsqueeze(2).broadcast_to([P, K16, K16]),
                                       hval[:, 1, :].unsqueeze(1).broadcast_to([P, K16, K16]), ALU.add), True)
                top16(top, pos, cand, cand2)
                step(dve.tensor_scalar(gsub, top, top[:, 0:1], None, ALU.subtract))
                step(dve.tensor_single_scalar(pos_hl[:, 0, :], pos[:, :], 4, ALU.logical_shift_right))
                step(dve.tensor_single_scalar(pos_hl[:, 1, :], pos[:, :], K16 - 1, ALU.bitwise_and))
                step(dve.tensor_copy(pos_f, pos_hl[:, :, :]))
                dve.sem_inc(gsub2_done, 1)
                for p in range(2):
                    step(dve.tensor_tensor(onehot, iota[:, 0:K16].unsqueeze(1).broadcast_to([P, K16, K16]),
                                           pos_f[:, p, :].unsqueeze(2).broadcast_to([P, K16, K16]), ALU.is_equal))
                    step(dve.tensor_tensor(onehot, onehot, hidx_f[:, p, :].unsqueeze(1).broadcast_to([P, K16, K16]), ALU.mult))
                    step(dve.tensor_reduce(half_i[:, p, :], onehot, AX, ALU.add))
                step(dve.scalar_tensor_tensor(out=id_f, in0=half_i[:, 0, :], scalar=float(P), in1=half_i[:, 1, :], op0=ALU.mult, op1=ALU.add))
                if n[1] >= 2:
                    dve.wait_ge(up_free, at_head(n, UP_SETS, 0))
                dve.tensor_copy(ids[b][:, :], id_f).then_inc(ids_done, 1)
                dve.wait_ge(gex_done, at_head(n, 1, 1))
                step(dve.reciprocal(gsum, gsum))
                step(dve.tensor_scalar(gate_p[b], gex, gsum, None, ALU.mult))
                while k < TOPK_STEPS:
                    k += 1
                    dve.sem_inc(topk_step, 1)
                assert k == TOPK_STEPS

            def peer_head(n, b, t, more):
                def dot(g):
                    dve.wait_ge(down_in[g % DOWN_SETS], at_head(n, 16 * G4 * (UP_SETS // DOWN_SETS), 16 * G4 * (g // DOWN_SETS + 1)))
                    for k in range(G4):
                        r = G4 * g + k
                        buf = down[r % (G4 * DOWN_SETS)]
                        d = dve.tensor_tensor_reduce(buf, buf, h2r_2[:, t, :], 1.0, 0.0, ALU.mult, ALU.add, dots[:, r:r + 1])
                    d.then_inc(down_free, 1)

                def gated(g):
                    at = slice(G4 * g, G4 * g + G4)
                    dve.wait_ge(gelu_done, at_head(n, UP_SETS, g + 1))
                    dve.tensor_tensor(coef[:, at], gel[:, at], gate_p[b][:, at], ALU.mult).then_inc(coef_done, 1)

                dot(0)
                dot(1)
                gated(0)
                if more:
                    topk((n[0], n[1] + 1), 1 - b)
                dot(2)
                gated(1)
                dot(3)
                gated(2)
                gated(3)

            def last_norm(t):
                for j in range(2):
                    at = slice(512 * j, 512 * j + 512)
                    dve.wait_ge(peer_done, t + 1)
                    link(dve.tensor_tensor(tmp_p, bank[4 + 2 * (t % 2) + j][:, :], gt2_2[:, at], ALU.mult))
                    link(dve.tensor_tensor(xr[:, t, at], xr[:, t, at], tmp_p, ALU.add), fin_add if j == 1 else None)
                one = slice(t, t + 1)
                dve.wait_ge(ssq_done, SQ_LAST + t + 1)
                link(dve.tensor_scalar(rms_t[:, one], ssq[:, one], 1.0 / D, EPS, ALU.mult, ALU.add), ms_done)
                inv_root((rms[:, one], rms_t[:, one], ssq[:, one]), (root_done, MS_LAST + t + 1))
                link(dve.scalar_tensor_tensor(out=xr[:, t, :], in0=xr[:, t, :], scalar=rms[:, one], in1=gfin, op0=ALU.mult, op1=ALU.mult), fin_done)

            topk((None, 0), 0)
            for t in range(TT):
                last = t == TT - 1
                with dve.Fori(0, H // 2 - last) as i:
                    for b in range(2):
                        peer_head((i, t * H + b), b, t, True)
                if last:
                    peer_head((None, TT * H - 2), 0, t, True)
                    peer_head((None, TT * H - 1), 1, t, False)
                if t == 0:
                    dve.wait_ge(rows2_in, 16 * 6)
                if t >= 1:
                    last_norm(t - 1)
            last_norm(TT - 1)

        @block.tensor
        def _(pe):
            def project(dst, w, at, rhs, chunks=DC, stationary=None):
                for c in range(chunks):
                    mm = pe.matmul(dst, w[:, c, at], rhs[:, c, :], start=(c == 0), stop=(c == chunks - 1))
                return mm

            def rows_of(dst, xT, t, w, at, chunks=DC):
                for c in range(chunks):
                    mm = pe.matmul(dst, xT[:, c, t * P:(t + 1) * P], w[:, c, at], start=(c == 0), stop=(c == chunks - 1))
                return mm

            def modulation(n, q, vecs):
                for j in range(4):
                    slab_ready(pe, n + 4 * q + j)
                for c in range(DC):
                    for j in range(4):
                        mm = pe.matmul(bank[q][32 * j:32 * j + vecs.stop - vecs.start, :], cvec[:, vecs, c],
                                       slab(n + 4 * q + j)[:, c, :], start=(c == 0), stop=(c == DC - 1))
                mm.then_inc(pe_mod, 1)

            pe.wait_ge(consts, 1)
            pe.wait_ge(cw_in, 16 * 4)
            for cc in range(CC):
                pe.transpose(bank[3][:, 34 * cc:34 * cc + 34], convw_in[0:34, cc * P:(cc + 1) * P], ident[0:34, 0:34])\
                    .then_inc(convw_T, 1)
            pe.wait_ge(silu_c, 1)
            for q in range(3):
                modulation(N_MOD, q, slice(0, 2))
            for g in range(2 * DC):
                c = g % DC
                if g >= 4:
                    pe.wait_ge(hT_done, g - 3)
                if g == 0:
                    pe.wait_ge(xn_done, CT)
                if g == DC:
                    pe.wait_ge(xn_done, CT + TT)
                for t in range(CT if g < DC else TT):
                    src = cr if g < DC else xr
                    mm = pe.transpose(bank[4 + g % 4][:, t * P:(t + 1) * P], src[:, t, c:D:DC], ident[:, :])
                mm.then_inc(xT_done, 1)
            pe.wait_ge(hT_done, 2 * DC)
            pe.wait_ge(mod_rows, 12)
            pe.wait_ge(convc_done, 1)
            slab_ready(pe, N_GLU)
            slab_ready(pe, N_GLU + 1)
            for cc in range(CC):
                if cc >= 2:
                    pe.wait_ge(u_done, cc - 1)
                at = slice(cc * P, (cc + 1) * P)
                project(bank[2 * (cc % 2)][:, :], slab(N_GLU), at, hT)
                project(bank[2 * (cc % 2) + 1][:, :], slab(N_GLU + 1), at, hT).then_inc(glu_done, 1)

            def conv_mean():
                pe.wait_ge(conv_done, CC)
                for cc in range(CC):
                    mm = pe.matmul(bank[0][:, :], mean_w[:, :], conv[:, cc, :], start=(cc == 0), stop=(cc == CC - 1))
                mm.then_inc(cmean_done, 1)

            def conv_var():
                pe.wait_ge(csq_done, CC)
                for cc in range(CC):
                    mm = pe.matmul(bank[1][:, :], mean_w[:, :], conv_sq[:, cc, :], start=(cc == 0), stop=(cc == CC - 1))
                mm.then_inc(cvar_done, 1)

            for m in range(18):
                if m >= 4:
                    pe.wait_ge(proj_out, m - 3)
                dst = bank[4 + m % 4]
                if m < 4:
                    if m == 0:
                        slab_ready(pe, N_K)
                    mm = project(dst[:, :], slab(N_K), slice(m * P, (m + 1) * P), hT)
                elif m < 8:
                    if m == 4:
                        slab_ready(pe, N_Q)
                    mm = project(dst[:, :], slab(N_Q), slice((m - 4) * P, (m - 3) * P), hT)
                elif m < 12:
                    mm = project(dst[:, 0:CTX], slab(N_K), slice((m - 8) * P, (m - 7) * P), hcT)
                elif m < 16:
                    if m == 12:
                        slab_ready(pe, N_V)
                    mm = rows_of(dst[:, :], hT, m - 12, slab(N_V), slice(0, 512))
                else:
                    mm = rows_of(dst[:, :], hcT, m - 16, slab(N_V), slice(0, 512))
                mm.then_inc(proj_done, 1)
            conv_mean()
            conv_var()

            def scores(n):
                h, t = n // TT, n % TT
                if n >= 2:
                    pe.wait_ge(p_done, n - 1)
                at = slice(HD * (h % 2), HD * (h % 2) + HD)
                q = qT[at, h // 2, t * P:(t + 1) * P]
                pe.matmul(bank[n % 2][:, :], q, kT[at, h // 2, :], start=True, stop=True)
                pe.matmul(bank[2 + n % 2][:, 0:CTX], q, kcT[at, h // 2, :], start=True, stop=True).then_inc(s_done, 1)

            def transposes(n):
                pe.wait_ge(p_done, n + 1)
                if n >= 1:
                    pe.wait_ge(pTa_out, n)
                    pe.wait_ge(pTb_out, n)
                for k in range(KEYS // P):
                    dst = bank[4][:, k * P:(k + 1) * P] if k < 4 else bank[5][:, (k - 4) * P:(k - 3) * P]
                    mm = pe.transpose(dst, prob[n % 2][:, k * P:(k + 1) * P], ident[:, :])
                mm.then_inc(pT_done, 1)

            def weighted(n):
                h, t = n // TT, n % TT
                pe.wait_ge(pTa_out, n + 1)
                pe.wait_ge(pTb_out, n + 1)
                if t == 0 and h >= 2:
                    pe.wait_ge(att_done, h - 1)
                at = slice(h * HD, (h + 1) * HD)
                for k in range(KEYS // P):
                    v = vrow[:, k, at] if k < TT else vcrow[:, k - TT, at]
                    mm = pe.matmul(bank[6 + h % 2][:, t * HD:(t + 1) * HD], probT[n % 2][:, k, :], v,
                                   start=(k == 0), stop=(k == KEYS // P - 1))
                mm.then_inc(o_done, 1)

            pe.wait_ge(proj_out, 18)
            pe.wait_ge(cnorm_done, 1)
            for n in range(H * TT + 2):
                if n < H * TT:
                    scores(n)
                if 1 <= n <= H * TT:
                    transposes(n - 1)
                if n >= 2:
                    weighted(n - 2)
            pe.wait_ge(att_done, H)
            pe.wait_ge(p_done, H * TT)
            for k in range(AC):
                for t in range(TT):
                    mm = pe.transpose(bank[k][:, t * P:(t + 1) * P], att[:, t, k * P:(k + 1) * P], ident[:, :])
                mm.then_inc(attT_pe, 1)
            pe.wait_ge(attT_done, AC)
            for q in range(3):
                modulation(N_ADA, q, slice(2, 3))
            pe.wait_ge(convy_done, CC)
            pe.wait_ge(mod_rows, 24)
            for c in range(DC):
                if c == 0:
                    for i in range(4):
                        slab_ready(pe, N_GA + i)
                if c == 4:
                    slab_ready(pe, N_GA + 4)
                    slab_ready(pe, N_GA + 5)
                if c >= 2:
                    pe.wait_ge(mix_done, c - 1)
                b = 4 * (c % 2)
                n = N_GA if c < 4 else N_GA + 4
                at = slice((c % 4) * P, (c % 4) * P + P)
                project(bank[b][:, :], slab(n), at, hT)
                project(bank[b + 1][:, :], slab(n + 1), at, hT)
                project(bank[b + 2][:, :], slab(N_GA + 2), slice(c * P, (c + 1) * P), attT, AC)
                project(bank[b + 3][:, :], slab(N_GA + 3), slice(c * P, (c + 1) * P), conv, CC).then_inc(merge_pe, 1)
            pe.wait_ge(mix_done, DC)
            slab_ready(pe, N_WO)
            slab_ready(pe, N_WO + 1)
            for g in range(2 * TT):
                rows_of(bank[g][:, :], mixT, g // 2, slab(N_WO + g % 2), slice(0, 512)).then_inc(wo_pe, 1)
            def second_T(t, block, h2):
                pe.wait_ge(h2_done, block * TT + t + 1)
                for c in range(DC):
                    mm = pe.transpose(bank[2 * t + c // 4][:, (c % 4) * P:(c % 4) * P + P], h2[:, t, c:D:DC], ident[:, :])
                mm.then_inc(h2T_pe, 1)

            for t in range(TT):
                second_T(t, 0, h2r)
                if t == 0:
                    pe.wait_ge(wr_in, 16 * 10)
                pe.wait_ge(h2T_done, 2 * t + 2)
                rows_of(bank[2 * t][:, 0:NG + NE], h2T, t, wr, slice(0, NG + NE)).then_inc(logit_pe, 1)
            pe.wait_ge(both_done, 1)
            for t in range(TT + 1):
                dst = bank[1][:, t * NE:(t + 1) * NE]
                for k in range(min(t, TT - 1) + 1):
                    mm = pe.matmul(dst, before[:, :] if k == t else ones[:, :], both[:, k, :], start=(k == 0),
                                   stop=(k == min(t, TT - 1)))
            mm.then_inc(rank_pe, 1)

            def block_T(b):
                for c in range(DC):
                    mm = pe.transpose(bank[b][:, c * CAP:(c + 1) * CAP], xblk[b][:, c:D:DC], ident[0:CAP, 0:CAP])
                return mm

            def block_gu(b, n):
                gu = ring[:, n % RING:n % RING + 2, :].rearrange("p g (c f) -> p g c f", c=DC)
                for c in range(DC):
                    for half in range(2):
                        at = slice(CAP * half, CAP * half + CAP)
                        mm = pe.matmul(bank[2 + b][at, :].rearrange("p (g f) -> p g f", g=2), xbT[b][:, c, :],
                                       gu[:, :, c, 256 * half:256 * half + 256], start=(c == 0), stop=(c == DC - 1))
                return mm

            def hidden_T(b):
                for k in range(2):
                    mm = pe.transpose(bank[4 + b][:, k * P:(k + 1) * P], hid[b][:, k:256:2], ident[:, :])
                return mm

            def block_dn(b, n):
                for i in range(4):
                    half, k = i // 2, i % 2
                    for j in range(2):
                        mm = pe.matmul(bank[6 + b][CAP * j:CAP * j + CAP, :], hidT[b][:, k, CAP * half:CAP * half + CAP],
                                       slab(n)[:, half, k, 512 * j:512 * j + 512], start=(i == 0), stop=(i == 3))
                return mm

            def expert(e, b, i):
                n = N_EXP + 3 * b

                def arrived(k):
                    pe.wait_ge(slab_in[(n + k) % RING], i * 16 + 16 * ((n + k) // RING + 1))

                pe.wait_ge(xb_in[b], i * 16 + 16)
                pe.sem_inc(mark, 1)
                block_T(b).then_inc(xbT_done, 1)
                pe.wait_ge(xbT_out, e + 1)
                arrived(0)
                arrived(1)
                block_gu(b, n).then_inc(gu_done, 1)
                pe.wait_ge(hid_done, e + 1)
                hidden_T(b).then_inc(hidT_pe, 1)
                pe.wait_ge(hidT_done, e + 1)
                arrived(2)
                unless_first(pe, yv_done, e - 1)
                block_dn(b, n + 2).then_inc(dn_done, 1)

            pe.wait_ge(route_done, 1)
            for b in range(2):
                expert(b, b, 0)
            with pe.Fori(1, NE // 2) as i:
                for b in range(2):
                    expert(i * 2 + b, b, i)
            n_over = pe.value_load(over_i[0:1, 0:1], min_val=0, max_val=OVER)
            with pe.Fori(0, OVER) as i:
                with pe.If(i < n_over):
                    pe.wait_ge(ov_xin, i * 16 + 16)
                    pe.sem_inc(mark, 1)
                    block_T(0).then_inc(xbT_done, 1)
                    pe.wait_ge(xbT_out, i + (NE + 1))
                    pe.wait_ge(ov_slab, i * 48 + 48)
                    block_gu(0, N_EXP).then_inc(gu_done, 1)
                    pe.wait_ge(hid_done, i + (NE + 1))
                    hidden_T(0).then_inc(hidT_pe, 1)
                    pe.wait_ge(hidT_done, i + (NE + 1))
                    block_dn(0, N_EXP + 2).then_inc(dn_done, 1)
            pe.wait_ge(xnb_done, TT)
            for c in range(DC):
                for t in range(TT):
                    mm = pe.transpose(bank[c][:, t * P:(t + 1) * P], xnb[:, t, c:D:DC], ident[:, :])
                mm.then_inc(xT_done, 1)
            pe.wait_ge(wr_in, 16 * 10)
            pe.wait_ge(hT_done, 3 * DC)
            for t in range(TT):
                mm = rows_of(bank[0][:, t * H:(t + 1) * H], hT, t, wf, slice(0, H))
            mm.then_inc(f_pe, 1)
            for m in range(24):
                if m == 0:
                    pe.wait_ge(f_dve, 1)
                if m >= 8:
                    pe.wait_ge(proj_out, 18 + m - 7)
                k = (S_STICK, S_FOX)[m // 12] + m // 4 % 3
                if m % 4 == 0:
                    slab2_ready(pe, k)
                if m // 4 % 3 < 2:
                    mm = project(bank[m % 8][:, :], slab2(k), slice((m % 4) * P, (m % 4 + 1) * P), hT)
                else:
                    mm = rows_of(bank[m % 8][:, :], hT, m % 4, slab2(k), slice(0, 512))
                mm.then_inc(proj_done, 1)
            pe.wait_ge(proj_out, 18 + 24)
            pe.wait_ge(f_dve, 2)
            for t in range(TT):
                for k in range(t):
                    pe.matmul(bank[0][:, t * H:(t + 1) * H], ones[:, :], flog[:, k, :], start=(k == 0), stop=False)
                pe.matmul(bank[0][:, t * H:(t + 1) * H], before[:, :], flog[:, t, :], start=(t == 0), stop=False)
                mm = pe.matmul(bank[0][:, t * H:(t + 1) * H], ident[:, :], flog[:, t, :], start=False, stop=True)
            mm.then_inc(f_pe, 1)
            pe.wait_ge(f_dve, 3)
            for t in range(TT):
                mm = pe.transpose(bank[1][0:H, t * P:(t + 1) * P], fcum[:, t, :], ident[:, :])
            mm.then_inc(f_pe, 1)
            pe.wait_ge(f_act, 2)

            def fox_scores(n):
                h, t = n // TT, n % TT
                w = (t + 1) * P
                if n >= 2:
                    pe.wait_ge(p_done, H * TT + n - 1)
                at = slice(HD * (h % 2), HD * (h % 2) + HD)
                dst = bank[3 + n % 2]
                pe.matmul(dst[:, 0:w], fqT[at, h // 2, t * P:(t + 1) * P], fkT[at, h // 2, 0:w], start=True, stop=False)
                pe.matmul(dst[:, 0:w], ident[0:H, h:h + 1].broadcast_to([H, P]), fcumT[:, 0:w], start=False, stop=False)
                pe.matmul(dst[:, t * P:w], ident[:, :], causal[:, :], start=False, stop=True).then_inc(s_done, 1)

            def fox_transposes(n):
                pe.wait_ge(p_done, H * TT + n + 1)
                if n >= 1:
                    pe.wait_ge(pTa_out, H * TT + n)
                for k in range(n % TT + 1):
                    mm = pe.transpose(bank[5][:, k * P:(k + 1) * P], fprob[n % 2][:, k * P:(k + 1) * P], ident[:, :])
                mm.then_inc(pT_done, 1)

            def fox_weighted(n):
                h, t = n // TT, n % TT
                pe.wait_ge(pTa_out, H * TT + n + 1)
                if t == 0 and h >= 1:
                    pe.wait_ge(att_done, H + h)
                for k in range(t + 1):
                    mm = pe.matmul(bank[7][:, t * HD:(t + 1) * HD], fprobT[n % 2][:, k * P:(k + 1) * P],
                                   fvr[:, k, h * HD:(h + 1) * HD], start=(k == 0), stop=(k == t))
                mm.then_inc(o_done, 1)

            def fox_step(n):
                if n < H * TT:
                    fox_scores(n)
                if 1 <= n <= H * TT:
                    fox_transposes(n - 1)
                if n >= 2:
                    fox_weighted(n - 2)

            def stick_scores(h):
                if h >= 1:
                    pe.wait_ge(sbc_done, h)
                at = slice(HD * (h % 2), HD * (h % 2) + HD)
                for j in range(TT):
                    b, o = stick_cols(j, j)
                    mm = pe.matmul(bank[b][:, o:o + T - j * P], skT_[at, h // 2, j * P:(j + 1) * P], sqT[at, h // 2, j * P:T],
                                   start=True, stop=True)
                mm.then_inc(sbz_pe, 1)

            def stick_sums(h):
                x = stick_a[h % 2]
                pe.wait_ge(mask_done, 2 * h + 1)
                pe.wait_ge(sbb_done, h + 1)
                for j in range(TT):
                    b, o = stick_cols(j, j)
                    w = T - j * P
                    mm = pe.matmul(bank[b][:, o:o + w], later_neg[:, :], x[:, b, o:o + w], start=True, stop=(j == TT - 1))
                    for k in range(j + 1, TT):
                        b2, o2 = stick_cols(k, k)
                        mm = pe.matmul(bank[b][:, o + (k - j) * P:o + w], ones_neg[:, :], x[:, b2, o2:o2 + T - k * P],
                                       start=False, stop=(k == TT - 1))
                mm.then_inc(sbr_pe, 1)

            def stick_out(h):
                y = stick_b[h % 2]
                pe.wait_ge(mask_done, 2 * h + 2)
                if h >= 1:
                    pe.wait_ge(sbo_done, h)
                for t in range(TT):
                    for j in range(t + 1):
                        b, o = stick_cols(j, t)
                        mm = pe.matmul(bank[6][:, t * HD:(t + 1) * HD], y[:, b, o:o + P], svr[:, j, h * HD:(h + 1) * HD],
                                       start=(j == 0), stop=(j == t))
                mm.then_inc(sbo_pe, 1)

            for h in range(H):
                stick_scores(h)
                if h >= 1:
                    stick_out(h - 1)
                for t in range(TT):
                    if t == 3:
                        stick_sums(h)
                    fox_step(h * TT + t)
            stick_out(H - 1)
            fox_step(H * TT)
            fox_step(H * TT + 1)
            pe.wait_ge(mixed_done, TT)
            for k in range(DC):
                for t in range(TT):
                    mm = pe.transpose(bank[k][:, t * P:(t + 1) * P], mixed[:, t, k * P:(k + 1) * P], ident[:, :])
                mm.then_inc(attT_pe, 1)
            pe.wait_ge(attT_done, AC + DC)
            slab2_ready(pe, S_WO)
            slab2_ready(pe, S_WO + 1)
            for g in range(2 * TT):
                rows_of(bank[g][:, :], mixT2, g // 2, slab2(S_WO + g % 2), slice(0, 512)).then_inc(wo_pe, 1)
            for t in range(TT):
                second_T(t, 1, h2r_2)
            pe.wait_ge(h2T_done, 4 * TT)
            for t in range(TT):
                for q in range(4):
                    m = 4 * t + q
                    if t == 0:
                        slab2_ready(pe, S_WQ + q)
                    if m >= 8:
                        pe.wait_ge(q_done, m - 7)
                    for k in range(4):
                        mm = project(bank[m % 8][:, k * P:(k + 1) * P], slab2(S_WQ + q), slice(k * P, (k + 1) * P), h2T[:, :, t * P:(t + 1) * P])
                    mm.then_inc(q_pe, 1)
            pe.wait_ge(q_done, 4 * TT)
            pe.wait_ge(sk_dma, 16)
            for m in range(4):
                for k in range(4):
                    mm = pe.transpose(bank[m][:, k * P:(k + 1) * P], sk_in[:, 4 * m + k, :], ident[:, :])
                mm.then_inc(skT_pe, 1)

            def peer_scores(n, head):
                pe.wait_ge(qh_done, at_head(n, 1, 1))
                if n[1] > 0:
                    pe.wait_ge(ids_done, at_head(n, 1, 0))
                pe.sem_inc(mark, 1)
                for p in range(2):
                    keys = skT[:, head, p * P:(p + 1) * P] if isinstance(head, int) else \
                        skT[:, bass.ds(head, 1), p * P:(p + 1) * P].rearrange("p a b -> p (a b)")
                    mm = pe.matmul(bank[0][:, p * P:(p + 1) * P], qh[:, p, :], keys, start=True, stop=True)
                mm.then_inc(sc_pe, 1)

            def peer_head(n, t, nxt):
                if nxt is not None:
                    peer_scores((n[0], n[1] + 1), nxt)
                for g in range(UP_SETS):
                    pe.wait_ge(diag_done, at_head(n, UP_SETS, g + 1))
                    pe.wait_ge(up_in[g], at_head(n, 16 * G4, 16 * G4))
                    for r in range(G4 * g, G4 * g + G4):
                        for j in range(2):
                            mm = pe.matmul(bank[4 + 2 * (t % 2) + j][:, :], diag[:, r, :], up[r][:, 512 * j:512 * j + 512], start=False, stop=False)
                    mm.then_inc(up_free, 1)

            def edge(t, first):
                for j in range(2):
                    mm = pe.matmul(bank[4 + 2 * (t % 2) + j][:, :], zeros[:, :], zeros[:, :].unsqueeze(1).broadcast_to([P, 4, P]),
                                   start=first, stop=not first)
                return mm

            pe.wait_ge(skT_done, 5)
            peer_scores((None, 0), 0)
            for t in range(TT):
                last = t == TT - 1
                if t >= 2:
                    pe.wait_ge(fin_add, t - 1)
                edge(t, True)
                with pe.Fori(0, H // 2 - last) as i:
                    for b in range(2):
                        peer_head((i, t * H + b), t, i * 2 + (b + 1))
                if last:
                    peer_head((None, TT * H - 2), t, H - 1)
                    peer_head((None, TT * H - 1), t, None)
                edge(t, False).then_inc(peer_done, 1)


_INS = ["x", "c", "ctx", "c_ctx", "w_mod", "b_mod", "norm_mix", "w_in", "rpb", "w_att_out", "conv_w", "conv_b",
        "conv_ln_g", "conv_ln_b", "w_conv_out", "w_o", "norm_ffn", "w_router_group", "b_router_group",
        "w_router_expert", "b_router_expert", "w_exp_gate", "w_exp_up", "w_exp_down", "final_norm", "c_2", "w_ada_2",
        "b_ada_2", "g_norm_mix_2", "w_in_2", "b_forget_2", "g_out_fox_2", "g_out_sb_2", "w_out_2", "g_norm_ffn_2",
        "w_query_2", "sub_keys_2", "expert_down_2", "expert_up_2", "g_final_2"]
_FLAT = {"c_ctx", "final_norm", "g_final_2"}


def kernel(**inputs):
    import concourse.bacc as _bacc
    from concourse.bass_utils import run_bass_kernel_spmd as _run

    nc = _bacc.Bacc("TRN2", target_bir_lowering=False, num_devices=1)
    arrays, A = {}, {}
    for name in _INS:
        a = np.ascontiguousarray(inputs[name])
        arrays[f"in_{name}"] = a
        ap = nc.dram_tensor(f"in_{name}", a.shape, F32, kind="ExternalInput").ap()
        A[name] = ap if name in _FLAT else ap[0]
    out = nc.dram_tensor("out_0", (T, D), F32, kind="ExternalOutput").ap()
    build(nc, A, out)
    r = _run(nc, [arrays], core_ids=[0])
    return r.results[0]["out_0"].reshape(1, T, D)
```

```python
from contextlib import ExitStack

import numpy as np
import concourse.bass as bass
from concourse import mybir

F32 = mybir.dt.float32
I32 = mybir.dt.int32
U32 = mybir.dt.uint32
ALU = mybir.AluOpType
ACT = mybir.ActivationFunctionType
AX = mybir.AxisListType.X

P = 128
T = 512
TT = T // P
D = 1024
DC = D // P
CTX = 256
CT = CTX // P
H = 8
HD = 64
DA = H * HD
AC = DA // P
GRID_W, WIN = 64, 16
ROWS = T // GRID_W
RPB_R, RPB_C = 2 * ROWS - 1, 2 * WIN - 1
SKEW = 128
CONV_W = 31
PADC = CONV_W // 2
CC = 512 // P
UW = T + 2 * PADC
NG, NE, EPG = 4, 32, 8
F = 512
CAP = 64
OVER = (2 * T) // (CAP + 1)
SLOTS = (NE + OVER) * CAP
EPS = 1e-6
NEG = -1e30
RING = 6
SLAB = 4096
KEYS = T + CTX
K16 = 16
G4 = 4
DOWN_SETS = 2
UP_SETS = K16 // G4


class Link:

    def __init__(self, eng, own):
        self.eng, self.own, self.count = eng, own, {}

    def __call__(self, ins, sem=None):
        sem = self.own if sem is None else sem
        n = self.count.get(id(sem), 0) + 1
        self.count[id(sem)] = n
        ins.then_inc(sem, 1)
        self.eng.wait_ge(sem, n)
        return n


def build(nc, A, out):
    with ExitStack() as ctx:
        def sb(name, shape, dt=F32):
            return ctx.enter_context(nc.sbuf_tensor(name, shape, dt))

        def sem(name):
            return ctx.enter_context(nc.semaphore(name))

        def dram(name, shape, dt=F32):
            return nc.dram_tensor(name, shape, dt, kind="Internal")

        bank = [ctx.enter_context(nc.psum_tensor(f"bank{i}", [P, 512], F32)) for i in range(8)]
        ring = sb("ring", [P, RING, SLAB])
        arena_x = sb("arena_x", [P, 4224])
        arena_h = sb("arena_h", [P, 4096])
        arena_q = sb("arena_q", [P, 4096])
        arena_v = sb("arena_v", [P, 8192])
        arena_w = sb("arena_w", [P, 4864])

        def view(arena, at, *shape):
            n = int(np.prod(shape))
            ap = arena[:, at:at + n]
            if len(shape) == 1:
                return ap
            names = "abcd"[:len(shape)]
            return ap.rearrange(f"p ({' '.join(names)}) -> p {' '.join(names)}",
                                **{k: v for k, v in zip(names[1:], shape[1:])})

        def slot(s, *shape):
            ap = ring[:, s, :]
            names = "abcd"[:len(shape)]
            return ap.rearrange(f"p ({' '.join(names)}) -> p {' '.join(names)}",
                                **{k: v for k, v in zip(names[1:], shape[1:])})

        ident = sb("ident", [P, P])
        before = sb("before", [P, P])
        ones = sb("ones", [P, P])
        later_neg = sb("later_neg", [P, P])
        ones_neg = sb("ones_neg", [P, P])
        causal = sb("causal", [P, P])
        mean_w = sb("mean_w", [P, P])
        iota_i = sb("iota_i", [P, 64], I32)
        iota = sb("iota", [P, 64])
        part_i = sb("part_i", [P, 1], I32)
        band = sb("band", [P, 64])
        band_t = sb("band_t", [P, 2, 64])
        wstart = sb("wstart", [P, 4])

        cvec = sb("cvec", [P, 3, DC])
        mcol = sb("mcol", [P, 2, DC])
        mcol_c = sb("mcol_c", [P, 2, DC])
        mcol_2 = sb("mcol_2", [P, 2, DC])
        gcol = sb("gcol", [P, 2, DC])
        acol = sb("acol", [P, 3, DC])
        convc = sb("convc", [P, CC, 34])
        ssq = sb("ssq", [P, 8])
        rms = sb("rms", [P, 8])
        rms_t = sb("rms_t", [P, 8])
        smx = sb("smx", [P, 3, 4])
        ssum = sb("ssum", [P, 2, 32])
        rinv = sb("rinv", [P, 8])

        xr = view(arena_x, 0, TT, D)
        u_pad = view(arena_x, 0, CC, UW)
        conv = view(arena_x, CC * UW, CC, T)
        hT = view(arena_h, 0, DC, T)
        modr = view(arena_q, 0, T)
        modb = view(arena_q, 3 * T, T)
        mod_row = view(arena_v, 4096, T)
        mod_bias = [view(arena_v, 4608 + T * i, T) for i in range(3)]
        junk = view(arena_q, 6 * T, D)
        kT = view(arena_q, 0, AC, T)
        qT = view(arena_q, AC * T, AC, T)
        mixT = view(arena_q, 0, DC, T)
        vrow = view(arena_v, 0, TT, DA)
        kcT = view(arena_v, 2048, AC, CTX)
        vcrow = view(arena_v, 3072, CT, DA)
        hcT = view(arena_v, 4096, DC, CTX)
        cr = view(arena_v, 6144, CT, D)
        attT = view(arena_v, 6144, AC, T)
        bias = [view(arena_w, 896 * i, 14, 64) for i in range(2)]
        prob = [view(arena_w, 1792 + KEYS * i, KEYS) for i in range(2)] + [sb("prob_2", [P, KEYS])[:, :]]
        probT = [view(arena_w, 3328 + KEYS * i, KEYS // P, P) for i in range(2)]
        sig = [prob[i][:, 0:T] for i in range(2)]
        convw_in = view(arena_w, 4096, T)
        rpb_pad = view(arena_w, 4608, SKEW)
        conv_sq = view(arena_x, 0, CC, T)
        conv_s, conv_t, conv_r = (conv_sq[:, i, :] for i in range(3))
        gate_a = [view(arena_w, T * i, T) for i in range(2)]
        gate_c = [view(arena_w, 1024 + T * i, T) for i in range(2)]
        tmp = view(arena_w, 2048, D)
        tmp2 = view(arena_w, 3072, D)
        g1_b = view(arena_v, 0, D)
        a2_b = view(arena_v, D, D)
        sh2_b = view(arena_v, 2 * D, D)
        g2_b = view(arena_v, 3 * D, D)
        h2r = view(arena_v, 4096, TT, D)

        def route(at, *shape):
            return view(arena_w, at, *shape)
        junk2 = view(arena_w, 0, D)
        h2T = view(arena_h, 0, DC, T)
        lg = route(1024, TT, NG + NE)
        lgp = route(1168, TT, 8)
        gval, eval_ = route(1200, TT, 8), route(1232, TT, 8)
        gexp, oneh, pen = route(1264, TT, NG), route(1280, TT, NG), route(1296, TT, NG)
        gif, psum_, eif = route(1312, TT), route(1316, TT), route(1320, TT, 2)
        dval, dexp, dden = route(1328, TT), route(1332, TT), route(1336, TT)
        emask = route(1344, TT, NE)
        pick = route(1472, 2, TT, NE)
        both = route(1728, TT, NE)
        rank = route(1856, TT, NE)
        cnt, nblk, incl, incl2, delta, e64 = (route(1984 + 32 * i, NE) for i in range(6))
        over_at = route(2176, TT, NE)
        sel = route(2304, TT, NE)
        slot_f = route(2432, 2, TT)
        tab = route(2440, OVER, NE)
        tab_e = route(2920, OVER)
        ridx = sb("ridx", [P, 2, TT, 8], U32)
        slot_i = sb("slot_i", [P, 2, TT], I32)
        gw = sb("gw", [P, 2, TT])
        over_i = sb("over_i", [P, 16], I32)
        wr = sb("wr", [P, DC, NG + NE])
        br = sb("br", [P, NG + NE])
        zeros = sb("zeros", [P, P])
        xblk = [arena_h[0:CAP, D * i:D * i + D] for i in range(2)]
        xbT = [view(arena_h, 2048 + 512 * i, DC, CAP) for i in range(2)]
        yblk = [view(arena_h, 3072 + 512 * i, 512) for i in range(2)]
        silu_g = [view(arena_q, 256 * i, 256) for i in range(2)]
        hid = [view(arena_q, 512 + 256 * i, 256) for i in range(2)]
        hidT = [view(arena_q, 1024 + 256 * i, 2, P) for i in range(2)]
        ygat = [[view(arena_v, 4096 + 2048 * i + 1024 * s, D) for s in range(2)] for i in range(2)]
        fn_b = g1_b
        xnb = view(arena_q, 0, TT, D)

        wf = sb("wf", [P, DC, H])
        bf = sb("bf", [P, H])
        gob = sb("gob", [P, 2])
        sqT, skT_ = view(arena_v, 0, AC, T), view(arena_v, 2048, AC, T)
        svr, fvr = view(arena_v, 4096, TT, DA), view(arena_v, 6144, TT, DA)
        fqT, fkT = view(arena_q, 0, AC, T), view(arena_q, 2048, AC, T)
        mixed = [view(arena_h, 0, TT, DA), view(ring[:, 4, :], 0, TT, DA)]
        flog = route(4096, TT, H)
        fabs = route(4128, TT, H)
        fcumT = arena_w[0:H, 4160:4160 + T]
        fcum = route(4672, TT, H)
        stick_a = [ring[:, s, 0:1536].rearrange("p (a b) -> p a b", b=512) for s in (5, 0)]
        stick_b = [ring[:, s, 1536:3072].rearrange("p (a b) -> p a b", b=512) for s in (5, 0)]
        fprob = [ring[:, 4, 2048 + 512 * i:2560 + 512 * i] for i in range(3)]
        fprobT = [ring[:, s, 3072:3584] for s in (5, 0)]
        msq = view(ring[:, 5, :], 0, TT, DA)
        mss, mrt, msc = (view(ring[:, 5, :], 2048 + TT * H * i, TT, H) for i in range(3))
        mixT2 = view(arena_v, 0, DC, T)
        gt1_2, a2_2, sh2_2, nf_2 = (route(D * i, D) for i in range(4))
        tmp_2 = route(4096, 512)
        h2r_2 = view(arena_q, 0, TT, D)
        qT2 = view(arena_v, 0, TT * H, 2 * P)
        sk_in = view(ring[:, 2, :], 2048, 2 * H, P)
        skT = route(0, H + 1, 2 * P)
        gt2_2, gfin = view(arena_h, 2048, D), view(arena_h, 3072, D)
        tmp_p = route(4352, 512)

        def small(at, *shape):
            return route(2304 + at, *shape)
        diag = view(arena_h, 0, K16, P)
        qh = small(0, 2, P)
        work = small(256, 2, P)
        cand = small(512, K16 * K16)
        cand2 = small(768, K16 * K16)
        onehot = small(1024, K16, K16)
        hval = small(1280, 2, K16)
        hidx_f = small(1312, 2, K16)
        pos_f = small(1344, 2, K16)
        top = small(1376, K16)
        half_i = small(1392, 2, K16)
        id_f = small(1424, K16)
        gsub, gex = small(1440, K16), small(1456, K16)
        gate_p = [small(1472 + K16 * i, K16) for i in range(2)]
        dots, gel, coef = small(1504, K16), small(1520, K16), small(1536, K16)
        gsum = small(1552, 1)
        hidx = sb("hidx", [P, 2, K16], U32)
        pos = sb("pos", [P, K16], U32)
        pos_hl = sb("pos_hl", [P, 2, K16], U32)
        ids = [sb(f"ids{i}", [P, K16], I32) for i in range(2)]
        gbuf = [ring[:, (1, 2, 3, 4, 5, 0)[i // 4], D * (i % 4):D * (i % 4) + D] for i in range(4 * RING)]
        down, up = gbuf[0:8], gbuf[8:24]

        mod_d = dram("mod_d", [2, 6 * D])
        mod2_d = dram("mod2_d", [1, 6 * D])
        skew_d = dram("skew_d", [H * RPB_R, GRID_W, SKEW])
        xs_d = dram("xs_d", [SLOTS, D])
        ys_d = dram("ys_d", [SLOTS, D])

        slab_in = [sem(f"slab_in{s}") for s in range(RING)]
        vec_in = sem("vec_in")
        x_in = sem("x_in")
        modb_in = sem("modb_in")
        cw_in = sem("cw_in")
        modb2_in = sem("modb2_in")
        modb3_in = sem("modb3_in")
        rpb_in = sem("rpb_in")
        skew_out = sem("skew_out")
        bias_in = [sem("bias_in0"), sem("bias_in1")]
        mod_out = sem("mod_out")
        mod2_out = sem("mod2_out")
        convc_done = sem("convc_done")
        mcol2_in = sem("mcol2_in")
        mod_out_rest = sem("mod_out_rest")
        mcol_in = sem("mcol_in")
        xres_in = sem("xres_in")
        rows_in = sem("rows_in")
        xs_zero = sem("xs_zero")
        ys_zero = sem("ys_zero")
        out_dma = sem("out_dma")
        const_step = sem("const_step")
        consts = sem("consts")
        pe_mod = sem("pe_mod")
        mod_rows = sem("mod_rows")
        dve_step = sem("dve_step")
        act_step = sem("act_step")
        silu_c = sem("silu_c")
        ssq_done = sem("ssq_done")
        ms_done = sem("ms_done")
        root_done = sem("root_done")
        xn_done = sem("xn_done")
        acol_done = sem("acol_done")
        xT_done = sem("xT_done")
        hT_done = sem("hT_done")
        convw_T = sem("convw_T")
        glu_done = sem("glu_done")
        sig_done = sem("sig_done")
        u_done = sem("u_done")
        conv_done = sem("conv_done")
        proj_done = sem("proj_done")
        proj_out = sem("proj_out")
        cmean_done = sem("cmean_done")
        ccen_done = sem("ccen_done")
        csq_done = sem("csq_done")
        cvar_done = sem("cvar_done")
        cms_done = sem("cms_done")
        croot_done = sem("croot_done")
        cnorm_done = sem("cnorm_done")
        convy_done = sem("convy_done")
        s_done = sem("s_done")
        nmax_done = sem("nmax_done")
        p_done = sem("p_done")
        pT_done = sem("pT_done")
        pTa_out = sem("pTa_out")
        pTb_out = sem("pTb_out")
        o_done = sem("o_done")
        att_done = sem("att_done")
        pn_done = sem("pn_done")
        head_done = sem("head_done")
        attT_pe = sem("attT_pe")
        attT_done = sem("attT_done")
        merge_pe = sem("merge_pe")
        gates_done = sem("gates_done")
        mix_done = sem("mix_done")
        wo_pe = sem("wo_pe")
        res_done = sem("res_done")

        h2_done = sem("h2_done")
        h2T_pe = sem("h2T_pe")
        h2T_done = sem("h2T_done")
        logit_pe = sem("logit_pe")
        gsub_done = sem("gsub_done")
        gexp_done = sem("gexp_done")
        both_done = sem("both_done")
        rank_pe = sem("rank_pe")
        route_done = sem("route_done")
        wr_in = sem("wr_in")
        fn_in = sem("fn_in")
        scat = sem("scat")
        xbT_done = sem("xbT_done")
        xbT_out = sem("xbT_out")
        gu_done = sem("gu_done")
        silu_done = sem("silu_done")
        hid_done = sem("hid_done")
        hidT_pe = sem("hidT_pe")
        hidT_done = sem("hidT_done")
        dn_done = sem("dn_done")
        yv_done = sem("yv_done")
        over_done = sem("over_done")
        ov_xin = sem("ov_xin")
        ov_slab = sem("ov_slab")
        ov_ydma = sem("ov_ydma")
        comb_done = sem("comb_done")
        x2_done = sem("x2_done")
        xnb_done = sem("xnb_done")
        mark = sem("mark")
        xb_in = [sem("xb_in0"), sem("xb_in1")]
        y_dma = [sem("y_dma0"), sem("y_dma1")]
        acol2_done = sem("acol2_done")
        f_pe = sem("f_pe")
        f_dve = sem("f_dve")
        f_act = sem("f_act")
        sbz_pe = sem("sbz_pe")
        sbl_done = sem("sbl_done")
        sbb_done = sem("sbb_done")
        mask_done = sem("mask_done")
        sbr_pe = sem("sbr_pe")
        sbc_done = sem("sbc_done")
        sbe_done = sem("sbe_done")
        sbo_pe = sem("sbo_pe")
        sbo_done = sem("sbo_done")
        msq_done = sem("msq_done")
        mms_done = sem("mms_done")
        mroot_done = sem("mroot_done")
        mixed_done = sem("mixed_done")
        sk_dma = sem("sk_dma")
        skT_pe = sem("skT_pe")
        skT_done = sem("skT_done")
        q_pe = sem("q_pe")
        q_done = sem("q_done")
        qh_done = sem("qh_done")
        sc_pe = sem("sc_pe")
        topk_step = sem("topk_step")
        gsub2_done = sem("gsub2_done")
        gex_done = sem("gex_done")
        ids_done = sem("ids_done")
        down_free = sem("down_free")
        up_free = sem("up_free")
        gelu_done = sem("gelu_done")
        coef_done = sem("coef_done")
        diag_done = sem("diag_done")
        peer_done = sem("peer_done")
        fin_add = sem("fin_add")
        fin_done = sem("fin_done")
        rows2_in = sem("rows2_in")
        last_rows_in = sem("last_rows_in")
        down_in = [sem(f"down_in{i}") for i in range(DOWN_SETS)]
        up_in = [sem(f"up_in{i}") for i in range(UP_SETS)]
        yg_in = [sem(f"yg_in{t}") for t in range(TT)]

        def cols_pc(w, j):
            return w[:, j * 512:(j + 1) * 512].rearrange("(p c) n -> p c n", c=DC)

        def cols_cp(w, j):
            return w[:, j * 512:(j + 1) * 512].rearrange("(c p) n -> p c n", p=P)

        def rows_kp(w):
            return w.rearrange("(k p) n -> p k n", p=P)

        w_in = A["w_in"]
        QKV, GLU, GA, GB = 0, 3, 5, 7
        slabs = []
        slabs += [(cols_pc(A["w_mod"], j), (DC, 512), pe_mod, 1) for j in range(4)]
        slabs += [(cols_pc(w_in, GLU), (DC, 512), glu_done, CC), (cols_pc(w_in, GLU + 1), (DC, 512), glu_done, CC)]
        slabs += [(cols_pc(w_in, QKV + 1), (DC, 512), proj_done, 8), (cols_pc(w_in, QKV + 2), (DC, 512), proj_done, 14),
                  (cols_pc(w_in, QKV), (DC, 512), proj_done, 18)]
        slabs += [(cols_pc(A["w_mod"], 4 + j), (DC, 512), pe_mod, 2 + j // 4) for j in range(8)]
        slabs += [(cols_pc(A["w_ada_2"], j), (DC, 512), pe_mod, 4 + j // 4) for j in range(12)]
        slabs += [(cols_pc(w_in, GA), (DC, 512), merge_pe, 4), (cols_pc(w_in, GB), (DC, 512), merge_pe, 4),
                  (rows_kp(A["w_att_out"]), (AC, D), merge_pe, 8), (rows_kp(A["w_conv_out"]), (CC, D), merge_pe, 8),
                  (cols_pc(w_in, GA + 1), (DC, 512), merge_pe, 8), (cols_pc(w_in, GB + 1), (DC, 512), merge_pe, 8)]
        slabs += [(cols_cp(A["w_o"], j), (DC, 512), wo_pe, 8) for j in range(2)]
        N_MOD, N_GLU, N_K, N_V, N_Q, N_JOB, N_GA, N_WO = 0, 4, 6, 7, 8, 9, 29, 35

        def w_gu(w, e):
            return w[e, :, :].rearrange("(p c) n -> p c n", c=DC)

        def w_dn(w, e):
            return w[e, :, :].rearrange("(h p k) n -> p h k n", h=2, k=2)

        PROJ_JOB, AT_MEAN, AT_VAR, AT_JOB = 10, 1, 4, (6, 11, 16, 21)
        N_EXP = len(slabs)
        for e in range(2):
            slabs += [(w_gu(A["w_exp_gate"], e), (DC, F), gu_done, 2 * NE), (w_gu(A["w_exp_up"], e), (DC, F), gu_done, 2 * NE),
                      (w_dn(A["w_exp_down"], e), (2, 2, D), dn_done, 2 * NE)]

        SQ_2ND, SQ_FINAL, SQ_LAST = (CT + TT, CT + 4 * TT), CT + 2 * TT, CT + 5 * TT
        MS_2ND, MS_FINAL, MS_LAST = (1, 3 * TT + 1), TT + 1, 4 * TT + 1

        def final_at(t):
            return max(1, 2 * t)

        def first_at(t):
            return min(2 * t + 3, 2 * TT)

        N2 = N_EXP + 3 * NE
        FOX_W, STICK_W = 3 * DA, 3 * DA + H
        slabs2 = [cols_pc(A["w_in_2"], j) for j in range(3)]
        slabs2 += [A["w_in_2"][:, STICK_W + j * 512:STICK_W + (j + 1) * 512].rearrange("(p c) n -> p c n", c=DC) for j in range(3)]
        slabs2 += [cols_cp(A["w_out_2"], j) for j in range(2)]
        slabs2 += [cols_pc(A["w_query_2"], j) for j in range(4)]
        S_FOX, S_STICK, S_WO, S_WQ = 0, 3, 6, 8

        def slab2(k):
            return slot((N2 + k) % RING, DC, 512)

        def slab2_ready(eng, k):
            eng.wait_ge(slab_in[(N2 + k) % RING], 16 * ((N2 + k) // RING + 1))

        PIECES = (512, 512, 256)

        def stick_cols(j, q):
            return (0, 1, 2, 1)[j], (0, 0, 0, 384)[j] + (q - j) * P

        stick_fill = [([12 + 2 * h], [13 + 2 * h]) if h < 4 else ([16 + h], []) if h < H else ([], []) for h in range(H + 1)]
        STICK_NORM, STICK_COLS = 6, (12, 16, 20, 24)

        def at_head(n, per, extra):
            i, off = n
            return per * off + extra if i is None else i * (2 * per) + (per * off + extra)

        def unless_first(eng, s, value):
            if not isinstance(value, int) or value > 0:
                eng.wait_ge(s, value)

        def slab(n):
            return slot(n % RING, *slabs[n][1])

        def slab_ready(eng, n):
            eng.wait_ge(slab_in[n % RING], 16 * (n // RING + 1))

        block = ctx.enter_context(nc.Block())

        @block.sync
        def _(sp):
            for n, (src, shape, _, _) in enumerate(slabs):
                if n >= RING:
                    _, _, free, value = slabs[n - RING]
                    sp.wait_ge(free, value)
                if n == RING:
                    sp.wait_ge(mcol_in, 32)
                sp.dma_start(slab(n), src).then_inc(slab_in[n % RING], 16)
                if n == 3:
                    sp.dma_start(cr, A["ctx"].rearrange("(t p) d -> p t d", p=P)).then_inc(x_in, 16)
                    sp.dma_start(xr, A["x"].rearrange("(t p) d -> p t d", p=P)).then_inc(x_in, 16)
                if n == N_WO + 1:
                    sp.wait_ge(consts, 1)
                    sp.dma_start(xs_d[:, :].rearrange("(p r) (a b) -> p (r a) b", p=CAP, b=P),
                                 zeros[0:CAP, :].unsqueeze(1).broadcast_to([CAP, SLOTS // CAP * DC, P])).then_inc(xs_zero, 16)
                    sp.dma_start(ys_d[NE * CAP:SLOTS, :].rearrange("(p r) (a b) -> p (r a) b", p=CAP, b=P),
                                 zeros[0:CAP, :].unsqueeze(1).broadcast_to([CAP, OVER * DC, P])).then_inc(ys_zero, 16)

            def rows(e, b):
                unless_first(sp, xbT_done, e - 1)
                sp.dma_start(xblk[b], xs_d[bass.ds(e * CAP, CAP), :]).then_inc(xb_in[b], 16)

            sp.wait_ge(scat, 16 * 2 * TT)
            for b in range(2):
                rows(b, b)
            with sp.Fori(1, NE // 2) as i:
                for b in range(2):
                    e = i * 2 + b
                    n = N_EXP + 3 * b
                    rows(e, b)
                    for w, k in (("w_exp_gate", 0), ("w_exp_up", 1)):
                        if k == 0:
                            sp.wait_ge(gu_done, e - 1)
                        sp.dma_start(slab(n + k), A[w][bass.ds(e, 1), :, :].rearrange("o (p c) n -> p (o c) n", c=DC))\
                            .then_inc(slab_in[(n + k) % RING], 16)
                    sp.wait_ge(dn_done, e - 1)
                    sp.dma_start(slab(n + 2), A["w_exp_down"][bass.ds(e, 1), :, :].rearrange("o (h p k) n -> p (o h) k n", h=2, k=2))\
                        .then_inc(slab_in[(n + 2) % RING], 16)
            sp.wait_ge(route_done, 1)
            sp.wait_ge(ys_zero, 16)
            n_over = sp.value_load(over_i[0:1, 0:1], min_val=0, max_val=OVER)
            with sp.Fori(0, OVER) as i:
                with sp.If(i < n_over):
                    sp.wait_ge(dn_done, NE - 1)
                    e = sp.value_load(over_i[0:1, bass.ds(i + 1, 1)], min_val=0, max_val=NE - 1)
                    sp.dma_start(xblk[0], xs_d[bass.ds(i * CAP + NE * CAP, CAP), :]).then_inc(ov_xin, 16)
                    for w, k in (("w_exp_gate", 0), ("w_exp_up", 1)):
                        sp.dma_start(slab(N_EXP + k), A[w][bass.ds(e, 1), :, :].rearrange("o (p c) n -> p (o c) n", c=DC))\
                            .then_inc(ov_slab, 16)
                    sp.dma_start(slab(N_EXP + 2), A["w_exp_down"][bass.ds(e, 1), :, :].rearrange("o (h p k) n -> p (o h) k n", h=2, k=2))\
                        .then_inc(ov_slab, 16)
                    sp.wait_ge(yv_done, i + (NE + 1))
                    for half in range(2):
                        sp.dma_start(ys_d[bass.ds(i * CAP + NE * CAP, CAP), 512 * half:512 * half + 512],
                                     yblk[0][CAP * half:CAP * half + CAP, :]).then_inc(ov_ydma, 16)
                    sp.wait_ge(ov_ydma, i * 32 + 32)
                    sp.sem_inc(mark, 1)
            sp.sem_inc(over_done, 1)
            def load2(k):
                sp.dma_start(slab2(k), slabs2[k]).then_inc(slab_in[(N2 + k) % RING], 16)

            sp.wait_ge(dn_done, NE)
            sp.wait_ge(yg_in[TT - 1], 32)
            for k in range(S_STICK, S_STICK + 3):
                load2(k)
            for k in range(S_FOX, S_FOX + 3):
                load2(k)
            sp.wait_ge(proj_done, 18 + 24)
            for k in range(S_WO, S_WO + 3):
                load2(k)
            sp.wait_ge(att_done, H)
            sp.wait_ge(attT_done, DC)
            for k in range(S_WO + 3, S_WO + 6):
                load2(k)
            sp.wait_ge(wo_pe, 4 * TT)
            sp.dma_start(sk_in, A["sub_keys_2"].rearrange("h p k d -> k (h p) d")).then_inc(sk_dma, 16)
            sp.wait_ge(q_pe, 4 * TT)
            for dst, src in ((gt2_2, mod2_d[0, 5 * D:6 * D]), (gfin, A["g_final_2"])):
                sp.dma_start(dst, src.partition_broadcast(P)).then_inc(last_rows_in, 16)
            for t in range(TT):
                sp.wait_ge(fin_done, t + 1)
                sp.dma_start(out[t * P:(t + 1) * P, :], xr[:, t, :]).then_inc(out_dma, 16)
            sp.wait_ge(out_dma, 16 * TT)
            sp.wait_ge(skew_out, 16)
            sp.wait_ge(mod_out_rest, 16 * 8)
            sp.wait_ge(mod2_out, 16 * 12)

        @block.gpsimd
        def _(pool):
            link = Link(pool, const_step)
            for t, v in ((ident, 0.0), (before, 1.0), (ones, 1.0), (later_neg, -1.0), (ones_neg, -1.0),
                         (causal, 0.0), (mean_w, 1.0 / 512), (zeros, 0.0)):
                link(pool.memset(t[:, :], v))
            link(pool.memset(rpb_pad, 0.0))
            link(pool.affine_select(out=ident[:, :], in_=ident[:, :], compare_op=ALU.not_equal, fill=1.0, base=0,
                                    pattern=[[-1, P]], channel_multiplier=1))
            link(pool.affine_select(out=before[:, :], in_=before[:, :], compare_op=ALU.is_gt, fill=0.0, base=0,
                                    pattern=[[1, P]], channel_multiplier=-1))
            link(pool.affine_select(out=later_neg[:, :], in_=later_neg[:, :], compare_op=ALU.is_gt, fill=0.0, base=0,
                                    pattern=[[-1, P]], channel_multiplier=1))
            link(pool.affine_select(out=causal[:, :], in_=causal[:, :], compare_op=ALU.is_ge, fill=NEG, base=0,
                                    pattern=[[-1, P]], channel_multiplier=1))
            link(pool.iota(iota_i[:, :], pattern=[[1, 64]], base=0, channel_multiplier=0))
            link(pool.iota(part_i[:, :], pattern=[[0, 1]], base=0, channel_multiplier=1), consts)
            pool.dma_start(rpb_pad[0:H * RPB_R, GRID_W - WIN:GRID_W - WIN + RPB_C],
                           A["rpb"].rearrange("h r c -> (h r) c")).then_inc(rpb_in, 16)
            pool.wait_ge(rpb_in, 16)
            pool.dma_start(skew_d[:, :, :], rpb_pad[0:H * RPB_R, :].unsqueeze(1).broadcast_to([H * RPB_R, GRID_W, SKEW]))\
                .then_inc(skew_out, 16)
            for j in range(4):
                pool.wait_ge(mod_rows, j + 1)
                pool.dma_start(mod_d[:, j * 512:(j + 1) * 512], modr[32 * j:32 * j + 2, :]).then_inc(mod_out, 16)
            pool.wait_ge(mod_out, 16 * 4)
            for r, dst in ((0, mcol), (1, mcol_c)):
                pool.dma_start(dst[:, :, :], mod_d[r, 0:2 * D].rearrange("(k p c) -> p k c", k=2, c=DC)).then_inc(mcol_in, 16)

            def store_rows(i):
                for j in range(4):
                    pool.wait_ge(mod_rows, 4 + 4 * i + j + 1)
                    at = (4 * (i + 1) + j if i < 2 else 4 * (i - 2) + j) * 512
                    dst, done = (mod_d, mod_out_rest) if i < 2 else (mod2_d, mod2_out)
                    pool.dma_start(dst[0:1, at:at + 512], mod_row[32 * j:32 * j + 1, :]).then_inc(done, 16)
                if i == 1:
                    for g in (1, 2):
                        pool.dma_start(mod_bias[g - 1][0:P:32, :], A["b_ada_2"][g * 4 * T:(g + 1) * 4 * T].rearrange("(j n) -> j n", n=T))\
                            .then_inc(modb3_in, 16)

            pool.wait_ge(skew_out, 16)
            skew = skew_d[:, :, :]
            for h in range(H):
                if h == 2:
                    store_rows(0)
                if h >= 2:
                    pool.wait_ge(nmax_done, 4 * (h - 1))
                for half in range(2):
                    src = bass.AP(skew.tensor, skew.offset + (h * RPB_R + 1 - half) * GRID_W * SKEW + GRID_W - 1,
                                  [[SKEW - 1, GRID_W], [GRID_W * SKEW, 14], [1, GRID_W]])
                    pool.dma_start(bias[h % 2][64 * half:64 * half + 64, :, :], src).then_inc(bias_in[h % 2], 16)
                for i, n in enumerate(AT_JOB):
                    if (n + 1) // TT + 1 == h:
                        store_rows(1 + i)
            pool.wait_ge(mod_out_rest, 16 * 8)
            pool.wait_ge(o_done, 32)
            for dst, src in ((g1_b, mod_d[0, 2 * D:3 * D]), (sh2_b, mod_d[0, 3 * D:4 * D]), (a2_b, mod_d[0, 4 * D:5 * D]),
                             (g2_b, mod_d[0, 5 * D:6 * D])):
                pool.dma_start(dst, src.partition_broadcast(P)).then_inc(rows_in, 16)
            pool.wait_ge(merge_pe, DC)
            pool.dma_start(xr, A["x"].rearrange("(t p) d -> p t d", p=P)).then_inc(xres_in, 16)
            pool.dma_start(tmp2, A["norm_ffn"].partition_broadcast(P)).then_inc(rows_in, 16)
            pool.wait_ge(mod2_out, 16 * 12)
            pool.dma_start(mcol_2[:, :, :], mod2_d[0, 0:2 * D].rearrange("(k p c) -> p k c", k=2, c=DC)).then_inc(mcol2_in, 16)
            pool.wait_ge(h2_done, TT)
            pool.wait_ge(route_done, 1)
            pool.wait_ge(xs_zero, 16)
            for t in range(TT):
                for s in range(2):
                    pool.indirect_dma_start(xs_d[:, :], bass.IndirectOffsetOnAxis(ap=slot_i[:, s, t:t + 1], axis=0),
                                            h2r[:, t, :], None).then_inc(scat, 16)
            pool.wait_ge(res_done, 2 * TT)
            pool.dma_start(fn_b, A["final_norm"].partition_broadcast(P)).then_inc(fn_in, 16)
            for b in range(2):
                pool.wait_ge(y_dma[b], 32 * (NE // 2))
            pool.wait_ge(over_done, 1)
            pool.wait_ge(ys_zero, 16)
            pool.wait_ge(scat, 16 * 2 * TT)
            for t in range(TT):
                if t >= 2:
                    pool.wait_ge(comb_done, t - 1)
                for s in range(2):
                    pool.indirect_dma_start(ygat[t % 2][s], None, ys_d[:, :],
                                            bass.IndirectOffsetOnAxis(ap=slot_i[:, s, t:t + 1], axis=0)).then_inc(yg_in[t], 16)
            pool.wait_ge(ssq_done, SQ_FINAL + 2 * TT)
            pool.wait_ge(wo_pe, 2 * TT)
            for dst, src in ((gt1_2, mod2_d[0, 2 * D:3 * D]), (sh2_2, mod2_d[0, 3 * D:4 * D]), (a2_2, mod2_d[0, 4 * D:5 * D]),
                             (nf_2, A["g_norm_ffn_2"])):
                pool.dma_start(dst, src.partition_broadcast(P)).then_inc(rows2_in, 16)

            def mask(x, done):
                link(pool.tensor_tensor(x[:, :, 0:P], x[:, :, 0:P], before[:, :].unsqueeze(1).broadcast_to([P, 3, P]), ALU.mult))
                link(pool.tensor_tensor(x[:, 1, 384:512], x[:, 1, 384:512], before[:, :], ALU.mult), done)

            for h in range(H + 1):
                if h >= 1:
                    pool.wait_ge(sbe_done, h)
                    mask(stick_b[(h - 1) % 2], mask_done)
                if h < H:
                    pool.wait_ge(sbb_done, h + 1)
                    mask(stick_a[h % 2], mask_done)
            pool.wait_ge(wo_pe, 4 * TT)
            pool.wait_ge(skT_pe, 4)
            pool.sem_inc(down_free, DOWN_SETS)

            def gathers(n, b):
                def down_rows(g):
                    pool.wait_ge(down_free, at_head(n, UP_SETS, g + 1))
                    pool.sem_inc(mark, 1)
                    for k in range(G4):
                        r = G4 * g + k
                        pool.indirect_dma_start(down[r % (G4 * DOWN_SETS)], None, A["expert_down_2"],
                                                bass.IndirectOffsetOnAxis(ap=ids[b][:, r:r + 1], axis=0)).then_inc(down_in[g % DOWN_SETS], 16)

                def up_rows(g):
                    pool.wait_ge(up_free, at_head(n, UP_SETS, g + 1))
                    pool.sem_inc(mark, 1)
                    for k in range(G4):
                        r = G4 * g + k
                        pool.indirect_dma_start(up[r], None, A["expert_up_2"],
                                                bass.IndirectOffsetOnAxis(ap=ids[b][:, r:r + 1], axis=0)).then_inc(up_in[g], 16)

                pool.wait_ge(ids_done, at_head(n, 1, 1))
                pool.sem_inc(mark, 1)
                down_rows(0)
                for g in range(1, UP_SETS):
                    down_rows(g)
                    up_rows(g - 1)
                up_rows(UP_SETS - 1)

            for t in range(TT):
                with pool.Fori(0, H // 2) as i:
                    for b in range(2):
                        gathers((i, t * H + b), b)

        @block.scalar
        def _(act):
            link = Link(act, act_step)
            for i, n in enumerate(("c", "c_ctx", "c_2")):
                act.dma_start(cvec[:, i, :], A[n].rearrange("(p c) -> p c", c=DC)).then_inc(vec_in, 16)
            for i, n in enumerate(("norm_mix", "g_norm_mix_2")):
                act.dma_start(gcol[:, i, :], A[n].rearrange("(p c) -> p c", c=DC)).then_inc(vec_in, 16)
            for r in range(2):
                act.dma_start(modb[r:P:32, :], A["b_mod"][0:4 * T].rearrange("(j n) -> j n", n=T)).then_inc(modb_in, 16)
            act.dma_start(convw_in[0:CONV_W, :], A["conv_w"]).then_inc(cw_in, 16)
            for i, n in enumerate(("conv_b", "conv_ln_g", "conv_ln_b")):
                act.dma_start(convw_in[CONV_W + i:CONV_W + i + 1, :], A[n].rearrange("(a n) -> a n", a=1)).then_inc(cw_in, 16)
            act.dma_start(wr[:, :, 0:NG], A["w_router_group"].rearrange("(p c) e -> p c e", c=DC)).then_inc(wr_in, 16)
            act.dma_start(wr[:, :, NG:NG + NE], A["w_router_expert"].rearrange("(p c) e -> p c e", c=DC)).then_inc(wr_in, 16)
            act.dma_start(br[:, 0:NG], A["b_router_group"].partition_broadcast(P)).then_inc(wr_in, 16)
            act.dma_start(br[:, NG:NG + NE], A["b_router_expert"].partition_broadcast(P)).then_inc(wr_in, 16)
            act.dma_start(wf[:, :, :], A["w_in_2"][:, FOX_W:FOX_W + H].rearrange("(p c) e -> p c e", c=DC)).then_inc(wr_in, 16)
            act.dma_start(bf[:, :], A["b_forget_2"].partition_broadcast(P)).then_inc(wr_in, 16)
            for i, n in enumerate(("g_out_fox_2", "g_out_sb_2")):
                for half in range(2):
                    act.dma_start(gob[HD * half:HD * half + HD, i:i + 1], A[n].rearrange("(d a) -> d a", a=1)).then_inc(wr_in, 16)
            act.wait_ge(vec_in, 16 * 5)
            link(act.activation(cvec[:, :, :], cvec[:, :, :], ACT.Silu), silu_c)
            act.wait_ge(x_in, 32)
            for i in range(CT + TT):
                row = cr[:, i, :] if i < CT else xr[:, i - CT, :]
                link(act.activation(junk, row, ACT.Square, accum_out=ssq[:, i:i + 1]), ssq_done)
            act.wait_ge(ms_done, 1)
            link(act.activation(rms[:, 0:6], rms_t[:, 0:6], ACT.Sqrt), root_done)
            act.wait_ge(acol_done, 2)
            for g in range(2 * DC):
                act.wait_ge(xT_done, g + 1)
                c = g % DC
                if g < DC:
                    link(act.activation(hcT[:, c, :], bank[4 + g % 4][:, 0:CTX], ACT.Identity,
                                        scale=acol[:, 1, c:c + 1], bias=mcol_c[:, 0, c:c + 1]), hT_done)
                else:
                    link(act.activation(hT[:, c, :], bank[4 + g % 4][:, :], ACT.Identity,
                                        scale=acol[:, 0, c:c + 1], bias=mcol[:, 0, c:c + 1]), hT_done)
            for cc in range(CC):
                act.wait_ge(glu_done, cc + 1)
                if cc >= 2:
                    act.wait_ge(u_done, cc - 1)
                link(act.activation(sig[cc % 2], bank[2 * (cc % 2) + 1][:, :], ACT.Sigmoid), sig_done)
            act.wait_ge(mod_out, 16 * 4)
            for m in range(18):
                act.wait_ge(proj_done, m + 1)
                src = bank[4 + m % 4]
                if m < 4:
                    link(act.activation(kT[:, m, :], src[:, :], ACT.Copy), proj_out)
                elif m < 8:
                    link(act.activation(kcT[:, m - 4, :], src[:, 0:CTX], ACT.Copy), proj_out)
                elif m < 10:
                    link(act.activation(vcrow[:, m - 8, :], src[:, :], ACT.Copy), proj_out)
                elif m < 14:
                    link(act.activation(vrow[:, m - 10, :], src[:, :], ACT.Copy), proj_out)
                else:
                    link(act.activation(qT[:, m - 14, :], src[:, :], ACT.Copy, scale=HD ** -0.5), proj_out)
                if m == 9:
                    for i, b in enumerate((A["b_mod"][4 * T:8 * T], A["b_mod"][8 * T:12 * T], A["b_ada_2"][0:4 * T])):
                        act.dma_start(mod_bias[i][0:P:32, :], b.rearrange("(j n) -> j n", n=T)).then_inc(modb2_in, 16)

            def conv_squares():
                act.wait_ge(ccen_done, CC)
                for cc in range(CC):
                    link(act.activation(conv_sq[:, cc, :], conv[:, cc, :], ACT.Square), csq_done)

            def conv_root():
                act.wait_ge(cms_done, 1)
                link(act.activation(conv_r, conv_t, ACT.Sqrt), croot_done)

            def conv_silu():
                for cc in range(CC):
                    act.wait_ge(cnorm_done, cc + 1)
                    link(act.activation(conv[:, cc, :], conv[:, cc, :], ACT.Silu, scale=convc[:, cc, CONV_W + 1:CONV_W + 2],
                                        bias=convc[:, cc, CONV_W + 2:CONV_W + 3]), convy_done)

            def probs_out(n):
                act.wait_ge(pT_done, n + 1)
                if n >= 2:
                    act.wait_ge(o_done, n - 1)
                link(act.activation(probT[n % 2][:, 0:4, :], bank[4][:, :].rearrange("p (a b) -> p a b", b=P), ACT.Copy), pTa_out)

                link(act.activation(probT[n % 2][:, 4:6, :], bank[5][:, 0:2 * P].rearrange("p (a b) -> p a b", b=P), ACT.Copy), pTb_out)

            def head_out(h):
                act.wait_ge(o_done, TT * (h + 1))
                at = slice(HD * (h % 2), HD * (h % 2) + HD)
                link(act.activation(attT[at, h // 2, :], bank[6][at, :], ACT.Copy), head_done)

            for n in range(H * TT):
                act.wait_ge(nmax_done, n + 1)
                link(act.activation(prob[n % 3][:, 0:T], prob[n % 3][:, 0:T], ACT.Exp, bias=smx[:, n % 3, 2:3],
                                    accum_out=ssum[:, 0, n:n + 1]))
                link(act.activation(prob[n % 3][:, T:KEYS], bank[2 + n % 2][:, 0:CTX], ACT.Exp, bias=smx[:, n % 3, 2:3],
                                    accum_out=ssum[:, 1, n:n + 1]), p_done)
                if n >= 2:
                    probs_out(n - 2)
                if n >= 3 and (n - 3) % TT == TT - 1:
                    head_out((n - 3) // TT)
                if n == AT_MEAN + 1:
                    conv_squares()
                if n == AT_VAR + 1:
                    conv_root()
                if n == AT_VAR + 2:
                    conv_silu()
            probs_out(H * TT - 2)
            probs_out(H * TT - 1)
            head_out(H - 1)
            for c in range(DC):
                act.wait_ge(merge_pe, c + 1)
                if c >= 2:
                    act.wait_ge(mix_done, c - 1)
                link(act.activation(gate_a[c % 2], bank[4 * (c % 2)][:, :], ACT.Sigmoid))
                link(act.activation(gate_c[c % 2], bank[4 * (c % 2) + 1][:, :], ACT.Sigmoid), gates_done)
            def second_norm(t, block, junk):
                n = block * TT + t
                act.wait_ge(res_done, 2 * n + 2)
                link(act.activation(junk, xr[:, t, :], ACT.Square, accum_out=ssq[:, t:t + 1]), ssq_done)
                act.wait_ge(ms_done, MS_2ND[block] + t + 1)
                link(act.activation(rms[:, t:t + 1], rms_t[:, t:t + 1], ACT.Sqrt), root_done)
                act.wait_ge(h2T_pe, n + 1)
                for i in range(2):
                    link(act.activation(h2T[:, 4 * i:4 * i + 4, t * P:(t + 1) * P],
                                        bank[2 * t + i][:, :].rearrange("p (a b) -> p a b", b=P), ACT.Copy), h2T_done)

            for t in range(TT):
                second_norm(t, 0, junk2)
            act.wait_ge(gsub_done, 1)
            link(act.activation(gexp, gexp, ACT.Exp), gexp_done)
            act.wait_ge(gsub_done, 2)
            link(act.activation(dexp, dval, ACT.Exp), gexp_done)

            def expert(e, b, i):
                act.wait_ge(xbT_done, e + 1)
                unless_first(act, gu_done, e - 1)
                act.activation(xbT[b], bank[b][:, :].rearrange("p (a c) -> p a c", c=CAP), ACT.Copy).then_inc(xbT_out, 1)
                act.wait_ge(gu_done, e + 1)
                unless_first(act, hid_done, e - 1)
                act.activation(silu_g[b], bank[2 + b][:, 0:256], ACT.Silu).then_inc(silu_done, 1)
                act.wait_ge(dn_done, e + 1)
                unless_first(act, y_dma[b], i * 32)
                act.activation(yblk[b], bank[6 + b][:, :], ACT.Copy).then_inc(yv_done, 1)
                act.wait_ge(yv_done, e + 1)
                for half in range(2):
                    act.dma_start(ys_d[bass.ds(e * CAP, CAP), 512 * half:512 * half + 512],
                                  yblk[b][CAP * half:CAP * half + CAP, :]).then_inc(y_dma[b], 16)

            for b in range(2):
                expert(b, b, 0)
            with act.Fori(1, NE // 2) as i:
                for b in range(2):
                    expert(i * 2 + b, b, i)
            act.wait_ge(route_done, 1)
            n_over = act.value_load(over_i[0:1, 0:1], min_val=0, max_val=OVER)
            with act.Fori(0, OVER) as i:
                with act.If(i < n_over):
                    act.wait_ge(xbT_done, i + (NE + 1))
                    act.activation(xbT[0], bank[0][:, :].rearrange("p (a c) -> p a c", c=CAP), ACT.Copy).then_inc(xbT_out, 1)
                    act.wait_ge(gu_done, i + (NE + 1))
                    act.activation(silu_g[0], bank[2][:, 0:256], ACT.Silu).then_inc(silu_done, 1)
                    act.wait_ge(y_dma[0], 32 * (NE // 2))
                    act.wait_ge(dn_done, i + (NE + 1))
                    act.activation(yblk[0], bank[6][:, :], ACT.Copy).then_inc(yv_done, 1)
            def root(at, count):
                act.wait_ge(ms_done, MS_FINAL + count)
                link(act.activation(rms[:, at:at + 1], rms_t[:, at:at + 1], ACT.Sqrt), root_done)

            def columns(t):
                for half in range(2):
                    act.wait_ge(xT_done, 2 * DC + 2 * t + half + 1)
                    for k in range(4):
                        c = 4 * half + k
                        link(act.activation(hT[:, c, t * P:(t + 1) * P], bank[2 * t + half][:, k * P:(k + 1) * P], ACT.Identity,
                                            scale=acol[:, 2, c:c + 1], bias=mcol_2[:, 0, c:c + 1]), hT_done)

            for n in range(TT + 3):
                if n < TT:
                    act.wait_ge(comb_done, n + 1)
                    link(act.activation(junk2, xr[:, n, :], ACT.Square, accum_out=ssq[:, n:n + 1]), ssq_done)
                if 1 <= n <= TT:
                    root(n - 1, final_at(n - 1))
                    act.wait_ge(x2_done, n)
                    link(act.activation(junk2, xr[:, n - 1, :], ACT.Square, accum_out=ssq[:, TT + n - 1:TT + n]), ssq_done)
                if 2 <= n <= TT + 1:
                    root(TT + n - 2, first_at(n - 2))
                if n == 2:
                    act.wait_ge(acol2_done, 1)
                if n >= 3:
                    columns(n - 3)
            def soft(x, done):
                link(act.activation(x, x, ACT.Exp))
                link(act.activation(x, x, ACT.Ln, bias=ones[:, 0:1]), done)

            act.wait_ge(f_dve, 1)
            soft(fabs, f_act)
            def proj2_out(m):
                act.wait_ge(proj_done, 18 + m + 1)
                dst, scale = ((sqT, HD ** -0.5), (skT_, 1.0), (svr, 1.0), (fqT, HD ** -0.5), (fkT, 1.0), (fvr, 1.0))[m // 4]
                src = bank[m % 6] if m < 12 else bank[7]
                link(act.activation(dst[:, m % 4, :], src[:, :], ACT.Copy, scale=scale), proj_out)

            for m in range(12):
                proj2_out(m)
            act.wait_ge(f_pe, 3)
            link(act.activation(fcumT, bank[6][0:H, :], ACT.Copy, scale=-1.0), f_act)

            def stick_soft(h):
                x, z = stick_a[h % 2], bank[3 * (h % 2):3 * (h % 2) + 3]
                act.wait_ge(sbz_pe, h + 1)
                if h >= 2:
                    act.wait_ge(sbr_pe, h - 1)
                for i, w in enumerate(PIECES):
                    link(act.activation(x[:, i, 0:w], z[i][:, 0:w], ACT.Abs))
                for at in (x[:, 0:2, :], x[:, 2, 0:256]):
                    link(act.activation(at, at, ACT.Exp, scale=-1.0))
                    link(act.activation(at, at, ACT.Ln, bias=ones[:, 0:1]), sbl_done)

            def stick_exp(h):
                x = stick_b[h % 2]
                act.wait_ge(sbc_done, h + 1)
                link(act.activation(x[:, 0:2, :], x[:, 0:2, :], ACT.Exp))
                link(act.activation(x[:, 2, 0:256], x[:, 2, 0:256], ACT.Exp), sbe_done)

            def stick_out(h):
                act.wait_ge(sbo_pe, h + 1)
                link(act.activation(mixed[1][:, :, h * HD:(h + 1) * HD], bank[6][:, 0:256].rearrange("p (t d) -> p t d", d=HD),
                                    ACT.Copy), sbo_done)

            for h in range(H + 1):
                if h < H:
                    stick_soft(h)
                for m in stick_fill[h][0]:
                    proj2_out(m)
                if h >= 2:
                    stick_out(h - 2)
                if h >= 1:
                    stick_exp(h - 1)
                for m in stick_fill[h][1]:
                    proj2_out(m)

            def fox_exp(n):
                w = (n % TT + 1) * P
                act.wait_ge(nmax_done, H * TT + n + 1)
                if n >= 3:
                    act.wait_ge(pT_done, H * TT + n - 2)
                link(act.activation(fprob[n % 3][:, 0:w], bank[n % 3][:, 0:w], ACT.Exp, bias=smx[:, n % 3, 2:3],
                                    accum_out=ssum[:, 0, n:n + 1]), p_done)

            def fox_T(n):
                w = (n % TT + 1) * P
                act.wait_ge(pT_done, H * TT + n + 1)
                if n >= 2:
                    act.wait_ge(o_done, H * TT + n - 1)
                link(act.activation(fprobT[n % 2][:, 0:w], bank[3 + n % 2][:, 0:w], ACT.Copy), pTa_out)

            def out_norm(part, half):
                for t in range(TT):
                    link(act.activation(msq[:, t, :], mixed[half][:, t, :], ACT.Square), msq_done)
                act.wait_ge(mms_done, 2 * part + 2)
                link(act.activation(mrt, mss, ACT.Sqrt), mroot_done)

            def mix_columns(i, k, b):
                act.wait_ge(attT_pe, i + 1)
                link(act.activation(mixT2[:, k, :], bank[b][:, :], ACT.Copy, scale=gob[:, k // AC:k // AC + 1]), attT_done)

            act.wait_ge(wr_in, 16 * 10)
            for n in range(H * TT + 2):
                if n < H * TT:
                    fox_exp(n)
                if n >= 2:
                    fox_T(n - 2)
                if n == 1:
                    stick_out(H - 1)
                if n == STICK_NORM:
                    out_norm(0, 1)
                if n in STICK_COLS:
                    i = STICK_COLS.index(n)
                    mix_columns(i, AC + i, 6)
            act.wait_ge(att_done, H)
            out_norm(1, 0)
            for k in range(AC):
                mix_columns(AC + k, k, k)
            for t in range(TT):
                second_norm(t, 1, nf_2)
            def query_out(m):
                act.wait_ge(q_pe, m + 1)
                at = (m // 4) * H + 2 * (m % 4)
                link(act.activation(qT2[:, at:at + 2, :], bank[1 + m % 3][:, :].rearrange("p (a b) -> p a b", a=2), ACT.Copy), q_done)

            for m in range(4):
                query_out(m)
            for m in range(4):
                act.wait_ge(skT_pe, m + 1)
                link(act.activation(skT[:, 2 * m:2 * m + 2, :], bank[4 + m][:, :].rearrange("p (a b) -> p a b", a=2), ACT.Copy), skT_done)
            link(act.activation(skT[:, H, :], bank[4][:, 0:2 * P], ACT.Copy), skT_done)

            def queries(n):
                i, off = n
                if off > 0:
                    act.wait_ge(sc_pe, at_head(n, 1, 0))
                    act.sem_inc(mark, 1)
                src = qT2[:, off, :] if i is None else qT2[:, bass.ds(i * 2 + off, 1), :].rearrange("p a b -> p (a b)")
                act.activation(qh.rearrange("p a b -> p (a b)"), src, ACT.Copy).then_inc(qh_done, 1)

            def gate_exp(n):
                act.wait_ge(gsub2_done, at_head(n, 1, 1))
                act.activation(gex, gsub, ACT.Exp, accum_out=gsum).then_inc(gex_done, 1)

            def peer_head(n, more):
                nxt = (n[0], n[1] + 1)

                def gelu(g):
                    act.wait_ge(down_free, at_head(n, UP_SETS, DOWN_SETS + g + 1))
                    act.activation(gel[:, G4 * g:G4 * g + G4], dots[:, G4 * g:G4 * g + G4], ACT.Gelu).then_inc(gelu_done, 1)

                def diagonals(g):
                    act.wait_ge(up_free, at_head(n, UP_SETS, g + 1))
                    act.wait_ge(coef_done, at_head(n, UP_SETS, g + 1))
                    for r in range(G4 * g, G4 * g + G4):
                        d = act.activation(diag[:, r, :], ident[:, :], ACT.Copy, scale=coef[:, r:r + 1])
                    d.then_inc(diag_done, 1)

                if more:
                    queries(nxt)
                gelu(0)
                gelu(1)
                diagonals(0)
                if more:
                    gate_exp(nxt)
                gelu(2)
                diagonals(1)
                gelu(3)
                diagonals(2)
                diagonals(3)

            def last_norm(t):
                act.wait_ge(fin_add, t + 1)
                link(act.activation(h2r_2[:, t, :], xr[:, t, :], ACT.Square, accum_out=ssq[:, t:t + 1]), ssq_done)
                act.wait_ge(ms_done, MS_LAST + t + 1)
                link(act.activation(rms[:, t:t + 1], rms_t[:, t:t + 1], ACT.Sqrt), root_done)

            queries((None, 0))
            for m in range(4, 4 * TT):
                query_out(m)
                if m == 8:
                    gate_exp((None, 0))
            for t in range(TT):
                last = t == TT - 1
                with act.Fori(0, H // 2 - last) as i:
                    for b in range(2):
                        peer_head((i, t * H + b), True)
                if last:
                    peer_head((None, TT * H - 2), True)
                    peer_head((None, TT * H - 1), False)
                if t >= 1:
                    last_norm(t - 1)
            last_norm(TT - 1)

        @block.vector
        def _(dve):
            link = Link(dve, dve_step)

            def inv_root(n, root, last=None):
                dve.wait_ge(*root)
                r, v, s = n
                link(dve.reciprocal(r, r))
                link(dve.tensor_tensor(s, r, r, ALU.mult))
                link(dve.tensor_tensor(s, s, v, ALU.mult))
                link(dve.tensor_scalar(s, s, -0.5, 1.5, ALU.mult, ALU.add))
                link(dve.tensor_tensor(r, r, s, ALU.mult), last)

            dve.wait_ge(consts, 1)
            link(dve.tensor_copy(iota[:, :], iota_i[:, :]))
            link(dve.tensor_copy(wstart[:, 0:1], part_i[:, :]))
            link(dve.tensor_scalar(wstart[:, 1:2], wstart[:, 0:1], float(GRID_W), -float(GRID_W), ALU.is_ge, ALU.mult))
            link(dve.tensor_tensor(wstart[:, 0:1], wstart[:, 0:1], wstart[:, 1:2], ALU.add))
            link(dve.tensor_scalar(wstart[:, 2:3], wstart[:, 0:1], -float(WIN // 2), 0.0, ALU.add, ALU.max))
            link(dve.tensor_scalar(wstart[:, 2:3], wstart[:, 2:3], float(GRID_W - WIN), None, ALU.min))
            link(dve.tensor_scalar(wstart[:, 3:4], wstart[:, 2:3], float(WIN), None, ALU.add))
            link(dve.tensor_scalar(band_t[:, 0, :], iota[:, :], wstart[:, 2:3], None, ALU.is_ge))
            link(dve.tensor_scalar(band_t[:, 1, :], iota[:, :], wstart[:, 3:4], None, ALU.is_lt))
            link(dve.tensor_tensor(band[:, :], band_t[:, 0, :], band_t[:, 1, :], ALU.mult))
            link(dve.tensor_scalar(band[:, :], band[:, :], -NEG, NEG, ALU.mult, ALU.add))

            dve.wait_ge(ssq_done, CT + TT)
            link(dve.tensor_scalar(rms_t[:, 0:6], ssq[:, 0:6], 1.0 / D, EPS, ALU.mult, ALU.add), ms_done)
            inv_root((rms[:, 0:6], rms_t[:, 0:6], ssq[:, 0:6]), (root_done, 1))
            for i in range(CT + TT):
                row = cr[:, i, :] if i < CT else xr[:, i - CT, :]
                link(dve.tensor_scalar(row, row, rms[:, i:i + 1], None, ALU.mult), xn_done)

            dve.wait_ge(modb_in, 32)
            dve.wait_ge(pe_mod, 1)
            for j in range(4):
                at = slice(32 * j, 32 * j + 2)
                link(dve.tensor_tensor(modr[at, :], bank[0][at, :], modb[at, :], ALU.add), mod_rows)
            dve.wait_ge(mcol_in, 32)
            for i, m in enumerate((mcol, mcol_c)):
                link(dve.scalar_tensor_tensor(out=acol[:, i, :], in0=m[:, 1, :], scalar=1.0, in1=gcol[:, 0, :],
                                              op0=ALU.add, op1=ALU.mult), acol_done)

            def job_rows(i):
                dve.wait_ge(pe_mod, 2 + i)
                if i in (0, 2):
                    dve.wait_ge(modb2_in, 16 * 3)
                if i == 3:
                    dve.wait_ge(modb3_in, 16 * 2)
                if i >= 1:
                    dve.wait_ge(*((mod_out_rest, 64 * i) if i <= 2 else (mod2_out, 64 * (i - 2))))
                for j in range(4):
                    at = slice(32 * j, 32 * j + 1)
                    link(dve.tensor_tensor(mod_row[at, :], bank[7 if i else 0][at, :], mod_bias[i % 3][at, :], ALU.add), mod_rows)

            dve.wait_ge(convw_T, CC)
            link(dve.tensor_copy(convc[:, :, :], bank[3][:, 0:CC * 34].rearrange("p (a b) -> p a b", b=34)), convc_done)
            dve.wait_ge(xT_done, 2 * DC)
            link(dve.memset(u_pad[:, :, 0:PADC], 0.0))
            link(dve.memset(u_pad[:, :, PADC + T:UW], 0.0))
            for cc in range(CC):
                dve.wait_ge(sig_done, cc + 1)
                link(dve.tensor_tensor(u_pad[:, cc, PADC:PADC + T], bank[2 * (cc % 2)][:, :], sig[cc % 2], ALU.mult), u_done)
            for cc in range(CC):
                link(dve.tensor_scalar(conv[:, cc, :], u_pad[:, cc, 0:T], convc[:, cc, 0:1], convc[:, cc, CONV_W:CONV_W + 1],
                                       ALU.mult, ALU.add))
                for k in range(1, CONV_W):
                    link(dve.scalar_tensor_tensor(out=conv[:, cc, :], in0=u_pad[:, cc, k:k + T], scalar=convc[:, cc, k:k + 1],
                                                  in1=conv[:, cc, :], op0=ALU.mult, op1=ALU.add),
                         conv_done if k == CONV_W - 1 else None)
            job_rows(0)
            def conv_centre():
                dve.wait_ge(cmean_done, 1)
                for cc in range(CC):
                    link(dve.tensor_tensor(conv[:, cc, :], conv[:, cc, :], bank[7][:, :], ALU.subtract), ccen_done)

            def conv_var():
                dve.wait_ge(cvar_done, 1)
                link(dve.tensor_scalar(conv_t, bank[7][:, :], EPS, None, ALU.add), cms_done)

            def conv_norm():
                inv_root((conv_r, conv_t, conv_s), (croot_done, 1))
                for cc in range(CC):
                    link(dve.tensor_tensor(conv[:, cc, :], conv[:, cc, :], conv_r, ALU.mult), cnorm_done)

            def normalise(n):
                dve.wait_ge(p_done, n + 1)
                one = slice(n % 2, n % 2 + 1)
                link(dve.tensor_tensor(rinv[:, one], ssum[:, 0, n:n + 1], ssum[:, 1, n:n + 1], ALU.add))
                link(dve.reciprocal(rinv[:, one], rinv[:, one]))
                link(dve.tensor_scalar(prob[n % 3], prob[n % 3], rinv[:, one], None, ALU.mult), pn_done)

            for n in range(H * TT):
                h, t = n // TT, n % TT
                if t == 0:
                    dve.wait_ge(bias_in[h % 2], 32 * (h // 2 + 1))
                    link(dve.tensor_tensor(bias[h % 2], bias[h % 2], band[:, :].unsqueeze(1).broadcast_to([P, 14, 64]), ALU.add))
                dve.wait_ge(s_done, n + 1)
                if n >= 3:
                    dve.wait_ge(pT_done, n - 2)
                at = 6 - 2 * t
                link(dve.tensor_tensor_reduce(prob[n % 3][:, 0:T], bank[n % 2][:, :], bias[h % 2][:, at:at + ROWS, :].rearrange("p a b -> p (a b)"),
                                              1.0, NEG, ALU.add, ALU.max, smx[:, n % 3, 0:1]))
                link(dve.tensor_reduce(smx[:, n % 3, 1:2], bank[2 + n % 2][:, 0:CTX], AX, ALU.max))
                link(dve.tensor_scalar(smx[:, n % 3, 2:3], smx[:, n % 3, 0:1], smx[:, n % 3, 1:2], -1.0, ALU.max, ALU.mult), nmax_done)
                if n >= 1:
                    normalise(n - 1)
                if n == AT_MEAN + 1:
                    conv_centre()
                if n == AT_VAR + 1:
                    conv_var()
                if n == AT_VAR + 2:
                    conv_norm()
                if n - 1 in AT_JOB:
                    job_rows(1 + AT_JOB.index(n - 1))
            normalise(H * TT - 1)
            for c in range(DC):
                dve.wait_ge(gates_done, c + 1)
                b = 4 * (c % 2)
                link(dve.tensor_tensor(gate_a[c % 2], bank[b + 2][:, :], gate_a[c % 2], ALU.mult))
                link(dve.tensor_tensor(gate_c[c % 2], bank[b + 3][:, :], gate_c[c % 2], ALU.mult))
                link(dve.tensor_tensor(mixT[:, c, :], gate_a[c % 2], gate_c[c % 2], ALU.add), mix_done)
            dve.wait_ge(rows_in, 16 * 5)
            link(dve.scalar_tensor_tensor(out=a2_b, in0=a2_b, scalar=1.0, in1=tmp2, op0=ALU.add, op1=ALU.mult))
            def second_norm(t, block, g1, a2, sh2, h2, tmp):
                n = block * TT + t
                for j in range(2):
                    at = slice(j * 512, j * 512 + 512)
                    dve.wait_ge(wo_pe, 2 * n + j + 1)
                    link(dve.tensor_tensor(tmp, bank[2 * t + j][:, :], g1[:, at], ALU.mult))
                    link(dve.tensor_tensor(xr[:, t, at], xr[:, t, at], tmp, ALU.add), res_done)
                dve.wait_ge(ssq_done, SQ_2ND[block] + t + 1)
                one = slice(t, t + 1)
                link(dve.tensor_scalar(rms_t[:, one], ssq[:, one], 1.0 / D, EPS, ALU.mult, ALU.add), ms_done)
                inv_root((rms[:, one], rms_t[:, one], ssq[:, one]), (root_done, MS_2ND[block] + t + 1))
                link(dve.tensor_scalar(h2[:, t, :], xr[:, t, :], rms[:, one], None, ALU.mult))
                link(dve.tensor_tensor(h2[:, t, :], h2[:, t, :], a2, ALU.mult))
                link(dve.tensor_tensor(h2[:, t, :], h2[:, t, :], sh2, ALU.add), h2_done)

            dve.wait_ge(xres_in, 16)
            dve.wait_ge(mod2_out, 16 * 12)
            for t in range(TT):
                second_norm(t, 0, g1_b, a2_b, sh2_b, h2r, tmp[:, 0:512])
            link(dve.memset(lgp, NEG))
            for t in range(TT):
                dve.wait_ge(logit_pe, t + 1)
                link(dve.tensor_tensor(lg[:, t, :], bank[2 * t][:, 0:NG + NE], br[:, :], ALU.add))
            link(dve.tensor_copy(lgp[:, :, 0:NG], lg[:, :, 0:NG]))
            for t in range(TT):
                link(dve.max(gval[:, t, :], lgp[:, t, :]))
                link(dve.max_index(ridx[:, 0, t, :], gval[:, t, :], lgp[:, t, :]))
            link(dve.tensor_tensor(gexp, lg[:, :, 0:NG], gval[:, :, 0:1].broadcast_to([P, TT, NG]), ALU.subtract), gsub_done)
            link(dve.tensor_copy(gif, ridx[:, 0, :, 0]))
            link(dve.tensor_tensor(oneh, iota[:, 0:NG].unsqueeze(1).broadcast_to([P, TT, NG]),
                                   gif.unsqueeze(2).broadcast_to([P, TT, NG]), ALU.is_equal))
            link(dve.tensor_scalar(pen, oneh, 1.0, -NEG, ALU.subtract, ALU.mult))
            em = emask.rearrange("p t (g e) -> p t g e", e=EPG)
            link(dve.tensor_tensor(em, lg[:, :, NG:NG + NE].rearrange("p t (g e) -> p t g e", e=EPG),
                                   oneh.unsqueeze(3).broadcast_to([P, TT, NG, EPG]), ALU.mult))
            link(dve.tensor_tensor(em, em, pen.unsqueeze(3).broadcast_to([P, TT, NG, EPG]), ALU.add))
            for t in range(TT):
                link(dve.max(eval_[:, t, :], emask[:, t, :]))
                link(dve.max_index(ridx[:, 1, t, :], eval_[:, t, :], emask[:, t, :]))
            link(dve.tensor_tensor(dval, eval_[:, :, 1], eval_[:, :, 0], ALU.subtract), gsub_done)
            link(dve.tensor_copy(eif, ridx[:, 1, :, 0:2]))
            for s in range(2):
                link(dve.tensor_tensor(pick[:, s, :, :], iota[:, 0:NE].unsqueeze(1).broadcast_to([P, TT, NE]),
                                       eif[:, :, s:s + 1].broadcast_to([P, TT, NE]), ALU.is_equal))
            link(dve.tensor_tensor(both, pick[:, 0, :, :], pick[:, 1, :, :], ALU.add), both_done)
            dve.wait_ge(gexp_done, 1)
            link(dve.tensor_reduce(psum_, gexp, AX, ALU.add))
            link(dve.reciprocal(psum_, psum_))
            dve.wait_ge(gexp_done, 2)
            link(dve.tensor_scalar(dden, dexp, 1.0, None, ALU.add))
            link(dve.reciprocal(dden, dden))
            link(dve.tensor_tensor(gw[:, 0, :], dden, psum_, ALU.mult))
            link(dve.tensor_tensor(gw[:, 1, :], gw[:, 0, :], dexp, ALU.mult))
            dve.wait_ge(rank_pe, 1)
            link(dve.tensor_copy(rank, bank[1][:, 0:TT * NE].rearrange("p (t e) -> p t e", e=NE)))
            link(dve.tensor_copy(cnt, bank[1][:, TT * NE:TT * NE + NE]))
            link(dve.tensor_scalar(nblk, cnt, float(CAP), None, ALU.is_gt))
            for k in range(2, T // CAP):
                link(dve.scalar_tensor_tensor(out=nblk, in0=cnt, scalar=float(CAP * k), in1=nblk, op0=ALU.is_gt, op1=ALU.add))
            a, b = incl, incl2
            link(dve.tensor_copy(a, nblk))
            for sh in (1, 2, 4, 8, 16):
                link(dve.tensor_copy(b[:, 0:sh], a[:, 0:sh]))
                link(dve.tensor_tensor(b[:, sh:NE], a[:, sh:NE], a[:, 0:NE - sh], ALU.add))
                a, b = b, a
            total = a
            link(dve.tensor_scalar(e64, iota[:, 0:NE], float(CAP), None, ALU.mult))
            link(dve.tensor_tensor(delta, total, nblk, ALU.subtract))
            link(dve.tensor_scalar(delta, delta, float(CAP), float(NE * CAP - CAP), ALU.mult, ALU.add))
            link(dve.tensor_tensor(delta, delta, e64, ALU.subtract))
            link(dve.tensor_scalar(over_at, rank, float(CAP), None, ALU.is_ge))
            link(dve.tensor_tensor(over_at, over_at, delta.unsqueeze(1).broadcast_to([P, TT, NE]), ALU.mult))
            link(dve.tensor_tensor(over_at, over_at, rank, ALU.add))
            link(dve.tensor_tensor(over_at, over_at, e64.unsqueeze(1).broadcast_to([P, TT, NE]), ALU.add))
            for s in range(2):
                link(dve.tensor_tensor(sel, pick[:, s, :, :], over_at, ALU.mult))
                link(dve.tensor_reduce(slot_f[:, s, :], sel, AX, ALU.add))
            link(dve.tensor_copy(slot_i[:, :, :], slot_f))
            link(dve.tensor_tensor(tab, total.unsqueeze(1).broadcast_to([P, OVER, NE]),
                                   iota[:, 0:OVER].unsqueeze(2).broadcast_to([P, OVER, NE]), ALU.is_le))
            link(dve.tensor_reduce(tab_e, tab, AX, ALU.add))
            link(dve.tensor_scalar(tab_e, tab_e, float(NE - 1), None, ALU.min))
            link(dve.tensor_copy(over_i[:, 1:1 + OVER], tab_e))
            link(dve.tensor_copy(over_i[:, 0:1], total[:, NE - 1:NE]), route_done)

            def expert(e, b):
                dve.wait_ge(silu_done, e + 1)
                unless_first(dve, hidT_pe, e - 1)
                dve.tensor_tensor(hid[b], silu_g[b], bank[2 + b][:, 256:512], ALU.mult).then_inc(hid_done, 1)
                dve.wait_ge(hidT_pe, e + 1)
                unless_first(dve, dn_done, e - 1)
                dve.tensor_copy(hidT[b], bank[4 + b][:, 0:256].rearrange("p (k r) -> p k r", k=2)).then_inc(hidT_done, 1)

            for b in range(2):
                expert(b, b)
            with dve.Fori(1, NE // 2) as i:
                for b in range(2):
                    expert(i * 2 + b, b)
            n_over = dve.value_load(over_i[0:1, 0:1], min_val=0, max_val=OVER)
            with dve.Fori(0, OVER) as i:
                with dve.If(i < n_over):
                    dve.wait_ge(silu_done, i + (NE + 1))
                    dve.tensor_tensor(hid[0], silu_g[0], bank[2][:, 256:512], ALU.mult).then_inc(hid_done, 1)
                    dve.wait_ge(hidT_pe, i + (NE + 1))
                    dve.tensor_copy(hidT[0], bank[4][:, 0:256].rearrange("p (k r) -> p k r", k=2)).then_inc(hidT_done, 1)
            dve.wait_ge(mcol2_in, 16)
            link(dve.scalar_tensor_tensor(out=acol[:, 2, :], in0=mcol_2[:, 1, :], scalar=1.0, in1=gcol[:, 1, :],
                                          op0=ALU.add, op1=ALU.mult), acol2_done)
            def combine(t):
                dve.wait_ge(yg_in[t], 32)
                y0, y1 = ygat[t % 2]
                link(dve.tensor_scalar(y0, y0, gw[:, 0, t:t + 1], None, ALU.mult))
                link(dve.scalar_tensor_tensor(out=y0, in0=y1, scalar=gw[:, 1, t:t + 1], in1=y0, op0=ALU.mult, op1=ALU.add))
                link(dve.tensor_tensor(y0, y0, g2_b, ALU.mult))
                link(dve.tensor_tensor(xr[:, t, :], xr[:, t, :], y0, ALU.add), comb_done)

            def inv_rms(at, count):
                one = slice(at, at + 1)
                dve.wait_ge(ssq_done, SQ_FINAL + count)
                link(dve.tensor_scalar(rms_t[:, one], ssq[:, one], 1.0 / D, EPS, ALU.mult, ALU.add), ms_done)
                inv_root((rms[:, one], rms_t[:, one], ssq[:, one]), (root_done, MS_FINAL + count))

            for n in range(TT + 2):
                if n < TT:
                    combine(n)
                if 1 <= n <= TT:
                    inv_rms(n - 1, final_at(n - 1))
                    if n == 1:
                        dve.wait_ge(fn_in, 16)
                    link(dve.scalar_tensor_tensor(out=xr[:, n - 1, :], in0=xr[:, n - 1, :], scalar=rms[:, n - 1:n], in1=fn_b,
                                                  op0=ALU.mult, op1=ALU.mult), x2_done)
                if n >= 2:
                    inv_rms(TT + n - 2, first_at(n - 2))
                    link(dve.tensor_scalar(xnb[:, n - 2, :], xr[:, n - 2, :], rms[:, TT + n - 2:TT + n - 1], None, ALU.mult), xnb_done)
            dve.wait_ge(f_pe, 1)
            dve.wait_ge(wr_in, 16 * 10)
            link(dve.tensor_tensor(flog, bank[6][:, 0:TT * H].rearrange("p (t h) -> p t h", h=H),
                                   bf[:, :].unsqueeze(1).broadcast_to([P, TT, H]), ALU.add))
            link(dve.scalar_tensor_tensor(out=fabs, in0=flog, scalar=-1.0, in1=flog, op0=ALU.mult, op1=ALU.min), f_dve)
            dve.wait_ge(f_act, 1)
            link(dve.scalar_tensor_tensor(out=flog, in0=flog, scalar=0.0, in1=fabs, op0=ALU.min, op1=ALU.subtract), f_dve)
            dve.wait_ge(f_pe, 2)
            link(dve.tensor_copy(fcum, bank[7][:, 0:TT * H].rearrange("p (t h) -> p t h", h=H)), f_dve)

            def stick_beta(h):
                x, y, z = stick_a[h % 2], stick_b[h % 2], bank[3 * (h % 2):3 * (h % 2) + 3]
                dve.wait_ge(sbl_done, 2 * h + 2)
                if h >= 2:
                    dve.wait_ge(sbo_pe, h - 1)
                for i, w in enumerate(PIECES):
                    link(dve.scalar_tensor_tensor(out=x[:, i, 0:w], in0=z[i][:, 0:w], scalar=0.0, in1=x[:, i, 0:w], op0=ALU.max, op1=ALU.add))
                for i, w in enumerate(PIECES):
                    link(dve.tensor_tensor(y[:, i, 0:w], z[i][:, 0:w], x[:, i, 0:w], ALU.subtract), sbb_done if i == 2 else None)

            def stick_rest(h):
                y, z = stick_b[h % 2], bank[3 * (h % 2):3 * (h % 2) + 3]
                dve.wait_ge(sbr_pe, h + 1)
                for i, w in enumerate(PIECES):
                    link(dve.tensor_tensor(y[:, i, 0:w], z[i][:, 0:w], y[:, i, 0:w], ALU.add), sbc_done if i == 2 else None)

            for h in range(H + 1):
                if h >= 1:
                    stick_rest(h - 1)
                if h < H:
                    stick_beta(h)

            def fox_max(n):
                w = (n % TT + 1) * P
                dve.wait_ge(s_done, H * TT + n + 1)
                if n >= 3:
                    dve.wait_ge(p_done, H * TT + n - 2)
                link(dve.tensor_reduce(smx[:, n % 3, 0:1], bank[n % 3][:, 0:w], AX, ALU.max))
                link(dve.tensor_scalar(smx[:, n % 3, 2:3], smx[:, n % 3, 0:1], -1.0, None, ALU.mult), nmax_done)

            def fox_out(h):
                dve.wait_ge(o_done, H * TT + TT * (h + 1))
                link(dve.reciprocal(rinv[:, 0:TT], ssum[:, 0, TT * h:TT * h + TT]))
                link(dve.tensor_tensor(mixed[0][:, :, h * HD:(h + 1) * HD], bank[(5, 7)[h % 2]][:, 0:256].rearrange("p (t d) -> p t d", d=HD),
                                       rinv[:, 0:TT].unsqueeze(2).broadcast_to([P, TT, HD]), ALU.mult), att_done)

            def out_norm(part, half):
                dve.wait_ge(msq_done, TT * part + TT)
                link(dve.tensor_reduce(mss, msq.rearrange("p t (h d) -> p t h d", d=HD), AX, ALU.add), mms_done)
                link(dve.tensor_scalar(mss, mss, 1.0 / HD, EPS, ALU.mult, ALU.add), mms_done)
                inv_root((mrt, mss, msc), (mroot_done, part + 1))
                for t in range(TT):
                    m = mixed[half][:, t, :].rearrange("p (h d) -> p h d", d=HD)
                    link(dve.tensor_tensor(m, m, mrt[:, t, :].unsqueeze(2).broadcast_to([P, H, HD]), ALU.mult), mixed_done)

            for n in range(H * TT):
                fox_max(n)
                if n >= TT + 3 and (n - 3) % TT == 0:
                    fox_out((n - 3) // TT - 1)
                if n == STICK_NORM + 1:
                    out_norm(0, 1)
            fox_out(H - 1)
            out_norm(1, 0)
            dve.wait_ge(rows2_in, 16 * 4)
            link(dve.scalar_tensor_tensor(out=a2_2, in0=a2_2, scalar=1.0, in1=nf_2, op0=ALU.add, op1=ALU.mult))
            for t in range(TT):
                second_norm(t, 1, gt1_2, a2_2, sh2_2, h2r_2, tmp_2)

            TOPK_STEPS = 33

            def topk(n, b):
                k = 0

                def step(ins, hold=False):
                    nonlocal k
                    k += 1
                    ins.then_inc(topk_step, 1)
                    dve.wait_ge(topk_step, at_head(n, TOPK_STEPS, k))
                    if hold:
                        dve.sem_inc(mark, 1)

                def top16(val, idx, src, rest):
                    step(dve.max(val[:, 0:8], src), True)
                    step(dve.max_index(idx[:, 0:8], val[:, 0:8], src), True)
                    step(dve.match_replace(rest, val[:, 0:8], src, NEG), True)
                    step(dve.max(val[:, 8:16], rest), True)
                    step(dve.max_index(idx[:, 8:16], val[:, 8:16], rest), True)

                dve.wait_ge(sc_pe, at_head(n, 1, 1))
                dve.sem_inc(mark, 1)
                for p in range(2):
                    top16(hval[:, p, :], hidx[:, p, :], bank[0][:, p * P:(p + 1) * P], work[:, p, :])
                step(dve.tensor_copy(hidx_f, hidx[:, :, :]))
                step(dve.tensor_tensor(cand.rearrange("p (a b) -> p a b", b=K16), hval[:, 0, :].unsqueeze(2).broadcast_to([P, K16, K16]),
                                       hval[:, 1, :].unsqueeze(1).broadcast_to([P, K16, K16]), ALU.add), True)
                top16(top, pos, cand, cand2)
                step(dve.tensor_scalar(gsub, top, top[:, 0:1], None, ALU.subtract))
                step(dve.tensor_single_scalar(pos_hl[:, 0, :], pos[:, :], 4, ALU.logical_shift_right))
                step(dve.tensor_single_scalar(pos_hl[:, 1, :], pos[:, :], K16 - 1, ALU.bitwise_and))
                step(dve.tensor_copy(pos_f, pos_hl[:, :, :]))
                dve.sem_inc(gsub2_done, 1)
                for p in range(2):
                    step(dve.tensor_tensor(onehot, iota[:, 0:K16].unsqueeze(1).broadcast_to([P, K16, K16]),
                                           pos_f[:, p, :].unsqueeze(2).broadcast_to([P, K16, K16]), ALU.is_equal))
                    step(dve.tensor_tensor(onehot, onehot, hidx_f[:, p, :].unsqueeze(1).broadcast_to([P, K16, K16]), ALU.mult))
                    step(dve.tensor_reduce(half_i[:, p, :], onehot, AX, ALU.add))
                step(dve.scalar_tensor_tensor(out=id_f, in0=half_i[:, 0, :], scalar=float(P), in1=half_i[:, 1, :], op0=ALU.mult, op1=ALU.add))
                if n[1] >= 2:
                    dve.wait_ge(up_free, at_head(n, UP_SETS, 0))
                dve.tensor_copy(ids[b][:, :], id_f).then_inc(ids_done, 1)
                dve.wait_ge(gex_done, at_head(n, 1, 1))
                step(dve.reciprocal(gsum, gsum))
                step(dve.tensor_scalar(gate_p[b], gex, gsum, None, ALU.mult))
                while k < TOPK_STEPS:
                    k += 1
                    dve.sem_inc(topk_step, 1)
                assert k == TOPK_STEPS

            def peer_head(n, b, t, more):
                def dot(g):
                    dve.wait_ge(down_in[g % DOWN_SETS], at_head(n, 16 * G4 * (UP_SETS // DOWN_SETS), 16 * G4 * (g // DOWN_SETS + 1)))
                    for k in range(G4):
                        r = G4 * g + k
                        buf = down[r % (G4 * DOWN_SETS)]
                        d = dve.tensor_tensor_reduce(buf, buf, h2r_2[:, t, :], 1.0, 0.0, ALU.mult, ALU.add, dots[:, r:r + 1])
                    d.then_inc(down_free, 1)

                def gated(g):
                    at = slice(G4 * g, G4 * g + G4)
                    dve.wait_ge(gelu_done, at_head(n, UP_SETS, g + 1))
                    dve.tensor_tensor(coef[:, at], gel[:, at], gate_p[b][:, at], ALU.mult).then_inc(coef_done, 1)

                dot(0)
                dot(1)
                gated(0)
                if more:
                    topk((n[0], n[1] + 1), 1 - b)
                dot(2)
                gated(1)
                dot(3)
                gated(2)
                gated(3)

            def last_norm(t):
                for j in range(2):
                    at = slice(512 * j, 512 * j + 512)
                    dve.wait_ge(peer_done, t + 1)
                    link(dve.tensor_tensor(tmp_p, bank[4 + 2 * (t % 2) + j][:, :], gt2_2[:, at], ALU.mult))
                    link(dve.tensor_tensor(xr[:, t, at], xr[:, t, at], tmp_p, ALU.add), fin_add if j == 1 else None)
                one = slice(t, t + 1)
                dve.wait_ge(ssq_done, SQ_LAST + t + 1)
                link(dve.tensor_scalar(rms_t[:, one], ssq[:, one], 1.0 / D, EPS, ALU.mult, ALU.add), ms_done)
                inv_root((rms[:, one], rms_t[:, one], ssq[:, one]), (root_done, MS_LAST + t + 1))
                link(dve.scalar_tensor_tensor(out=xr[:, t, :], in0=xr[:, t, :], scalar=rms[:, one], in1=gfin, op0=ALU.mult, op1=ALU.mult), fin_done)

            topk((None, 0), 0)
            for t in range(TT):
                last = t == TT - 1
                with dve.Fori(0, H // 2 - last) as i:
                    for b in range(2):
                        peer_head((i, t * H + b), b, t, True)
                if last:
                    peer_head((None, TT * H - 2), 0, t, True)
                    peer_head((None, TT * H - 1), 1, t, False)
                if t == 0:
                    dve.wait_ge(last_rows_in, 16 * 2)
                if t >= 1:
                    last_norm(t - 1)
            last_norm(TT - 1)

        @block.tensor
        def _(pe):
            def project(dst, w, at, rhs, chunks=DC, stationary=None):
                for c in range(chunks):
                    mm = pe.matmul(dst, w[:, c, at], rhs[:, c, :], start=(c == 0), stop=(c == chunks - 1))
                return mm

            def rows_of(dst, xT, t, w, at, chunks=DC):
                for c in range(chunks):
                    mm = pe.matmul(dst, xT[:, c, t * P:(t + 1) * P], w[:, c, at], start=(c == 0), stop=(c == chunks - 1))
                return mm

            def modulation(n, b, vecs):
                for j in range(4):
                    slab_ready(pe, n + j)
                for c in range(DC):
                    for j in range(4):
                        mm = pe.matmul(bank[b][32 * j:32 * j + vecs.stop - vecs.start, :], cvec[:, vecs, c],
                                       slab(n + j)[:, c, :], start=(c == 0), stop=(c == DC - 1))
                mm.then_inc(pe_mod, 1)

            pe.wait_ge(consts, 1)
            pe.wait_ge(cw_in, 16 * 4)
            for cc in range(CC):
                pe.transpose(bank[3][:, 34 * cc:34 * cc + 34], convw_in[0:34, cc * P:(cc + 1) * P], ident[0:34, 0:34])\
                    .then_inc(convw_T, 1)
            pe.wait_ge(silu_c, 1)
            modulation(N_MOD, 0, slice(0, 2))
            for g in range(2 * DC):
                c = g % DC
                if g >= 4:
                    pe.wait_ge(hT_done, g - 3)
                if g == 0:
                    pe.wait_ge(xn_done, CT)
                if g == DC:
                    pe.wait_ge(xn_done, CT + TT)
                for t in range(CT if g < DC else TT):
                    src = cr if g < DC else xr
                    mm = pe.transpose(bank[4 + g % 4][:, t * P:(t + 1) * P], src[:, t, c:D:DC], ident[:, :])
                mm.then_inc(xT_done, 1)
            pe.wait_ge(hT_done, 2 * DC)
            pe.wait_ge(mod_rows, 4)
            pe.wait_ge(convc_done, 1)
            slab_ready(pe, N_GLU)
            slab_ready(pe, N_GLU + 1)
            for cc in range(CC):
                if cc >= 2:
                    pe.wait_ge(u_done, cc - 1)
                at = slice(cc * P, (cc + 1) * P)
                project(bank[2 * (cc % 2)][:, :], slab(N_GLU), at, hT)
                project(bank[2 * (cc % 2) + 1][:, :], slab(N_GLU + 1), at, hT).then_inc(glu_done, 1)

            def conv_mean():
                pe.wait_ge(conv_done, CC)
                for cc in range(CC):
                    mm = pe.matmul(bank[7][:, :], mean_w[:, :], conv[:, cc, :], start=(cc == 0), stop=(cc == CC - 1))
                mm.then_inc(cmean_done, 1)

            def conv_var():
                pe.wait_ge(csq_done, CC)
                for cc in range(CC):
                    mm = pe.matmul(bank[7][:, :], mean_w[:, :], conv_sq[:, cc, :], start=(cc == 0), stop=(cc == CC - 1))
                mm.then_inc(cvar_done, 1)

            for m in range(18):
                if m >= 4:
                    pe.wait_ge(proj_out, m - 3)
                if m in (0, 8, 14):
                    slab_ready(pe, {0: N_K, 8: N_V, 14: N_Q}[m])
                dst = bank[4 + m % 4]
                if m < 4:
                    mm = project(dst[:, :], slab(N_K), slice(m * P, (m + 1) * P), hT)
                elif m < 8:
                    mm = project(dst[:, 0:CTX], slab(N_K), slice((m - 4) * P, (m - 3) * P), hcT)
                elif m < 10:
                    mm = rows_of(dst[:, :], hcT, m - 8, slab(N_V), slice(0, 512))
                elif m < 14:
                    mm = rows_of(dst[:, :], hT, m - 10, slab(N_V), slice(0, 512))
                else:
                    mm = project(dst[:, :], slab(N_Q), slice((m - 14) * P, (m - 13) * P), hT)
                mm.then_inc(proj_done, 1)
                if m == PROJ_JOB:
                    pe.wait_ge(u_done, CC)
                    modulation(N_JOB, 0, slice(0, 1))

            def scores(n):
                h, t = n // TT, n % TT
                if n >= 2:
                    pe.wait_ge(p_done, n - 1)
                at = slice(HD * (h % 2), HD * (h % 2) + HD)
                q = qT[at, h // 2, t * P:(t + 1) * P]
                pe.matmul(bank[n % 2][:, :], q, kT[at, h // 2, :], start=True, stop=True)
                pe.matmul(bank[2 + n % 2][:, 0:CTX], q, kcT[at, h // 2, :], start=True, stop=True).then_inc(s_done, 1)

            def transposes(n):
                pe.wait_ge(pn_done, n + 1)
                if n >= 1:
                    pe.wait_ge(pTa_out, n)
                    pe.wait_ge(pTb_out, n)
                for k in range(KEYS // P):
                    dst = bank[4][:, k * P:(k + 1) * P] if k < 4 else bank[5][:, (k - 4) * P:(k - 3) * P]
                    mm = pe.transpose(dst, prob[n % 3][:, k * P:(k + 1) * P], ident[:, :])
                mm.then_inc(pT_done, 1)

            def weighted(n):
                h, t = n // TT, n % TT
                pe.wait_ge(pTa_out, n + 1)
                pe.wait_ge(pTb_out, n + 1)
                if t == 0 and h >= 2:
                    pe.wait_ge(head_done, h - 1)
                at = slice(h * HD, (h + 1) * HD)
                half = slice(HD * (h % 2), HD * (h % 2) + HD)
                for k in range(KEYS // P):
                    v = vrow[:, k, at] if k < TT else vcrow[:, k - TT, at]
                    mm = pe.matmul(bank[6][half, t * P:(t + 1) * P], v, probT[n % 2][:, k, :], start=(k == 0), stop=(k == KEYS // P - 1))
                mm.then_inc(o_done, 1)

            pe.wait_ge(proj_out, 18)
            pe.wait_ge(mod_rows, 4 + 4)
            for n in range(H * TT + 3):
                if n < H * TT:
                    scores(n)
                if 2 <= n <= H * TT + 1:
                    transposes(n - 2)
                if n >= 3:
                    weighted(n - 3)
                if n == AT_MEAN:
                    conv_mean()
                if n == AT_VAR:
                    conv_var()
                if n in AT_JOB:
                    i = 1 + AT_JOB.index(n)
                    if i == 1:
                        pe.wait_ge(cms_done, 1)
                    else:
                        pe.wait_ge(mod_rows, 4 + 4 * i)
                    modulation(N_JOB + 4 * i, 7, slice(0, 1) if i < 2 else slice(2, 3))
            pe.wait_ge(head_done, H)
            pe.wait_ge(convy_done, CC)
            pe.wait_ge(mod_rows, 24)
            for c in range(DC):
                if c == 0:
                    for i in range(4):
                        slab_ready(pe, N_GA + i)
                if c == 4:
                    slab_ready(pe, N_GA + 4)
                    slab_ready(pe, N_GA + 5)
                if c >= 2:
                    pe.wait_ge(mix_done, c - 1)
                b = 4 * (c % 2)
                n = N_GA if c < 4 else N_GA + 4
                at = slice((c % 4) * P, (c % 4) * P + P)
                project(bank[b][:, :], slab(n), at, hT)
                project(bank[b + 1][:, :], slab(n + 1), at, hT)
                project(bank[b + 2][:, :], slab(N_GA + 2), slice(c * P, (c + 1) * P), attT, AC)
                project(bank[b + 3][:, :], slab(N_GA + 3), slice(c * P, (c + 1) * P), conv, CC).then_inc(merge_pe, 1)
            pe.wait_ge(mix_done, DC)
            slab_ready(pe, N_WO)
            slab_ready(pe, N_WO + 1)
            for g in range(2 * TT):
                rows_of(bank[g][:, :], mixT, g // 2, slab(N_WO + g % 2), slice(0, 512)).then_inc(wo_pe, 1)
            def second_T(t, block, h2):
                pe.wait_ge(h2_done, block * TT + t + 1)
                for c in range(DC):
                    mm = pe.transpose(bank[2 * t + c // 4][:, (c % 4) * P:(c % 4) * P + P], h2[:, t, c:D:DC], ident[:, :])
                mm.then_inc(h2T_pe, 1)

            for t in range(TT):
                second_T(t, 0, h2r)
                if t == 0:
                    pe.wait_ge(wr_in, 16 * 10)
                pe.wait_ge(h2T_done, 2 * t + 2)
                rows_of(bank[2 * t][:, 0:NG + NE], h2T, t, wr, slice(0, NG + NE)).then_inc(logit_pe, 1)
            pe.wait_ge(both_done, 1)
            for t in range(TT + 1):
                dst = bank[1][:, t * NE:(t + 1) * NE]
                for k in range(min(t, TT - 1) + 1):
                    mm = pe.matmul(dst, before[:, :] if k == t else ones[:, :], both[:, k, :], start=(k == 0),
                                   stop=(k == min(t, TT - 1)))
            mm.then_inc(rank_pe, 1)

            def block_T(b):
                for c in range(DC):
                    mm = pe.transpose(bank[b][:, c * CAP:(c + 1) * CAP], xblk[b][:, c:D:DC], ident[0:CAP, 0:CAP])
                return mm

            def block_gu(b, n):
                gu = ring[:, n % RING:n % RING + 2, :].rearrange("p g (c f) -> p g c f", c=DC)
                for c in range(DC):
                    for half in range(2):
                        at = slice(CAP * half, CAP * half + CAP)
                        mm = pe.matmul(bank[2 + b][at, :].rearrange("p (g f) -> p g f", g=2), xbT[b][:, c, :],
                                       gu[:, :, c, 256 * half:256 * half + 256], start=(c == 0), stop=(c == DC - 1))
                return mm

            def hidden_T(b):
                for k in range(2):
                    mm = pe.transpose(bank[4 + b][:, k * P:(k + 1) * P], hid[b][:, k:256:2], ident[:, :])
                return mm

            def block_dn(b, n):
                for i in range(4):
                    half, k = i // 2, i % 2
                    for j in range(2):
                        mm = pe.matmul(bank[6 + b][CAP * j:CAP * j + CAP, :], hidT[b][:, k, CAP * half:CAP * half + CAP],
                                       slab(n)[:, half, k, 512 * j:512 * j + 512], start=(i == 0), stop=(i == 3))
                return mm

            def expert(e, b, i):
                n = N_EXP + 3 * b

                def arrived(k):
                    pe.wait_ge(slab_in[(n + k) % RING], i * 16 + 16 * ((n + k) // RING + 1))

                pe.wait_ge(xb_in[b], i * 16 + 16)
                pe.sem_inc(mark, 1)
                block_T(b).then_inc(xbT_done, 1)
                pe.wait_ge(xbT_out, e + 1)
                arrived(0)
                arrived(1)
                block_gu(b, n).then_inc(gu_done, 1)
                pe.wait_ge(hid_done, e + 1)
                hidden_T(b).then_inc(hidT_pe, 1)
                pe.wait_ge(hidT_done, e + 1)
                arrived(2)
                unless_first(pe, yv_done, e - 1)
                block_dn(b, n + 2).then_inc(dn_done, 1)

            pe.wait_ge(route_done, 1)
            for b in range(2):
                expert(b, b, 0)
            with pe.Fori(1, NE // 2) as i:
                for b in range(2):
                    expert(i * 2 + b, b, i)
            n_over = pe.value_load(over_i[0:1, 0:1], min_val=0, max_val=OVER)
            with pe.Fori(0, OVER) as i:
                with pe.If(i < n_over):
                    pe.wait_ge(ov_xin, i * 16 + 16)
                    pe.sem_inc(mark, 1)
                    block_T(0).then_inc(xbT_done, 1)
                    pe.wait_ge(xbT_out, i + (NE + 1))
                    pe.wait_ge(ov_slab, i * 48 + 48)
                    block_gu(0, N_EXP).then_inc(gu_done, 1)
                    pe.wait_ge(hid_done, i + (NE + 1))
                    hidden_T(0).then_inc(hidT_pe, 1)
                    pe.wait_ge(hidT_done, i + (NE + 1))
                    block_dn(0, N_EXP + 2).then_inc(dn_done, 1)
            for t in range(TT):
                pe.wait_ge(xnb_done, t + 1)
                for c in range(DC):
                    mm = pe.transpose(bank[2 * t + c // 4][:, (c % 4) * P:(c % 4 + 1) * P], xnb[:, t, c:D:DC], ident[:, :])
                    if c % 4 == 3:
                        mm.then_inc(xT_done, 1)
            pe.wait_ge(wr_in, 16 * 10)
            pe.wait_ge(hT_done, 2 * DC + TT * DC)
            for t in range(TT):
                mm = rows_of(bank[6][:, t * H:(t + 1) * H], hT, t, wf, slice(0, H))
            mm.then_inc(f_pe, 1)

            def project2(m):
                if m >= 6:
                    pe.wait_ge(proj_out, 18 + (m - 5 if m < 12 else m))
                k = (S_STICK, S_FOX)[m // 12] + m // 4 % 3
                if m % 4 == 0:
                    slab2_ready(pe, k)
                dst = bank[m % 6] if m < 12 else bank[7]
                if m // 4 % 3 < 2:
                    mm = project(dst[:, :], slab2(k), slice((m % 4) * P, (m % 4 + 1) * P), hT)
                else:
                    mm = rows_of(dst[:, :], hT, m % 4, slab2(k), slice(0, 512))
                mm.then_inc(proj_done, 1)

            for m in range(12):
                project2(m)
                if m == 7:
                    pe.wait_ge(f_dve, 2)
                    for t in range(TT):
                        at = slice(t * H, (t + 1) * H)
                        for k in range(t):
                            pe.matmul(bank[7][:, at], ones[:, :], flog[:, k, :], start=(k == 0), stop=False)
                        pe.matmul(bank[7][:, at], before[:, :], flog[:, t, :], start=(t == 0), stop=False)
                        mm = pe.matmul(bank[7][:, at], ident[:, :], flog[:, t, :], start=False, stop=True)
                    mm.then_inc(f_pe, 1)
                if m == 9:
                    pe.wait_ge(f_dve, 3)
                    for t in range(TT):
                        mm = pe.transpose(bank[6][0:H, t * P:(t + 1) * P], fcum[:, t, :], ident[:, :])
                    mm.then_inc(f_pe, 1)
            pe.wait_ge(proj_out, 18 + 12)
            pe.wait_ge(f_act, 2)

            def fox_scores(n):
                h, t = n // TT, n % TT
                w = (t + 1) * P
                if n >= 3:
                    pe.wait_ge(p_done, H * TT + n - 2)
                at = slice(HD * (h % 2), HD * (h % 2) + HD)
                dst = bank[n % 3]
                pe.matmul(dst[:, 0:w], fqT[at, h // 2, t * P:(t + 1) * P], fkT[at, h // 2, 0:w], start=True, stop=False)
                pe.matmul(dst[:, 0:w], ident[0:H, h:h + 1].broadcast_to([H, P]), fcumT[:, 0:w], start=False, stop=False)
                pe.matmul(dst[:, t * P:w], ident[:, :], causal[:, :], start=False, stop=True).then_inc(s_done, 1)

            def fox_transposes(n):
                pe.wait_ge(p_done, H * TT + n + 1)
                if n >= 2:
                    pe.wait_ge(pTa_out, H * TT + n - 1)
                for k in range(n % TT + 1):
                    mm = pe.transpose(bank[3 + n % 2][:, k * P:(k + 1) * P], fprob[n % 3][:, k * P:(k + 1) * P], ident[:, :])
                mm.then_inc(pT_done, 1)

            def fox_weighted(n):
                h, t = n // TT, n % TT
                pe.wait_ge(pTa_out, H * TT + n + 1)
                if t == 0 and h >= 2:
                    pe.wait_ge(att_done, h - 1)
                for k in range(t + 1):
                    mm = pe.matmul(bank[(5, 7)[h % 2]][:, t * HD:(t + 1) * HD], fprobT[n % 2][:, k * P:(k + 1) * P],
                                   fvr[:, k, h * HD:(h + 1) * HD], start=(k == 0), stop=(k == t))
                mm.then_inc(o_done, 1)

            def fox_step(n):
                if n < H * TT:
                    fox_scores(n)
                if 2 <= n <= H * TT + 1:
                    fox_transposes(n - 2)
                if n >= 3:
                    fox_weighted(n - 3)

            def stick_scores(h):
                if h >= 2:
                    pe.wait_ge(sbc_done, h - 1)
                at = slice(HD * (h % 2), HD * (h % 2) + HD)
                for j in range(TT):
                    b, o = stick_cols(j, j)
                    mm = pe.matmul(bank[3 * (h % 2) + b][:, o:o + T - j * P], skT_[at, h // 2, j * P:(j + 1) * P], sqT[at, h // 2, j * P:T],
                                   start=True, stop=True)
                mm.then_inc(sbz_pe, 1)

            def stick_sums(h):
                x = stick_a[h % 2]
                pe.wait_ge(mask_done, 2 * h + 1)
                pe.wait_ge(sbb_done, h + 1)
                for j in range(TT):
                    b, o = stick_cols(j, j)
                    w = T - j * P
                    mm = pe.matmul(bank[3 * (h % 2) + b][:, o:o + w], later_neg[:, :], x[:, b, o:o + w], start=True, stop=(j == TT - 1))
                    for k in range(j + 1, TT):
                        b2, o2 = stick_cols(k, k)
                        mm = pe.matmul(bank[3 * (h % 2) + b][:, o + (k - j) * P:o + w], ones_neg[:, :], x[:, b2, o2:o2 + T - k * P],
                                       start=False, stop=(k == TT - 1))
                mm.then_inc(sbr_pe, 1)

            def stick_out(h):
                y = stick_b[h % 2]
                pe.wait_ge(mask_done, 2 * h + 2)
                if h >= 1:
                    pe.wait_ge(sbo_done, h)
                for t in range(TT):
                    for j in range(t + 1):
                        b, o = stick_cols(j, t)
                        mm = pe.matmul(bank[6][:, t * HD:(t + 1) * HD], y[:, b, o:o + P], svr[:, j, h * HD:(h + 1) * HD],
                                       start=(j == 0), stop=(j == t))
                mm.then_inc(sbo_pe, 1)

            for h in range(H + 1):
                if h < H:
                    stick_scores(h)
                for m in stick_fill[h][0]:
                    project2(m)
                if h >= 2:
                    stick_out(h - 2)
                if h >= 1:
                    stick_sums(h - 1)
                for m in stick_fill[h][1]:
                    project2(m)

            def mix_columns(k, b):
                for t in range(TT):
                    mm = pe.transpose(bank[b][:, t * P:(t + 1) * P], mixed[k // AC][:, t, k % AC * P:(k % AC + 1) * P], ident[:, :])
                mm.then_inc(attT_pe, 1)

            pe.wait_ge(proj_out, 18 + 24)
            for n in range(H * TT + 3):
                if n == 2:
                    stick_out(H - 1)
                    pe.wait_ge(sbc_done, H)
                fox_step(n)
                if n in STICK_COLS:
                    i = STICK_COLS.index(n)
                    pe.wait_ge(mixed_done, TT)
                    if i == 0:
                        pe.wait_ge(sbo_done, H)
                    else:
                        pe.wait_ge(attT_done, i)
                    mix_columns(AC + i, 6)
            pe.wait_ge(mixed_done, 2 * TT)
            for k in range(AC):
                mix_columns(k, k)
            pe.wait_ge(attT_done, DC)
            slab2_ready(pe, S_WO)
            slab2_ready(pe, S_WO + 1)
            for g in range(2 * TT):
                rows_of(bank[g][:, :], mixT2, g // 2, slab2(S_WO + g % 2), slice(0, 512)).then_inc(wo_pe, 1)
            for t in range(TT):
                second_T(t, 1, h2r_2)
            pe.wait_ge(h2T_done, 4 * TT)
            def query(t, q):
                m = 4 * t + q
                if t == 0:
                    slab2_ready(pe, S_WQ + q)
                if m >= 3:
                    pe.wait_ge(q_done, m - 2)
                for k in range(4):
                    mm = project(bank[1 + m % 3][:, k * P:(k + 1) * P], slab2(S_WQ + q), slice(k * P, (k + 1) * P), h2T[:, :, t * P:(t + 1) * P])
                mm.then_inc(q_pe, 1)

            for q in range(4):
                query(0, q)
            pe.wait_ge(sk_dma, 16)
            for m in range(4):
                for k in range(4):
                    mm = pe.transpose(bank[4 + m][:, k * P:(k + 1) * P], sk_in[:, 4 * m + k, :], ident[:, :])
                mm.then_inc(skT_pe, 1)

            def peer_scores(n, head):
                pe.wait_ge(qh_done, at_head(n, 1, 1))
                if n[1] > 0:
                    pe.wait_ge(ids_done, at_head(n, 1, 0))
                pe.sem_inc(mark, 1)
                for p in range(2):
                    keys = skT[:, head, p * P:(p + 1) * P] if isinstance(head, int) else \
                        skT[:, bass.ds(head, 1), p * P:(p + 1) * P].rearrange("p a b -> p (a b)")
                    mm = pe.matmul(bank[0][:, p * P:(p + 1) * P], qh[:, p, :], keys, start=True, stop=True)
                mm.then_inc(sc_pe, 1)

            def peer_head(n, t, nxt):
                if nxt is not None:
                    peer_scores((n[0], n[1] + 1), nxt)
                for g in range(UP_SETS):
                    pe.wait_ge(diag_done, at_head(n, UP_SETS, g + 1))
                    pe.wait_ge(up_in[g], at_head(n, 16 * G4, 16 * G4))
                    for r in range(G4 * g, G4 * g + G4):
                        for j in range(2):
                            mm = pe.matmul(bank[4 + 2 * (t % 2) + j][:, :], diag[:, r, :], up[r][:, 512 * j:512 * j + 512], start=False, stop=False)
                    mm.then_inc(up_free, 1)

            def edge(t, first):
                for j in range(2):
                    mm = pe.matmul(bank[4 + 2 * (t % 2) + j][:, :], zeros[:, :], zeros[:, :].unsqueeze(1).broadcast_to([P, 4, P]),
                                   start=first, stop=not first)
                return mm

            query(1, 0)
            pe.wait_ge(skT_done, 5)
            peer_scores((None, 0), 0)
            for m in range(5, 4 * TT):
                query(m // 4, m % 4)
            pe.wait_ge(q_pe, 4 * TT)
            pe.sem_inc(up_free, UP_SETS)
            for t in range(TT):
                last = t == TT - 1
                if t >= 2:
                    pe.wait_ge(fin_add, t - 1)
                edge(t, True)
                with pe.Fori(0, H // 2 - last) as i:
                    for b in range(2):
                        peer_head((i, t * H + b), t, i * 2 + (b + 1))
                if last:
                    peer_head((None, TT * H - 2), t, H - 1)
                    peer_head((None, TT * H - 1), t, None)
                edge(t, False).then_inc(peer_done, 1)


_INS = ["x", "c", "ctx", "c_ctx", "w_mod", "b_mod", "norm_mix", "w_in", "rpb", "w_att_out", "conv_w", "conv_b",
        "conv_ln_g", "conv_ln_b", "w_conv_out", "w_o", "norm_ffn", "w_router_group", "b_router_group",
        "w_router_expert", "b_router_expert", "w_exp_gate", "w_exp_up", "w_exp_down", "final_norm", "c_2", "w_ada_2",
        "b_ada_2", "g_norm_mix_2", "w_in_2", "b_forget_2", "g_out_fox_2", "g_out_sb_2", "w_out_2", "g_norm_ffn_2",
        "w_query_2", "sub_keys_2", "expert_down_2", "expert_up_2", "g_final_2"]
_FLAT = {"c_ctx", "final_norm", "g_final_2"}


def kernel(**inputs):
    import concourse.bacc as _bacc
    from concourse.bass_utils import run_bass_kernel_spmd as _run

    nc = _bacc.Bacc("TRN2", target_bir_lowering=False, num_devices=1)
    arrays, A = {}, {}
    for name in _INS:
        a = np.ascontiguousarray(inputs[name])
        arrays[f"in_{name}"] = a
        ap = nc.dram_tensor(f"in_{name}", a.shape, F32, kind="ExternalInput").ap()
        A[name] = ap if name in _FLAT else ap[0]
    out = nc.dram_tensor("out_0", (T, D), F32, kind="ExternalOutput").ap()
    build(nc, A, out)
    r = _run(nc, [arrays], core_ids=[0])
    return r.results[0]["out_0"].reshape(1, T, D)
```

```python
from contextlib import ExitStack

import numpy as np
import concourse.bass as bass
from concourse import mybir

F32 = mybir.dt.float32
I32 = mybir.dt.int32
U32 = mybir.dt.uint32
ALU = mybir.AluOpType
ACT = mybir.ActivationFunctionType
AX = mybir.AxisListType.X

P = 128
T = 512
TT = T // P
D = 1024
DC = D // P
CTX = 256
CT = CTX // P
H = 8
HD = 64
DA = H * HD
AC = DA // P
GRID_W, WIN = 64, 16
ROWS = T // GRID_W
RPB_R, RPB_C = 2 * ROWS - 1, 2 * WIN - 1
SKEW = 128
CONV_W = 31
PADC = CONV_W // 2
CC = 512 // P
UW = T + 2 * PADC
NG, NE, EPG = 4, 32, 8
F = 512
CAP = 64
OVER = (2 * T) // (CAP + 1)
SLOTS = (NE + OVER) * CAP
EPS = 1e-6
NEG = -1e30
RING = 6
SLAB = 4096
KEYS = T + CTX
K16 = 16
G4 = 4
DOWN_SETS = 2
GROUPS = K16 // G4
UP_FIRST, UP_SETS = 2, GROUPS


class Link:

    def __init__(self, eng, own):
        self.eng, self.own, self.count = eng, own, {}

    def __call__(self, ins, sem=None):
        sem = self.own if sem is None else sem
        n = self.count.get(id(sem), 0) + 1
        self.count[id(sem)] = n
        ins.then_inc(sem, 1)
        self.eng.wait_ge(sem, n)
        return n


def build(nc, A, out):
    with ExitStack() as ctx:
        def sb(name, shape, dt=F32):
            return ctx.enter_context(nc.sbuf_tensor(name, shape, dt))

        def sem(name):
            return ctx.enter_context(nc.semaphore(name))

        def dram(name, shape, dt=F32):
            return nc.dram_tensor(name, shape, dt, kind="Internal")

        bank = [ctx.enter_context(nc.psum_tensor(f"bank{i}", [P, 512], F32)) for i in range(8)]
        ring = sb("ring", [P, RING, SLAB])
        arena_x = sb("arena_x", [P, 4224])
        arena_h = sb("arena_h", [P, 4096])
        arena_q = sb("arena_q", [P, 4096])
        arena_v = sb("arena_v", [P, 8192])
        arena_w = sb("arena_w", [P, 4864])

        def view(arena, at, *shape):
            n = int(np.prod(shape))
            ap = arena[:, at:at + n]
            if len(shape) == 1:
                return ap
            names = "abcd"[:len(shape)]
            return ap.rearrange(f"p ({' '.join(names)}) -> p {' '.join(names)}",
                                **{k: v for k, v in zip(names[1:], shape[1:])})

        def slot(s, *shape):
            ap = ring[:, s, :]
            names = "abcd"[:len(shape)]
            return ap.rearrange(f"p ({' '.join(names)}) -> p {' '.join(names)}",
                                **{k: v for k, v in zip(names[1:], shape[1:])})

        ident = sb("ident", [P, P])
        before = sb("before", [P, P])
        ones = sb("ones", [P, P])
        later_neg = sb("later_neg", [P, P])
        ones_neg = sb("ones_neg", [P, P])
        causal = sb("causal", [P, P])
        mean_w = sb("mean_w", [P, P])
        iota_i = sb("iota_i", [P, 64], I32)
        iota = sb("iota", [P, 64])
        part_i = sb("part_i", [P, 1], I32)
        band = sb("band", [P, 64])
        band_t = sb("band_t", [P, 2, 64])
        stick_neg = band_t[:, :, :].rearrange("p a b -> p (a b)")
        wstart = sb("wstart", [P, 4])

        cvec = sb("cvec", [P, 3, DC])
        mcol = sb("mcol", [P, 2, DC])
        mcol_c = sb("mcol_c", [P, 2, DC])
        mcol_2 = sb("mcol_2", [P, 2, DC])
        gcol = sb("gcol", [P, 2, DC])
        acol = sb("acol", [P, 3, DC])
        convc = sb("convc", [P, CC, 34])
        ssq = sb("ssq", [P, 8])
        rms = sb("rms", [P, 8])
        rms_t = sb("rms_t", [P, 8])
        smx = sb("smx", [P, 3, 4])
        ssum = sb("ssum", [P, 2, 32])
        rinv = sb("rinv", [P, 8])

        xr = view(arena_x, 0, TT, D)
        u_pad = view(arena_x, 0, CC, UW)
        conv = view(arena_x, CC * UW, CC, T)
        hT = view(arena_h, 0, DC, T)
        modr = view(arena_q, 0, T)
        modb = view(arena_q, 3 * T, T)
        mod_row = view(arena_v, 4096, T)
        mod_bias = [view(arena_v, 4608 + T * i, T) for i in range(3)]
        junk = view(arena_q, 6 * T, D)
        kT = view(arena_q, 0, AC, T)
        qT = view(arena_q, AC * T, AC, T)
        mixT = view(arena_q, 0, DC, T)
        vrow = view(arena_v, 0, TT, DA)
        kcT = view(arena_v, 2048, AC, CTX)
        vcrow = view(arena_v, 3072, CT, DA)
        hcT = view(arena_v, 4096, DC, CTX)
        cr = view(arena_v, 6144, CT, D)
        attT = view(arena_v, 6144, AC, T)
        bias = [view(arena_w, 896 * i, 14, 64) for i in range(2)]
        spare = sb("spare", [P, KEYS])
        prob = [view(arena_w, 1792 + KEYS * i, KEYS) for i in range(2)] + [spare[:, :]]
        probT = [view(arena_w, 3328 + KEYS * i, KEYS // P, P) for i in range(2)]
        sig = [prob[i][:, 0:T] for i in range(2)]
        convw_in = view(arena_w, 4096, T)
        rpb_pad = view(arena_w, 4608, SKEW)
        conv_sq = view(arena_x, 0, CC, T)
        conv_s, conv_t, conv_r = (conv_sq[:, i, :] for i in range(3))
        gate_a = [view(arena_w, T * i, T) for i in range(2)]
        gate_c = [view(arena_w, 1024 + T * i, T) for i in range(2)]
        tmp = view(arena_w, 2048, D)
        tmp2 = view(arena_w, 3072, D)
        g1_b = view(arena_v, 0, D)
        a2_b = view(arena_v, D, D)
        sh2_b = view(arena_v, 2 * D, D)
        g2_b = view(arena_v, 3 * D, D)
        h2r = view(arena_v, 4096, TT, D)

        def route(at, *shape):
            return view(arena_w, at, *shape)
        junk2 = view(arena_w, 0, D)
        h2T = view(arena_h, 0, DC, T)
        lg = route(1024, TT, NG + NE)
        lgp = route(1168, TT, 8)
        gval, eval_ = route(1200, TT, 8), route(1232, TT, 8)
        gexp, oneh, pen = route(1264, TT, NG), route(1280, TT, NG), route(1296, TT, NG)
        gif, psum_, eif = route(1312, TT), route(1316, TT), route(1320, TT, 2)
        dval, dexp, dden = route(1328, TT), route(1332, TT), route(1336, TT)
        emask = route(1344, TT, NE)
        pick = route(1472, 2, TT, NE)
        both = route(1728, TT, NE)
        rank = route(1856, TT, NE)
        cnt, nblk, incl, incl2, delta, e64 = (route(1984 + 32 * i, NE) for i in range(6))
        over_at = route(2176, TT, NE)
        sel = route(2304, TT, NE)
        slot_f = route(2432, 2, TT)
        tab = route(2440, OVER, NE)
        tab_e = route(2920, OVER)
        ridx = sb("ridx", [P, 2, TT, 8], U32)
        slot_i = sb("slot_i", [P, 2, TT], I32)
        gw = sb("gw", [P, 2, TT])
        over_i = sb("over_i", [P, 16], I32)
        wr = sb("wr", [P, DC, NG + NE])
        br = sb("br", [P, NG + NE])
        zeros = sb("zeros", [P, P])
        xblk = [arena_h[0:CAP, D * i:D * i + D] for i in range(2)]
        xbT = [view(arena_h, 2048 + 512 * i, DC, CAP) for i in range(2)]
        yblk = [view(arena_h, 3072 + 512 * i, 512) for i in range(2)]
        silu_g = [view(arena_q, 256 * i, 256) for i in range(2)]
        hid = [view(arena_q, 512 + 256 * i, 256) for i in range(2)]
        hidT = [view(arena_q, 1024 + 256 * i, 2, P) for i in range(2)]
        ygat = [[view(arena_v, 4096 + 2048 * i + 1024 * s, D) for s in range(2)] for i in range(2)]
        fn_b = g1_b
        xnb = view(arena_q, 0, TT, D)

        wf = sb("wf", [P, DC, H])
        bf = sb("bf", [P, H])
        gob = sb("gob", [P, 2])
        sqT, skT_ = view(arena_v, 0, AC, T), view(arena_v, 2048, AC, T)
        svr, fvr = view(arena_v, 4096, TT, DA), view(arena_v, 6144, TT, DA)
        fqT, fkT = view(arena_q, 0, AC, T), view(arena_q, 2048, AC, T)
        junk3 = view(arena_w, 2304, D)
        flog = route(4256, TT, H)
        fabs = route(4288, TT, H)
        fcum = route(4320, TT, H)
        fcumT = arena_w[0:H, 4352:4352 + T]
        hold_a, hold_b = ring[:, 0, :], ring[:, 1, :]
        NT = (1, TT - 1)
        stick_x = [[spare[:, P * i:P * i + P] for i in range(3)], [view(hold_a, T * i, T) for i in range(3)]]
        stick_y = [[spare[:, P * (3 + i):P * (4 + i)] for i in range(3)], [view(hold_a, T * (3 + i), T) for i in range(5)]]
        mixed = [[view(arena_w, 2304 + DA * i, 1, DA) for i in range(2)],
                 [view(hold_b, 3 * DA * i, 3, DA) for i in range(2)]]
        mixed_heads = [view(arena_w, 2304, 2 * H, HD), view(hold_b, 0, 6 * H, HD)]
        fprob = [[view(arena_h, P * i, P) for i in range(3)], [view(arena_v, 4096 + T * i, T) for i in range(3)]]
        fprobT = [[view(arena_h, P * (3 + i), P) for i in range(2)], [view(arena_v, 5632, T), view(hold_b, 3072, T)]]
        msq = [view(arena_h, 640, 2 * H, HD), view(arena_q, 0, 6 * H, HD)]
        mss, mrt, msc = ([view(arena_h, 1664 + 16 * i, 2 * H), view(arena_q, 3072 + 48 * i, 6 * H)] for i in range(3))
        mixT2 = [view(arena_h, 2048, DC, P), view(arena_q, 0, DC, 3 * P)]
        rows_2 = [[view(ring[:, 3, :], D * i, D) for i in range(4)], [view(arena_v, 4096 + D * i, D) for i in range(4)]]
        tmp_2 = [view(arena_h, 0, 512), view(hold_b, 3072, 512)]
        h2r_2 = [view(arena_w, 3092, D)] + [view(hold_b, D * i, D) for i in range(TT - 1)]
        h2T_2 = [view(arena_h, 3072, DC, P), view(arena_q, 0, DC, 3 * P)]
        wo_b = [view(arena_v, 0, DC, 512), view(hold_a, 0, DC, 512)]
        wq_b = [view(hold_a, 0, DC, 2 * P), view(arena_v, 6144, DC, 2 * P)]
        qT2_a = view(arena_h, 0, H, 2 * P)
        qT2_b = view(arena_v, 0, 3 * H, 2 * P)
        sk_in = view(arena_q, 2048, 2 * H, P)
        skT = route(0, H + 1, 2 * P)
        gt2_2, gfin = view(arena_q, 0, D), view(arena_q, D, D)
        tmp_p = route(4256, 512)
        diag = view(arena_h, 2048, K16, P)
        qh = view(spare, 0, 2, P)
        work = view(spare, 256, 2, P)
        cand = view(spare, 512, K16 * K16)

        def small(at, *shape):
            return route(2304 + at, *shape)
        cand2 = small(0, K16 * K16)
        onehot = small(256, K16, K16)
        hval = small(512, 2, K16)
        hidx_f = small(544, 2, K16)
        pos_f = small(576, 2, K16)
        top = small(608, K16)
        half_i = small(624, 2, K16)
        id_f = small(656, K16)
        gsub, gex = small(672, K16), small(688, K16)
        gate_p = [small(704 + K16 * i, K16) for i in range(2)]
        dots, gel, coef = small(736, K16), small(752, K16), small(768, K16)
        gsum = small(784, 1)
        hidx = sb("hidx", [P, 2, K16], U32)
        pos = sb("pos", [P, K16], U32)
        pos_hl = sb("pos_hl", [P, 2, K16], U32)
        ids = [sb(f"ids{i}", [P, K16], I32) for i in range(2)]
        down = [ring[:, 2 + r // 4, D * (r % 4):D * (r % 4) + D] for r in range(G4 * DOWN_SETS)]
        up = [ring[:, 4 + r // 4, D * (r % 4):D * (r % 4) + D] for r in range(G4 * UP_FIRST)]
        up += [hold_b[:, 3 * D:4 * D], arena_q[:, 3 * D:4 * D], arena_h[:, 0:D], arena_h[:, D:2 * D]]
        up += [hold_a[:, 2 * D:3 * D], hold_a[:, 3 * D:4 * D], arena_v[:, 6144:6144 + D], arena_v[:, 7168:7168 + D]]

        def up_set(n, g):
            per = 16 * G4
            if n[1] < H:
                return g % UP_FIRST, (per * GROUPS // UP_FIRST, per * (g // UP_FIRST + 1))
            at = (g + UP_FIRST) % GROUPS
            before = per * GROUPS // UP_FIRST * H if at < UP_FIRST else 0
            return at, (per, per + before - per * H)

        def up_used(n, g):
            return at_head(n, GROUPS, UP_FIRST + g + 1)

        mod_d = dram("mod_d", [2, 6 * D])
        mod2_d = dram("mod2_d", [1, 6 * D])
        skew_d = dram("skew_d", [H * RPB_R, GRID_W, SKEW])
        xs_d = dram("xs_d", [SLOTS, D])
        ys_d = dram("ys_d", [SLOTS, D])

        slab_in = [sem(f"slab_in{s}") for s in range(RING)]
        vec_in = sem("vec_in")
        x_in = sem("x_in")
        modb_in = sem("modb_in")
        cw_in = sem("cw_in")
        modb2_in = sem("modb2_in")
        modb3_in = sem("modb3_in")
        rpb_in = sem("rpb_in")
        skew_out = sem("skew_out")
        bias_in = [sem("bias_in0"), sem("bias_in1")]
        mod_out = sem("mod_out")
        mod2_out = sem("mod2_out")
        convc_done = sem("convc_done")
        mcol2_in = sem("mcol2_in")
        mod_out_rest = sem("mod_out_rest")
        mcol_in = sem("mcol_in")
        xres_in = sem("xres_in")
        rows_in = sem("rows_in")
        xs_zero = sem("xs_zero")
        ys_zero = sem("ys_zero")
        out_dma = sem("out_dma")
        const_step = sem("const_step")
        consts = sem("consts")
        pe_mod = sem("pe_mod")
        mod_rows = sem("mod_rows")
        dve_step = sem("dve_step")
        act_step = sem("act_step")
        silu_c = sem("silu_c")
        ssq_done = sem("ssq_done")
        ms_done = sem("ms_done")
        root_done = sem("root_done")
        xn_done = sem("xn_done")
        acol_done = sem("acol_done")
        xT_done = sem("xT_done")
        hT_done = sem("hT_done")
        convw_T = sem("convw_T")
        glu_done = sem("glu_done")
        sig_done = sem("sig_done")
        u_done = sem("u_done")
        conv_done = sem("conv_done")
        proj_done = sem("proj_done")
        proj_out = sem("proj_out")
        cmean_done = sem("cmean_done")
        ccen_done = sem("ccen_done")
        csq_done = sem("csq_done")
        cvar_done = sem("cvar_done")
        cms_done = sem("cms_done")
        croot_done = sem("croot_done")
        cnorm_done = sem("cnorm_done")
        convy_done = sem("convy_done")
        s_done = sem("s_done")
        nmax_done = sem("nmax_done")
        p_done = sem("p_done")
        pT_done = sem("pT_done")
        pTa_out = sem("pTa_out")
        pTb_out = sem("pTb_out")
        o_done = sem("o_done")
        att_done = sem("att_done")
        pn_done = sem("pn_done")
        head_done = sem("head_done")
        attT_pe = sem("attT_pe")
        attT_done = sem("attT_done")
        merge_pe = sem("merge_pe")
        gates_done = sem("gates_done")
        mix_done = sem("mix_done")
        wo_pe = sem("wo_pe")
        res_done = sem("res_done")

        h2_done = sem("h2_done")
        h2T_pe = sem("h2T_pe")
        h2T_done = sem("h2T_done")
        logit_pe = sem("logit_pe")
        gsub_done = sem("gsub_done")
        gexp_done = sem("gexp_done")
        both_done = sem("both_done")
        rank_pe = sem("rank_pe")
        route_done = sem("route_done")
        wr_in = sem("wr_in")
        wo_b_in = sem("wo_b_in")
        fn_in = sem("fn_in")
        scat = sem("scat")
        xbT_done = sem("xbT_done")
        xbT_out = sem("xbT_out")
        gu_done = sem("gu_done")
        silu_done = sem("silu_done")
        hid_done = sem("hid_done")
        hidT_pe = sem("hidT_pe")
        hidT_done = sem("hidT_done")
        dn_done = sem("dn_done")
        yv_done = sem("yv_done")
        over_done = sem("over_done")
        ov_xin = sem("ov_xin")
        ov_slab = sem("ov_slab")
        ov_ydma = sem("ov_ydma")
        comb_done = sem("comb_done")
        x2_done = sem("x2_done")
        xnb_done = sem("xnb_done")
        mark = sem("mark")
        xb_in = [sem("xb_in0"), sem("xb_in1")]
        y_dma = [sem("y_dma0"), sem("y_dma1")]
        acol2_done = sem("acol2_done")
        f_pe = sem("f_pe")
        f_dve = sem("f_dve")
        f_act = sem("f_act")
        sbz_pe = sem("sbz_pe")
        sbl_done = sem("sbl_done")
        sbb_done = sem("sbb_done")
        sbr_pe = sem("sbr_pe")
        sbc_done = sem("sbc_done")
        sbe_done = sem("sbe_done")
        sbo_pe = sem("sbo_pe")
        sbo_done = sem("sbo_done")
        msq_done = sem("msq_done")
        mms_done = sem("mms_done")
        mroot_done = sem("mroot_done")
        mixed_done = sem("mixed_done")
        sk_dma = sem("sk_dma")
        skT_pe = sem("skT_pe")
        skT_done = sem("skT_done")
        q_pe = sem("q_pe")
        q_done = sem("q_done")
        qh_done = sem("qh_done")
        sc_pe = sem("sc_pe")
        topk_step = sem("topk_step")
        gsub2_done = sem("gsub2_done")
        gex_done = sem("gex_done")
        ids_done = sem("ids_done")
        down_free = sem("down_free")
        up_free = sem("up_free")
        gelu_done = sem("gelu_done")
        coef_done = sem("coef_done")
        diag_done = sem("diag_done")
        peer_done = sem("peer_done")
        fin_add = sem("fin_add")
        fin_done = sem("fin_done")
        rows2_in = sem("rows2_in")
        last_rows_in = sem("last_rows_in")
        down_in = [sem(f"down_in{i}") for i in range(DOWN_SETS)]
        up_in = [sem(f"up_in{i}") for i in range(UP_SETS)]
        yg_in = [sem(f"yg_in{t}") for t in range(TT)]

        def cols_pc(w, j):
            return w[:, j * 512:(j + 1) * 512].rearrange("(p c) n -> p c n", c=DC)

        def cols_cp(w, j):
            return w[:, j * 512:(j + 1) * 512].rearrange("(c p) n -> p c n", p=P)

        def rows_kp(w):
            return w.rearrange("(k p) n -> p k n", p=P)

        w_in = A["w_in"]
        QKV, GLU, GA, GB = 0, 3, 5, 7
        slabs = []
        slabs += [(cols_pc(A["w_mod"], j), (DC, 512), pe_mod, 1) for j in range(4)]
        slabs += [(cols_pc(w_in, GLU), (DC, 512), glu_done, CC), (cols_pc(w_in, GLU + 1), (DC, 512), glu_done, CC)]
        slabs += [(cols_pc(w_in, QKV + 1), (DC, 512), proj_done, 8), (cols_pc(w_in, QKV + 2), (DC, 512), proj_done, 14),
                  (cols_pc(w_in, QKV), (DC, 512), proj_done, 18)]
        slabs += [(cols_pc(A["w_mod"], 4 + j), (DC, 512), pe_mod, 2 + j // 4) for j in range(8)]
        slabs += [(cols_pc(A["w_ada_2"], j), (DC, 512), pe_mod, 4 + j // 4) for j in range(12)]
        slabs += [(cols_pc(w_in, GA), (DC, 512), merge_pe, 4), (cols_pc(w_in, GB), (DC, 512), merge_pe, 4),
                  (rows_kp(A["w_att_out"]), (AC, D), merge_pe, 8), (rows_kp(A["w_conv_out"]), (CC, D), merge_pe, 8),
                  (cols_pc(w_in, GA + 1), (DC, 512), merge_pe, 8), (cols_pc(w_in, GB + 1), (DC, 512), merge_pe, 8)]
        slabs += [(cols_cp(A["w_o"], j), (DC, 512), wo_pe, 8) for j in range(2)]
        N_MOD, N_GLU, N_K, N_V, N_Q, N_JOB, N_GA, N_WO = 0, 4, 6, 7, 8, 9, 29, 35

        def w_gu(w, e):
            return w[e, :, :].rearrange("(p c) n -> p c n", c=DC)

        def w_dn(w, e):
            return w[e, :, :].rearrange("(h p k) n -> p h k n", h=2, k=2)

        PROJ_JOB, AT_MEAN, AT_VAR, AT_JOB = 10, 1, 4, (6, 11, 16, 21)
        N_EXP = len(slabs)
        for e in range(2):
            slabs += [(w_gu(A["w_exp_gate"], e), (DC, F), gu_done, 2 * NE), (w_gu(A["w_exp_up"], e), (DC, F), gu_done, 2 * NE),
                      (w_dn(A["w_exp_down"], e), (2, 2, D), dn_done, 2 * NE)]

        SQ_2ND, SQ_FINAL, SQ_LAST = (CT + TT, CT + 4 * TT), CT + 2 * TT, CT + 5 * TT
        MS_2ND, MS_FINAL, MS_LAST = (1, 3 * TT + 1), TT + 1, 4 * TT + 1

        def final_at(t):
            return max(1, 2 * t)

        def first_at(t):
            return min(2 * t + 3, 2 * TT)

        N2 = N_EXP + 3 * NE
        FOX_W, STICK_W = 3 * DA, 3 * DA + H
        slabs2 = [cols_pc(A["w_in_2"], j) for j in range(3)]
        slabs2 += [A["w_in_2"][:, STICK_W + j * 512:STICK_W + (j + 1) * 512].rearrange("(p c) n -> p c n", c=DC) for j in range(3)]
        slabs2 += [cols_cp(A["w_out_2"], j) for j in range(2)]
        slabs2 += [None]
        slabs2 += [cols_pc(A["w_query_2"], j) for j in range(4)]
        S_FOX, S_STICK, S_WO, S_WQ = 0, 3, 6, 9

        def slab2(k):
            return slot((N2 + k) % RING, DC, 512)

        PROJ_V, PROJ_STICK, PROJS = 2 * TT, 2 * TT + 2 * AC, 2 * TT + 4 * AC

        def proj_slab(m):
            if m < PROJ_V:
                return (S_STICK + 2, S_FOX + 2)[m % 2]
            return (S_STICK if m < PROJ_STICK else S_FOX) + (m - PROJ_V) // AC % 2

        def proj_bank(m):
            return m if m < PROJ_V else (m - PROJ_V) % 6 if m < PROJ_STICK else (0, 4, 5, 7)[m % 4]

        def loaded2(k):
            return 16 * ((N2 + k) // RING + 1)

        def slab2_ready(eng, k):
            eng.wait_ge(slab_in[(N2 + k) % RING], loaded2(k))

        def wq_b_of(h):
            if h == 1:
                return wq_b[1], slab_in[(N2 + S_WQ) % RING], loaded2(S_WQ) + 16
            return wq_b[0], slab_in[(N2 + S_FOX + 2) % RING], loaded2(S_FOX + 2) + 16 * max(1, h)

        UNITS = H * TT

        def unit(n):
            return (n, 0, 0) if n < H else ((n - H) // NT[1], 1 + (n - H) % NT[1], 1)

        BETA, SUMS, REST, EXPS, OUTS = (0, 1), (2, 2), (2, 3), (2, 4), (3, 5)
        FOX_EXP, FOX_T, FOX_OUT = (0, 1), (2, 3), (3, 4)

        EXP_LN = "natural_log_exp_and_others"

        def stick_bank(n):
            return bank[1 + n % 3] if n < H else bank[(1, 2, 3, 7)[n % 4]]

        def of_part(n, first):
            return first <= n < (H if first == 0 else UNITS)

        def last_of_head(n):
            return n == H - 1 or n >= H and unit(n)[1] == TT - 1

        STICK_STEPS, FOX_STEPS = UNITS - H + OUTS[1], UNITS - H + FOX_OUT[1]
        ST_FOX = STICK_STEPS
        ST_NORM = ST_FOX + FOX_STEPS
        ST_OUT = ST_NORM + 2
        ST_QUERY = ST_OUT + 6
        AHEAD = 2
        STEPS = ST_QUERY + AHEAD
        weight = [4] * (UNITS - H) + [3] * OUTS[1] + [3] * (UNITS - H) + [3] * FOX_OUT[1]
        weight += [4, 8, 14, 14, 14, 4, 4, 4] + [8] * AHEAD
        PARTS = 8
        LEAD = 6
        PLAN = [[[s for s in range(LEAD, STEPS) if int(sum(weight[LEAD:s]) / sum(weight[LEAD:]) * (H * PARTS - 4)) == h * PARTS + p]
                 for p in range(PARTS)] for h in range(H)]
        WO_BANKS = ((4, 5), (1, 2), (3, 6), (7, 1))
        SK_BANKS = (3, 5, 7, 4)
        H2T_BANKS = ((4, 5), (2, 3), (6, 7), (1, 2))

        def at_head(n, per, extra):
            i, off = n
            return per * off + extra if i is None else i * (2 * per) + (per * off + extra)

        def unless_first(eng, s, value):
            if not isinstance(value, int) or value > 0:
                eng.wait_ge(s, value)

        def slab(n):
            return slot(n % RING, *slabs[n][1])

        def slab_ready(eng, n):
            eng.wait_ge(slab_in[n % RING], 16 * (n // RING + 1))

        block = ctx.enter_context(nc.Block())

        @block.sync
        def _(sp):
            for n, (src, shape, _, _) in enumerate(slabs):
                if n >= RING:
                    _, _, free, value = slabs[n - RING]
                    sp.wait_ge(free, value)
                if n == 1:
                    sp.wait_ge(vec_in, 16 * 5)
                    sp.wait_ge(modb_in, 32)
                    sp.wait_ge(cw_in, 16 * 4)
                if n == N_GLU:
                    sp.wait_ge(mcol_in, 32)
                sp.dma_start(slab(n), src).then_inc(slab_in[n % RING], 16)
                if n == 3:
                    sp.dma_start(cr, A["ctx"].rearrange("(t p) d -> p t d", p=P)).then_inc(x_in, 16)
                    sp.dma_start(xr, A["x"].rearrange("(t p) d -> p t d", p=P)).then_inc(x_in, 16)
                if n == N_WO + 1:
                    sp.wait_ge(consts, 1)
                    sp.dma_start(xs_d[:, :].rearrange("(p r) (a b) -> p (r a) b", p=CAP, b=P),
                                 zeros[0:CAP, :].unsqueeze(1).broadcast_to([CAP, SLOTS // CAP * DC, P])).then_inc(xs_zero, 16)
                    sp.dma_start(ys_d[NE * CAP:SLOTS, :].rearrange("(p r) (a b) -> p (r a) b", p=CAP, b=P),
                                 zeros[0:CAP, :].unsqueeze(1).broadcast_to([CAP, OVER * DC, P])).then_inc(ys_zero, 16)

            def rows(e, b):
                unless_first(sp, xbT_done, e - 1)
                sp.dma_start(xblk[b], xs_d[bass.ds(e * CAP, CAP), :]).then_inc(xb_in[b], 16)

            sp.wait_ge(wo_pe, 2 * TT)
            sp.dma_start(sk_in, A["sub_keys_2"].rearrange("h p k d -> k (h p) d")).then_inc(sk_dma, 16)
            sp.wait_ge(scat, 16 * 2 * TT)
            for b in range(2):
                rows(b, b)
            with sp.Fori(1, NE // 2) as i:
                for b in range(2):
                    e = i * 2 + b
                    n = N_EXP + 3 * b
                    rows(e, b)
                    for w, k in (("w_exp_gate", 0), ("w_exp_up", 1)):
                        if k == 0:
                            sp.wait_ge(gu_done, e - 1)
                        sp.dma_start(slab(n + k), A[w][bass.ds(e, 1), :, :].rearrange("o (p c) n -> p (o c) n", c=DC))\
                            .then_inc(slab_in[(n + k) % RING], 16)
                    sp.wait_ge(dn_done, e - 1)
                    sp.dma_start(slab(n + 2), A["w_exp_down"][bass.ds(e, 1), :, :].rearrange("o (h p k) n -> p (o h) k n", h=2, k=2))\
                        .then_inc(slab_in[(n + 2) % RING], 16)
            sp.wait_ge(route_done, 2)
            sp.wait_ge(ys_zero, 16)
            n_over = sp.value_load(over_i[0:1, 0:1], min_val=0, max_val=OVER)
            sp.sem_inc(over_done, 1)
            with sp.Fori(0, OVER) as i:
                with sp.If(i < n_over):
                    sp.wait_ge(gu_done, NE - 1)
                    e = sp.value_load(over_i[0:1, bass.ds(i + 1, 1)], min_val=0, max_val=NE - 1)
                    sp.dma_start(xblk[0], xs_d[bass.ds(i * CAP + NE * CAP, CAP), :]).then_inc(ov_xin, 16)
                    for w, k in (("w_exp_gate", 0), ("w_exp_up", 1)):
                        sp.dma_start(slab(N_EXP + k), A[w][bass.ds(e, 1), :, :].rearrange("o (p c) n -> p (o c) n", c=DC))\
                            .then_inc(ov_slab, 16)
                    sp.wait_ge(dn_done, NE - 1)
                    sp.dma_start(slab(N_EXP + 2), A["w_exp_down"][bass.ds(e, 1), :, :].rearrange("o (h p k) n -> p (o h) k n", h=2, k=2))\
                        .then_inc(ov_slab, 16)
                    sp.wait_ge(yv_done, i + (NE + 1))
                    for half in range(2):
                        sp.dma_start(ys_d[bass.ds(i * CAP + NE * CAP, CAP), 512 * half:512 * half + 512],
                                     yblk[0][CAP * half:CAP * half + CAP, :]).then_inc(ov_ydma, 16)
                    sp.wait_ge(ov_ydma, i * 32 + 32)
                    sp.sem_inc(over_done, 1)
            def load2(k):
                sp.dma_start(slab2(k), slabs2[k]).then_inc(slab_in[(N2 + k) % RING], 16)

            sp.wait_ge(dn_done, NE)
            sp.wait_ge(yg_in[TT - 1], 32)
            for k in (S_STICK + 2, S_FOX + 2, S_STICK, S_STICK + 1, S_FOX, S_FOX + 1):
                load2(k)
            def load_rows(part):
                gt1, a2, sh2, nf = rows_2[part]
                for dst, src in ((gt1, mod2_d[0, 2 * D:3 * D]), (sh2, mod2_d[0, 3 * D:4 * D]), (a2, mod2_d[0, 4 * D:5 * D]),
                                 (nf, A["g_norm_ffn_2"])):
                    sp.dma_start(dst, src.partition_broadcast(P)).then_inc(rows2_in, 16)

            sp.wait_ge(mod2_out, 16 * 12)
            sp.wait_ge(proj_done, 18 + PROJ_V)
            load2(S_WQ + 2)
            load_rows(0)
            for k, used in ((S_WQ, 1), (S_WQ + 1, 2), (S_WO, 3), (S_WO + 1, 4)):
                sp.wait_ge(proj_done, 18 + PROJ_V + AC * used)
                load2(k)
            sp.wait_ge(wo_pe, 2 * TT + 2)
            load2(S_WQ + 3)
            sp.wait_ge(sbo_pe, UNITS)
            for j in range(2):
                sp.dma_start(wo_b[j], cols_cp(A["w_out_2"], j)).then_inc(wo_b_in, 16)
            sp.wait_ge(o_done, H * TT + UNITS)
            load_rows(1)
            for h in range(H):
                dst, there, _ = wq_b_of(h)
                if h == 0:
                    sp.wait_ge(wo_pe, 4 * TT)
                elif h == 1:
                    sp.wait_ge(h2_done, 2 * TT)
                else:
                    sp.wait_ge(q_pe, 4 + 2 * (h if h > 2 else 1))
                sp.dma_start(dst, A["w_query_2"][:, h * 2 * P:(h + 1) * 2 * P].rearrange("(p c) n -> p c n", c=DC)).then_inc(there, 16)
            sp.wait_ge(q_pe, 4 + 2 * H)
            for dst, src in ((gt2_2, mod2_d[0, 5 * D:6 * D]), (gfin, A["g_final_2"])):
                sp.dma_start(dst, src.partition_broadcast(P)).then_inc(last_rows_in, 16)
            for t in range(TT):
                sp.wait_ge(fin_done, t + 1)
                sp.dma_start(out[t * P:(t + 1) * P, :], xr[:, t, :]).then_inc(out_dma, 16)
            sp.wait_ge(out_dma, 16 * TT)
            sp.wait_ge(skew_out, 16)
            sp.wait_ge(mod_out_rest, 16 * 8)
            sp.wait_ge(mod2_out, 16 * 12)

        @block.gpsimd
        def _(pool):
            link = Link(pool, const_step)
            for t, v in ((ident, 0.0), (before, 1.0), (ones, 1.0), (later_neg, -1.0), (ones_neg, -1.0),
                         (causal, 0.0), (mean_w, 1.0 / 512), (zeros, 0.0)):
                link(pool.memset(t[:, :], v))
            link(pool.memset(rpb_pad, 0.0))
            link(pool.affine_select(out=ident[:, :], in_=ident[:, :], compare_op=ALU.not_equal, fill=1.0, base=0,
                                    pattern=[[-1, P]], channel_multiplier=1))
            link(pool.affine_select(out=before[:, :], in_=before[:, :], compare_op=ALU.is_gt, fill=0.0, base=0,
                                    pattern=[[1, P]], channel_multiplier=-1))
            link(pool.affine_select(out=later_neg[:, :], in_=later_neg[:, :], compare_op=ALU.is_gt, fill=0.0, base=0,
                                    pattern=[[-1, P]], channel_multiplier=1))
            link(pool.affine_select(out=causal[:, :], in_=causal[:, :], compare_op=ALU.is_ge, fill=NEG, base=0,
                                    pattern=[[-1, P]], channel_multiplier=1))
            link(pool.iota(iota_i[:, :], pattern=[[1, 64]], base=0, channel_multiplier=0))
            link(pool.iota(part_i[:, :], pattern=[[0, 1]], base=0, channel_multiplier=1), consts)
            for j in range(4):
                pool.wait_ge(mod_rows, j + 1)
                pool.dma_start(mod_d[:, j * 512:(j + 1) * 512], modr[32 * j:32 * j + 2, :]).then_inc(mod_out, 16)
            pool.wait_ge(mod_out, 16 * 4)
            for r, dst in ((0, mcol), (1, mcol_c)):
                pool.dma_start(dst[:, :, :], mod_d[r, 0:2 * D].rearrange("(k p c) -> p k c", k=2, c=DC)).then_inc(mcol_in, 16)

            pool.dma_start(rpb_pad[0:H * RPB_R, GRID_W - WIN:GRID_W - WIN + RPB_C],
                           A["rpb"].rearrange("h r c -> (h r) c")).then_inc(rpb_in, 16)
            pool.wait_ge(rpb_in, 16)
            pool.dma_start(skew_d[:, :, :], rpb_pad[0:H * RPB_R, :].unsqueeze(1).broadcast_to([H * RPB_R, GRID_W, SKEW]))\
                .then_inc(skew_out, 16)

            def store_rows(i):
                for j in range(4):
                    pool.wait_ge(mod_rows, 4 + 4 * i + j + 1)
                    at = (4 * (i + 1) + j if i < 2 else 4 * (i - 2) + j) * 512
                    dst, done = (mod_d, mod_out_rest) if i < 2 else (mod2_d, mod2_out)
                    pool.dma_start(dst[0:1, at:at + 512], mod_row[32 * j:32 * j + 1, :]).then_inc(done, 16)
                if i == 1:
                    for g in (1, 2):
                        pool.dma_start(mod_bias[g - 1][0:P:32, :], A["b_ada_2"][g * 4 * T:(g + 1) * 4 * T].rearrange("(j n) -> j n", n=T))\
                            .then_inc(modb3_in, 16)

            pool.wait_ge(skew_out, 16)
            skew = skew_d[:, :, :]
            for h in range(H):
                if h == 2:
                    store_rows(0)
                if h >= 2:
                    pool.wait_ge(nmax_done, 4 * (h - 1))
                for half in range(2):
                    src = bass.AP(skew.tensor, skew.offset + (h * RPB_R + 1 - half) * GRID_W * SKEW + GRID_W - 1,
                                  [[SKEW - 1, GRID_W], [GRID_W * SKEW, 14], [1, GRID_W]])
                    pool.dma_start(bias[h % 2][64 * half:64 * half + 64, :, :], src).then_inc(bias_in[h % 2], 16)
                for i, n in enumerate(AT_JOB):
                    if (n + 1) // TT + 1 == h:
                        store_rows(1 + i)
            pool.wait_ge(mod_out_rest, 16 * 8)
            pool.wait_ge(o_done, 32)
            for dst, src in ((g1_b, mod_d[0, 2 * D:3 * D]), (sh2_b, mod_d[0, 3 * D:4 * D]), (a2_b, mod_d[0, 4 * D:5 * D]),
                             (g2_b, mod_d[0, 5 * D:6 * D])):
                pool.dma_start(dst, src.partition_broadcast(P)).then_inc(rows_in, 16)
            pool.wait_ge(merge_pe, DC)
            pool.dma_start(xr, A["x"].rearrange("(t p) d -> p t d", p=P)).then_inc(xres_in, 16)
            pool.dma_start(tmp2, A["norm_ffn"].partition_broadcast(P)).then_inc(rows_in, 16)
            pool.wait_ge(mod2_out, 16 * 12)
            pool.dma_start(mcol_2[:, :, :], mod2_d[0, 0:2 * D].rearrange("(k p c) -> p k c", k=2, c=DC)).then_inc(mcol2_in, 16)
            pool.wait_ge(h2_done, TT)
            pool.wait_ge(route_done, 1)
            pool.wait_ge(xs_zero, 16)
            for t in range(TT):
                for s in range(2):
                    pool.indirect_dma_start(xs_d[:, :], bass.IndirectOffsetOnAxis(ap=slot_i[:, s, t:t + 1], axis=0),
                                            h2r[:, t, :], None).then_inc(scat, 16)
            pool.wait_ge(res_done, 2 * TT)
            pool.dma_start(fn_b, A["final_norm"].partition_broadcast(P)).then_inc(fn_in, 16)
            for b in range(2):
                pool.wait_ge(y_dma[b], 32 * (NE // 2))
            pool.wait_ge(route_done, 2)
            n_over = pool.value_load(over_i[0:1, 0:1], min_val=0, max_val=OVER)
            pool.wait_ge(over_done, n_over + 1)
            pool.sem_inc(mark, 1)
            pool.wait_ge(ys_zero, 16)
            pool.wait_ge(scat, 16 * 2 * TT)
            for t in range(TT):
                if t >= 2:
                    pool.wait_ge(comb_done, t - 1)
                for s in range(2):
                    pool.indirect_dma_start(ygat[t % 2][s], None, ys_d[:, :],
                                            bass.IndirectOffsetOnAxis(ap=slot_i[:, s, t:t + 1], axis=0)).then_inc(yg_in[t], 16)
            pool.wait_ge(wo_pe, 2 * TT + 2)
            pool.wait_ge(h2_done, TT + 1)
            pool.sem_inc(down_free, DOWN_SETS)

            def down_rows(n, b, g):
                pool.wait_ge(down_free, at_head(n, GROUPS, g + 1))
                pool.sem_inc(mark, 1)
                for k in range(G4):
                    r = G4 * g + k
                    pool.indirect_dma_start(down[r % (G4 * DOWN_SETS)], None, A["expert_down_2"],
                                            bass.IndirectOffsetOnAxis(ap=ids[b][:, r:r + 1], axis=0)).then_inc(down_in[g % DOWN_SETS], 16)

            def up_rows(n, b, g):
                at, _ = up_set(n, g)
                pool.wait_ge(up_free, up_used(n, g - (UP_FIRST if n[1] < H else UP_SETS)))
                pool.sem_inc(mark, 1)
                for k in range(G4):
                    r = G4 * g + k
                    pool.indirect_dma_start(up[G4 * at + k], None, A["expert_up_2"],
                                            bass.IndirectOffsetOnAxis(ap=ids[b][:, r:r + 1], axis=0)).then_inc(up_in[at], 16)

            def ids_ready(n):
                pool.wait_ge(ids_done, at_head(n, 1, 1))
                pool.sem_inc(mark, 1)

            def gathers(n, b):
                ids_ready(n)
                down_rows(n, b, 0)
                for g in range(1, GROUPS):
                    down_rows(n, b, g)
                    up_rows(n, b, g - 1)
                up_rows(n, b, GROUPS - 1)

            ids_ready((None, 0))
            down_rows((None, 0), 0, 0)
            down_rows((None, 0), 0, 1)
            for h in range(H):
                n, nxt, b = (None, h), (None, h + 1), h % 2
                for g in range(2):
                    down_rows(n, b, 2 + g)
                    up_rows(n, b, g)
                if h + 1 < H:
                    ids_ready(nxt)
                for g in range(2):
                    if h + 1 < H:
                        down_rows(nxt, 1 - b, g)
                    up_rows(n, b, 2 + g)
            pool.wait_ge(qh_done, H + 1)
            pool.wait_ge(q_done, 4 + 2 * AHEAD)
            for t in range(1, TT):
                with pool.Fori(0, H // 2) as i:
                    for b in range(2):
                        gathers((i, t * H + b), b)

        @block.scalar
        def _(act):
            link = Link(act, act_step)
            for i, n in enumerate(("c", "c_ctx", "c_2")):
                act.dma_start(cvec[:, i, :], A[n].rearrange("(p c) -> p c", c=DC)).then_inc(vec_in, 16)
            for i, n in enumerate(("norm_mix", "g_norm_mix_2")):
                act.dma_start(gcol[:, i, :], A[n].rearrange("(p c) -> p c", c=DC)).then_inc(vec_in, 16)
            for r in range(2):
                act.dma_start(modb[r:P:32, :], A["b_mod"][0:4 * T].rearrange("(j n) -> j n", n=T)).then_inc(modb_in, 16)
            act.dma_start(convw_in[0:CONV_W, :], A["conv_w"]).then_inc(cw_in, 16)
            for i, n in enumerate(("conv_b", "conv_ln_g", "conv_ln_b")):
                act.dma_start(convw_in[CONV_W + i:CONV_W + i + 1, :], A[n].rearrange("(a n) -> a n", a=1)).then_inc(cw_in, 16)
            act.dma_start(wr[:, :, 0:NG], A["w_router_group"].rearrange("(p c) e -> p c e", c=DC)).then_inc(wr_in, 16)
            act.dma_start(wr[:, :, NG:NG + NE], A["w_router_expert"].rearrange("(p c) e -> p c e", c=DC)).then_inc(wr_in, 16)
            act.dma_start(br[:, 0:NG], A["b_router_group"].partition_broadcast(P)).then_inc(wr_in, 16)
            act.dma_start(br[:, NG:NG + NE], A["b_router_expert"].partition_broadcast(P)).then_inc(wr_in, 16)
            act.dma_start(wf[:, :, :], A["w_in_2"][:, FOX_W:FOX_W + H].rearrange("(p c) e -> p c e", c=DC)).then_inc(wr_in, 16)
            act.dma_start(bf[:, :], A["b_forget_2"].partition_broadcast(P)).then_inc(wr_in, 16)
            for i, n in enumerate(("g_out_fox_2", "g_out_sb_2")):
                for half in range(2):
                    act.dma_start(gob[HD * half:HD * half + HD, i:i + 1], A[n].rearrange("(d a) -> d a", a=1)).then_inc(wr_in, 16)
            act.wait_ge(vec_in, 16 * 5)
            link(act.activation(cvec[:, :, :], cvec[:, :, :], ACT.Silu), silu_c)
            act.wait_ge(x_in, 32)
            for i in range(CT + TT):
                row = cr[:, i, :] if i < CT else xr[:, i - CT, :]
                link(act.activation(junk, row, ACT.Square, accum_out=ssq[:, i:i + 1]), ssq_done)
            act.wait_ge(ms_done, 1)
            link(act.activation(rms[:, 0:6], rms_t[:, 0:6], ACT.Sqrt), root_done)
            act.wait_ge(acol_done, 2)
            for g in range(2 * DC):
                act.wait_ge(xT_done, g + 1)
                c = g % DC
                if g < DC:
                    link(act.activation(hcT[:, c, :], bank[4 + g % 4][:, 0:CTX], ACT.Identity,
                                        scale=acol[:, 1, c:c + 1], bias=mcol_c[:, 0, c:c + 1]), hT_done)
                else:
                    link(act.activation(hT[:, c, :], bank[4 + g % 4][:, :], ACT.Identity,
                                        scale=acol[:, 0, c:c + 1], bias=mcol[:, 0, c:c + 1]), hT_done)
            for cc in range(CC):
                act.wait_ge(glu_done, cc + 1)
                if cc >= 2:
                    act.wait_ge(u_done, cc - 1)
                link(act.activation(sig[cc % 2], bank[2 * (cc % 2) + 1][:, :], ACT.Sigmoid), sig_done)
            act.wait_ge(mod_out, 16 * 4)
            for m in range(18):
                act.wait_ge(proj_done, m + 1)
                src = bank[4 + m % 4]
                if m < 4:
                    link(act.activation(kT[:, m, :], src[:, :], ACT.Copy), proj_out)
                elif m < 8:
                    link(act.activation(kcT[:, m - 4, :], src[:, 0:CTX], ACT.Copy), proj_out)
                elif m < 10:
                    link(act.activation(vcrow[:, m - 8, :], src[:, :], ACT.Copy), proj_out)
                elif m < 14:
                    link(act.activation(vrow[:, m - 10, :], src[:, :], ACT.Copy), proj_out)
                else:
                    link(act.activation(qT[:, m - 14, :], src[:, :], ACT.Copy, scale=HD ** -0.5), proj_out)
                if m == 9:
                    for i, b in enumerate((A["b_mod"][4 * T:8 * T], A["b_mod"][8 * T:12 * T], A["b_ada_2"][0:4 * T])):
                        act.dma_start(mod_bias[i][0:P:32, :], b.rearrange("(j n) -> j n", n=T)).then_inc(modb2_in, 16)

            def conv_squares():
                act.wait_ge(ccen_done, CC)
                for cc in range(CC):
                    link(act.activation(conv_sq[:, cc, :], conv[:, cc, :], ACT.Square), csq_done)

            def conv_root():
                act.wait_ge(cms_done, 1)
                link(act.activation(conv_r, conv_t, ACT.Sqrt), croot_done)

            def conv_silu():
                for cc in range(CC):
                    act.wait_ge(cnorm_done, cc + 1)
                    link(act.activation(conv[:, cc, :], conv[:, cc, :], ACT.Silu, scale=convc[:, cc, CONV_W + 1:CONV_W + 2],
                                        bias=convc[:, cc, CONV_W + 2:CONV_W + 3]), convy_done)

            def probs_out(n):
                act.wait_ge(pT_done, n + 1)
                if n >= 2:
                    act.wait_ge(o_done, n - 1)
                link(act.activation(probT[n % 2][:, 0:4, :], bank[4][:, :].rearrange("p (a b) -> p a b", b=P), ACT.Copy), pTa_out)

                link(act.activation(probT[n % 2][:, 4:6, :], bank[5][:, 0:2 * P].rearrange("p (a b) -> p a b", b=P), ACT.Copy), pTb_out)

            def head_out(h):
                act.wait_ge(o_done, TT * (h + 1))
                at = slice(HD * (h % 2), HD * (h % 2) + HD)
                link(act.activation(attT[at, h // 2, :], bank[6][at, :], ACT.Copy), head_done)

            for n in range(H * TT):
                act.wait_ge(nmax_done, n + 1)
                link(act.activation(prob[n % 3][:, 0:T], prob[n % 3][:, 0:T], ACT.Exp, bias=smx[:, n % 3, 2:3],
                                    accum_out=ssum[:, 0, n:n + 1]))
                link(act.activation(prob[n % 3][:, T:KEYS], bank[2 + n % 2][:, 0:CTX], ACT.Exp, bias=smx[:, n % 3, 2:3],
                                    accum_out=ssum[:, 1, n:n + 1]), p_done)
                if n >= 2:
                    probs_out(n - 2)
                if n >= 3 and (n - 3) % TT == TT - 1:
                    head_out((n - 3) // TT)
                if n == AT_MEAN + 1:
                    conv_squares()
                if n == AT_VAR + 1:
                    conv_root()
                if n == AT_VAR + 2:
                    conv_silu()
            probs_out(H * TT - 2)
            probs_out(H * TT - 1)
            head_out(H - 1)
            for c in range(DC):
                act.wait_ge(merge_pe, c + 1)
                if c >= 2:
                    act.wait_ge(mix_done, c - 1)
                link(act.activation(gate_a[c % 2], bank[4 * (c % 2)][:, :], ACT.Sigmoid))
                link(act.activation(gate_c[c % 2], bank[4 * (c % 2) + 1][:, :], ACT.Sigmoid), gates_done)
            def second_norm(t, block, junk):
                act.wait_ge(res_done, 2 * (block * TT + t) + 2)
                link(act.activation(junk, xr[:, t, :], ACT.Square, accum_out=ssq[:, t:t + 1]), ssq_done)
                act.wait_ge(ms_done, MS_2ND[block] + t + 1)
                link(act.activation(rms[:, t:t + 1], rms_t[:, t:t + 1], ACT.Sqrt), root_done)

            def second_columns(t, block, columns, banks):
                act.wait_ge(h2T_pe, block * TT + t + 1)
                for i, b in enumerate(banks):
                    link(act.activation(columns[:, 4 * i:4 * i + 4, :], bank[b][:, :].rearrange("p (a b) -> p a b", b=P), ACT.Copy), h2T_done)

            for t in range(TT):
                second_norm(t, 0, junk2)
                second_columns(t, 0, h2T[:, :, t * P:(t + 1) * P], (2 * t, 2 * t + 1))
            act.wait_ge(gsub_done, 1)
            link(act.activation(gexp, gexp, ACT.Exp), gexp_done)
            act.wait_ge(gsub_done, 2)
            link(act.activation(dexp, dval, ACT.Exp), gexp_done)
            act.wait_ge(route_done, 2)
            for m in range(4):
                act.wait_ge(skT_pe, m + 1)
                link(act.activation(skT[:, 2 * m:2 * m + 2, :], bank[SK_BANKS[m]][:, :].rearrange("p (a b) -> p a b", a=2), ACT.Copy), skT_done)
            link(act.activation(skT[:, H, :], bank[SK_BANKS[0]][:, 0:2 * P], ACT.Copy), skT_done)

            def expert(e, b, i):
                act.wait_ge(xbT_done, e + 1)
                unless_first(act, gu_done, e - 1)
                act.activation(xbT[b], bank[b][:, :].rearrange("p (a c) -> p a c", c=CAP), ACT.Copy).then_inc(xbT_out, 1)
                act.wait_ge(gu_done, e + 1)
                unless_first(act, hid_done, e - 1)
                act.activation(silu_g[b], bank[2 + b][:, 0:256], ACT.Silu).then_inc(silu_done, 1)
                act.wait_ge(dn_done, e + 1)
                unless_first(act, y_dma[b], i * 32)
                act.activation(yblk[b], bank[6 + b][:, :], ACT.Copy).then_inc(yv_done, 1)
                act.wait_ge(yv_done, e + 1)
                for half in range(2):
                    act.dma_start(ys_d[bass.ds(e * CAP, CAP), 512 * half:512 * half + 512],
                                  yblk[b][CAP * half:CAP * half + CAP, :]).then_inc(y_dma[b], 16)

            for b in range(2):
                expert(b, b, 0)
            with act.Fori(1, NE // 2) as i:
                for b in range(2):
                    expert(i * 2 + b, b, i)
            act.wait_ge(route_done, 2)
            n_over = act.value_load(over_i[0:1, 0:1], min_val=0, max_val=OVER)
            with act.Fori(0, OVER) as i:
                with act.If(i < n_over):
                    act.wait_ge(xbT_done, i + (NE + 1))
                    act.activation(xbT[0], bank[0][:, :].rearrange("p (a c) -> p a c", c=CAP), ACT.Copy).then_inc(xbT_out, 1)
                    act.wait_ge(gu_done, i + (NE + 1))
                    act.activation(silu_g[0], bank[2][:, 0:256], ACT.Silu).then_inc(silu_done, 1)
                    act.wait_ge(y_dma[0], 32 * (NE // 2))
                    act.wait_ge(dn_done, i + (NE + 1))
                    act.activation(yblk[0], bank[6][:, :], ACT.Copy).then_inc(yv_done, 1)
            def root(at, count):
                act.wait_ge(ms_done, MS_FINAL + count)
                link(act.activation(rms[:, at:at + 1], rms_t[:, at:at + 1], ACT.Sqrt), root_done)

            def columns(t):
                for half in range(2):
                    act.wait_ge(xT_done, 2 * DC + 2 * t + half + 1)
                    for k in range(4):
                        c = 4 * half + k
                        link(act.activation(hT[:, c, t * P:(t + 1) * P], bank[2 * t + half][:, k * P:(k + 1) * P], ACT.Identity,
                                            scale=acol[:, 2, c:c + 1], bias=mcol_2[:, 0, c:c + 1]), hT_done)

            for n in range(TT + 3):
                if n < TT:
                    act.wait_ge(comb_done, n + 1)
                    link(act.activation(junk3, xr[:, n, :], ACT.Square, accum_out=ssq[:, n:n + 1]), ssq_done)
                if 1 <= n <= TT:
                    root(n - 1, final_at(n - 1))
                    act.wait_ge(x2_done, n)
                    link(act.activation(junk3, xr[:, n - 1, :], ACT.Square, accum_out=ssq[:, TT + n - 1:TT + n]), ssq_done)
                if 2 <= n <= TT + 1:
                    root(TT + n - 2, first_at(n - 2))
                if n == 2:
                    act.wait_ge(acol2_done, 1)
                if n >= 3:
                    columns(n - 3)
            def soft(x, done):
                link(act.activation(x, x, ACT.Exp))
                link(act.activation(x, x, ACT.Ln, bias=ones[:, 0:1]), done)

            def proj2_out(m):
                act.wait_ge(proj_done, 18 + m + 1)
                if m < PROJ_V:
                    dst, scale = (svr, fvr)[m % 2][:, m // 2, :], 1.0
                else:
                    dst, scale = ((sqT, HD ** -0.5), (skT_, 1.0), (fqT, HD ** -0.5), (fkT, 1.0))[(m - PROJ_V) // AC]
                    dst = dst[:, m % AC, :]
                link(act.activation(dst, bank[proj_bank(m)][:, :], ACT.Copy, scale=scale), proj_out)

            for m in range(PROJ_STICK):
                proj2_out(m)
                if m == PROJ_V:
                    act.wait_ge(f_dve, 1)
                    act.preload_act_table_set(EXP_LN)
                    soft(fabs, f_act)
            act.wait_ge(f_pe, 3)
            link(act.activation(fcumT, bank[6][0:H, :], ACT.Copy, scale=-1.0), f_act)

            def stick_soft(n):
                h, t, part = unit(n)
                w = (t + 1) * P
                x = stick_x[part][n % 3][:, 0:w]
                act.wait_ge(sbz_pe, n + 1)
                if n >= 3:
                    act.wait_ge(sbr_pe, n - 2)
                link(act.activation(x, stick_bank(n)[:, 0:w], ACT.Abs))
                link(act.activation(x, x, ACT.Exp, scale=-1.0))
                link(act.activation(x, x, ACT.Ln, bias=ones[:, 0:1]), sbl_done)

            def stick_exp(n):
                h, t, part = unit(n)
                y = stick_y[part][n % len(stick_y[part])][:, 0:(t + 1) * P]
                act.wait_ge(sbc_done, n + 1)
                link(act.activation(y, y, ACT.Exp), sbe_done)

            def stick_rows(n):
                h, t, part = unit(n)
                act.wait_ge(sbo_pe, n + 1)
                if part == 0:
                    link(act.activation(mixed[0][1][:, 0, :], bank[6][:, :], ACT.Copy), sbo_done)
                else:
                    link(act.activation(mixed[1][1][:, :, h * HD:(h + 1) * HD],
                                        bank[6][:, 0:3 * HD].rearrange("p (t d) -> p t d", d=HD), ACT.Copy), sbo_done)

            def stick_step(k, first):
                part = int(first > 0)
                if part == 1 and of_part(k - EXPS[1], first):
                    stick_exp(k - EXPS[1])
                if of_part(k, first):
                    stick_soft(k)
                if part == 0 and of_part(k - EXPS[0], first):
                    stick_exp(k - EXPS[0])
                if of_part(k - OUTS[part], first) and last_of_head(k - OUTS[part]):
                    stick_rows(k - OUTS[part])

            def fox_exp(n):
                h, t, part = unit(n)
                w = (t + 1) * P
                act.wait_ge(nmax_done, H * TT + n + 1)
                if n >= 3:
                    act.wait_ge(pT_done, H * TT + n - 2)
                link(act.activation(fprob[part][n % 3][:, 0:w], bank[1 + n % 3][:, 0:w], ACT.Exp, bias=smx[:, n % 3, 2:3],
                                    accum_out=ssum[:, 0, n:n + 1]), p_done)

            def fox_T(n):
                h, t, part = unit(n)
                w = (t + 1) * P
                act.wait_ge(pT_done, H * TT + n + 1)
                if n >= 2:
                    act.wait_ge(o_done, H * TT + n - 1)
                link(act.activation(fprobT[part][n % 2][:, 0:w], bank[6][:, 0:w], ACT.Copy), pTa_out)

            def fox_step(k, first):
                part = int(first > 0)
                if of_part(k - FOX_EXP[part], first):
                    fox_exp(k - FOX_EXP[part])
                if of_part(k - FOX_T[part], first):
                    fox_T(k - FOX_T[part])

            def out_norm(part):
                act.wait_ge(att_done, 1 + H * part)
                for half in range(2):
                    at = slice(half * NT[part] * H, (half + 1) * NT[part] * H)
                    link(act.activation(msq[part][:, at, :], mixed_heads[part][:, at, :], ACT.Square), msq_done)
                act.wait_ge(mms_done, 2 * part + 2)
                link(act.activation(mrt[part], mss[part], ACT.Sqrt), mroot_done)

            for k in range(H + 3):
                stick_step(k, 0)
                if PROJ_STICK + k < PROJS:
                    proj2_out(PROJ_STICK + k)
            act.wait_ge(wr_in, 16 * 10)
            for n in range(H + 3):
                fox_step(n, 0)
            out_norm(0)
            for half in range(2):
                act.wait_ge(attT_pe, half + 1)
                link(act.activation(mixT2[0][:, 4 * half:4 * half + 4, :], bank[1 + half][:, :].rearrange("p (a b) -> p a b", b=P),
                                    ACT.Copy, scale=gob[:, half:half + 1]), attT_done)
            second_norm(0, 1, rows_2[0][3])
            second_columns(0, 1, h2T_2[0], H2T_BANKS[0])

            def query_out(m):
                act.wait_ge(q_pe, m + 1)
                link(act.activation(qT2_a[:, 2 * m:2 * m + 2, :], bank[(1, 2, 3, 6)[m]][:, :].rearrange("p (a b) -> p a b", a=2), ACT.Copy), q_done)

            def query_out_b(h):
                for half in range(2):
                    m = 2 * h + half
                    act.wait_ge(q_pe, 4 + m + 1)
                    dst = qT2_b.rearrange("p (t h) n -> p t h n", h=H)[:, :, h, P * half:P * half + P]
                    link(act.activation(dst, bank[1 + m % 3][:, 0:3 * P].rearrange("p (a b) -> p a b", b=P), ACT.Copy), q_done)

            def attend(s):
                if s < ST_FOX:
                    stick_step(H + s, H)
                elif s < ST_NORM:
                    fox_step(H + s - ST_FOX, H)
                elif s == ST_NORM:
                    out_norm(1)
                elif s < ST_OUT:
                    for k in range(DC):
                        act.wait_ge(attT_pe, 2 + k + 1)
                        link(act.activation(mixT2[1][:, k, :], bank[(1, 2, 3, 6, 7)[k % 5]][:, 0:3 * P], ACT.Copy,
                                            scale=gob[:, k // AC:k // AC + 1]), attT_done)
                elif s < ST_QUERY:
                    t = s - ST_OUT
                    if 1 <= t < TT:
                        second_norm(t, 1, rows_2[1][3])
                    for u in {4: (1,), 5: (2, 3)}.get(t, ()):
                        second_columns(u, 1, h2T_2[1][:, :, (u - 1) * P:u * P], H2T_BANKS[u])
                else:
                    query_out_b(s - ST_QUERY)

            def queries(n):
                i, off = n
                if off > 0:
                    act.wait_ge(sc_pe, at_head(n, 1, 0))
                    act.sem_inc(mark, 1)
                if i is None:
                    src = qT2_a[:, off, :] if off < H else qT2_b[:, off - H, :]
                else:
                    src = qT2_b[:, bass.ds(i * 2 + (off - H), 1), :].rearrange("p a b -> p (a b)")
                act.activation(qh.rearrange("p a b -> p (a b)"), src, ACT.Copy).then_inc(qh_done, 1)

            def gate_exp(n):
                act.wait_ge(gsub2_done, at_head(n, 1, 1))
                act.activation(gex, gsub, ACT.Exp, accum_out=gsum).then_inc(gex_done, 1)

            def gelu(n, g):
                act.wait_ge(down_free, at_head(n, GROUPS, DOWN_SETS + g + 1))
                act.activation(gel[:, G4 * g:G4 * g + G4], dots[:, G4 * g:G4 * g + G4], ACT.Gelu).then_inc(gelu_done, 1)

            def diagonals(n, g):
                if n[1] > 0:
                    act.wait_ge(up_free, up_used(n, g - GROUPS))
                act.wait_ge(coef_done, at_head(n, GROUPS, g + 1))
                for r in range(G4 * g, G4 * g + G4):
                    d = act.activation(diag[:, r, :], ident[:, :], ACT.Copy, scale=coef[:, r:r + 1])
                d.then_inc(diag_done, 1)

            def peer_head(n, more, query=None):
                nxt = (n[0], n[1] + 1)
                if query is not None:
                    query_out_b(query)
                if more:
                    queries(nxt)
                gelu(n, 0)
                gelu(n, 1)
                diagonals(n, 0)
                if more:
                    gate_exp(nxt)
                gelu(n, 2)
                diagonals(n, 1)
                gelu(n, 3)
                diagonals(n, 2)
                diagonals(n, 3)

            def peer_part(h, part):
                n, nxt = (None, h), (None, h + 1)
                if part == 2:
                    queries(nxt)
                    gelu(n, 0)
                    gelu(n, 1)
                elif part == 4:
                    gelu(n, 2)
                    gelu(n, 3)
                    diagonals(n, 0)
                    diagonals(n, 1)
                elif part == 6:
                    gate_exp(nxt)
                elif part == 7:
                    diagonals(n, 2)
                    diagonals(n, 3)
                if part in (2, 4) and any(s < ST_FOX for parts in PLAN[h:] for steps in parts for s in steps):
                    act.preload_act_table_set(EXP_LN)

            def last_norm(t):
                act.wait_ge(fin_add, t + 1)
                link(act.activation(h2r_2[t], xr[:, t, :], ACT.Square, accum_out=ssq[:, t:t + 1]), ssq_done)
                act.wait_ge(ms_done, MS_LAST + t + 1)
                link(act.activation(rms[:, t:t + 1], rms_t[:, t:t + 1], ACT.Sqrt), root_done)

            query_out(0)
            queries((None, 0))
            for m in range(1, 4):
                query_out(m)
            act.preload_act_table_set(EXP_LN)
            gate_exp((None, 0))
            for s in range(LEAD):
                attend(s)
            for h in range(H):
                for part in range(PARTS):
                    peer_part(h, part)
                    for s in PLAN[h][part]:
                        attend(s)
            for h in range(H):
                peer_head((None, H + h), True, h + AHEAD - 1 if h >= 1 and h + AHEAD - 1 < H else None)
            last_norm(0)
            for t in range(2, TT):
                last = t == TT - 1
                with act.Fori(0, H // 2 - last) as i:
                    for b in range(2):
                        peer_head((i, t * H + b), True)
                if last:
                    peer_head((None, TT * H - 2), True)
                    peer_head((None, TT * H - 1), False)
                last_norm(t - 1)
            last_norm(TT - 1)

        @block.vector
        def _(dve):
            link = Link(dve, dve_step)

            def inv_root(n, root, last=None):
                dve.wait_ge(*root)
                r, v, s = n
                link(dve.reciprocal(r, r))
                link(dve.tensor_tensor(s, r, r, ALU.mult))
                link(dve.tensor_tensor(s, s, v, ALU.mult))
                link(dve.tensor_scalar(s, s, -0.5, 1.5, ALU.mult, ALU.add))
                link(dve.tensor_tensor(r, r, s, ALU.mult), last)

            dve.wait_ge(consts, 1)
            link(dve.tensor_copy(iota[:, :], iota_i[:, :]))
            link(dve.tensor_copy(wstart[:, 0:1], part_i[:, :]))
            link(dve.tensor_scalar(wstart[:, 1:2], wstart[:, 0:1], float(GRID_W), -float(GRID_W), ALU.is_ge, ALU.mult))
            link(dve.tensor_tensor(wstart[:, 0:1], wstart[:, 0:1], wstart[:, 1:2], ALU.add))
            link(dve.tensor_scalar(wstart[:, 2:3], wstart[:, 0:1], -float(WIN // 2), 0.0, ALU.add, ALU.max))
            link(dve.tensor_scalar(wstart[:, 2:3], wstart[:, 2:3], float(GRID_W - WIN), None, ALU.min))
            link(dve.tensor_scalar(wstart[:, 3:4], wstart[:, 2:3], float(WIN), None, ALU.add))
            link(dve.tensor_scalar(band_t[:, 0, :], iota[:, :], wstart[:, 2:3], None, ALU.is_ge))
            link(dve.tensor_scalar(band_t[:, 1, :], iota[:, :], wstart[:, 3:4], None, ALU.is_lt))
            link(dve.tensor_tensor(band[:, :], band_t[:, 0, :], band_t[:, 1, :], ALU.mult))
            link(dve.tensor_scalar(band[:, :], band[:, :], -NEG, NEG, ALU.mult, ALU.add))

            link(dve.tensor_scalar(stick_neg, before[:, :], 1.0, -NEG, ALU.subtract, ALU.mult))

            dve.wait_ge(modb_in, 32)
            dve.wait_ge(pe_mod, 1)
            for j in range(4):
                at = slice(32 * j, 32 * j + 2)
                link(dve.tensor_tensor(modr[at, :], bank[0][at, :], modb[at, :], ALU.add), mod_rows)
            dve.wait_ge(ssq_done, CT + TT)
            link(dve.tensor_scalar(rms_t[:, 0:6], ssq[:, 0:6], 1.0 / D, EPS, ALU.mult, ALU.add), ms_done)
            inv_root((rms[:, 0:6], rms_t[:, 0:6], ssq[:, 0:6]), (root_done, 1))
            for i in range(CT + TT):
                row = cr[:, i, :] if i < CT else xr[:, i - CT, :]
                link(dve.tensor_scalar(row, row, rms[:, i:i + 1], None, ALU.mult), xn_done)

            dve.wait_ge(mcol_in, 32)
            for i, m in enumerate((mcol, mcol_c)):
                link(dve.scalar_tensor_tensor(out=acol[:, i, :], in0=m[:, 1, :], scalar=1.0, in1=gcol[:, 0, :],
                                              op0=ALU.add, op1=ALU.mult), acol_done)

            def job_rows(i):
                dve.wait_ge(pe_mod, 2 + i)
                if i in (0, 2):
                    dve.wait_ge(modb2_in, 16 * 3)
                if i == 3:
                    dve.wait_ge(modb3_in, 16 * 2)
                if i >= 1:
                    dve.wait_ge(*((mod_out_rest, 64 * i) if i <= 2 else (mod2_out, 64 * (i - 2))))
                for j in range(4):
                    at = slice(32 * j, 32 * j + 1)
                    link(dve.tensor_tensor(mod_row[at, :], bank[7 if i else 0][at, :], mod_bias[i % 3][at, :], ALU.add), mod_rows)

            dve.wait_ge(convw_T, CC)
            link(dve.tensor_copy(convc[:, :, :], bank[3][:, 0:CC * 34].rearrange("p (a b) -> p a b", b=34)), convc_done)
            dve.wait_ge(xT_done, 2 * DC)
            link(dve.memset(u_pad[:, :, 0:PADC], 0.0))
            link(dve.memset(u_pad[:, :, PADC + T:UW], 0.0))
            for cc in range(CC):
                dve.wait_ge(sig_done, cc + 1)
                link(dve.tensor_tensor(u_pad[:, cc, PADC:PADC + T], bank[2 * (cc % 2)][:, :], sig[cc % 2], ALU.mult), u_done)
            for cc in range(CC):
                link(dve.tensor_scalar(conv[:, cc, :], u_pad[:, cc, 0:T], convc[:, cc, 0:1], convc[:, cc, CONV_W:CONV_W + 1],
                                       ALU.mult, ALU.add))
                for k in range(1, CONV_W):
                    link(dve.scalar_tensor_tensor(out=conv[:, cc, :], in0=u_pad[:, cc, k:k + T], scalar=convc[:, cc, k:k + 1],
                                                  in1=conv[:, cc, :], op0=ALU.mult, op1=ALU.add),
                         conv_done if k == CONV_W - 1 else None)
            job_rows(0)
            def conv_centre():
                dve.wait_ge(cmean_done, 1)
                for cc in range(CC):
                    link(dve.tensor_tensor(conv[:, cc, :], conv[:, cc, :], bank[7][:, :], ALU.subtract), ccen_done)

            def conv_var():
                dve.wait_ge(cvar_done, 1)
                link(dve.tensor_scalar(conv_t, bank[7][:, :], EPS, None, ALU.add), cms_done)

            def conv_norm():
                inv_root((conv_r, conv_t, conv_s), (croot_done, 1))
                for cc in range(CC):
                    link(dve.tensor_tensor(conv[:, cc, :], conv[:, cc, :], conv_r, ALU.mult), cnorm_done)

            def normalise(n):
                dve.wait_ge(p_done, n + 1)
                one = slice(n % 2, n % 2 + 1)
                link(dve.tensor_tensor(rinv[:, one], ssum[:, 0, n:n + 1], ssum[:, 1, n:n + 1], ALU.add))
                link(dve.reciprocal(rinv[:, one], rinv[:, one]))
                link(dve.tensor_scalar(prob[n % 3], prob[n % 3], rinv[:, one], None, ALU.mult), pn_done)

            for n in range(H * TT):
                h, t = n // TT, n % TT
                if t == 0:
                    dve.wait_ge(bias_in[h % 2], 32 * (h // 2 + 1))
                    link(dve.tensor_tensor(bias[h % 2], bias[h % 2], band[:, :].unsqueeze(1).broadcast_to([P, 14, 64]), ALU.add))
                dve.wait_ge(s_done, n + 1)
                if n >= 3:
                    dve.wait_ge(pT_done, n - 2)
                at = 6 - 2 * t
                link(dve.tensor_tensor_reduce(prob[n % 3][:, 0:T], bank[n % 2][:, :], bias[h % 2][:, at:at + ROWS, :].rearrange("p a b -> p (a b)"),
                                              1.0, NEG, ALU.add, ALU.max, smx[:, n % 3, 0:1]))
                link(dve.tensor_reduce(smx[:, n % 3, 1:2], bank[2 + n % 2][:, 0:CTX], AX, ALU.max))
                link(dve.tensor_scalar(smx[:, n % 3, 2:3], smx[:, n % 3, 0:1], smx[:, n % 3, 1:2], -1.0, ALU.max, ALU.mult), nmax_done)
                if n >= 1:
                    normalise(n - 1)
                if n == AT_MEAN + 1:
                    conv_centre()
                if n == AT_VAR + 1:
                    conv_var()
                if n == AT_VAR + 2:
                    conv_norm()
                if n - 1 in AT_JOB:
                    job_rows(1 + AT_JOB.index(n - 1))
            normalise(H * TT - 1)
            for c in range(DC):
                dve.wait_ge(gates_done, c + 1)
                b = 4 * (c % 2)
                link(dve.tensor_tensor(gate_a[c % 2], bank[b + 2][:, :], gate_a[c % 2], ALU.mult))
                link(dve.tensor_tensor(gate_c[c % 2], bank[b + 3][:, :], gate_c[c % 2], ALU.mult))
                link(dve.tensor_tensor(mixT[:, c, :], gate_a[c % 2], gate_c[c % 2], ALU.add), mix_done)
            dve.wait_ge(rows_in, 16 * 5)
            link(dve.scalar_tensor_tensor(out=a2_b, in0=a2_b, scalar=1.0, in1=tmp2, op0=ALU.add, op1=ALU.mult))
            def second_norm(t, block, g1, a2, sh2, h2, tmp, banks):
                n = block * TT + t
                for j in range(2):
                    at = slice(j * 512, j * 512 + 512)
                    dve.wait_ge(wo_pe, 2 * n + j + 1)
                    link(dve.tensor_tensor(tmp, bank[banks[j]][:, :], g1[:, at], ALU.mult))
                    link(dve.tensor_tensor(xr[:, t, at], xr[:, t, at], tmp, ALU.add), res_done)
                dve.wait_ge(ssq_done, SQ_2ND[block] + t + 1)
                one = slice(t, t + 1)
                link(dve.tensor_scalar(rms_t[:, one], ssq[:, one], 1.0 / D, EPS, ALU.mult, ALU.add), ms_done)
                inv_root((rms[:, one], rms_t[:, one], ssq[:, one]), (root_done, MS_2ND[block] + t + 1))
                link(dve.tensor_scalar(h2, xr[:, t, :], rms[:, one], None, ALU.mult))
                link(dve.tensor_tensor(h2, h2, a2, ALU.mult))
                link(dve.tensor_tensor(h2, h2, sh2, ALU.add), h2_done)

            dve.wait_ge(xres_in, 16)
            dve.wait_ge(mod2_out, 16 * 12)
            for t in range(TT):
                second_norm(t, 0, g1_b, a2_b, sh2_b, h2r[:, t, :], tmp[:, 0:512], (2 * t, 2 * t + 1))
            link(dve.memset(lgp, NEG))
            for t in range(TT):
                dve.wait_ge(logit_pe, t + 1)
                link(dve.tensor_tensor(lg[:, t, :], bank[2 * t][:, 0:NG + NE], br[:, :], ALU.add))
            link(dve.tensor_copy(lgp[:, :, 0:NG], lg[:, :, 0:NG]))
            for t in range(TT):
                link(dve.max(gval[:, t, :], lgp[:, t, :]))
                link(dve.max_index(ridx[:, 0, t, :], gval[:, t, :], lgp[:, t, :]))
            link(dve.tensor_tensor(gexp, lg[:, :, 0:NG], gval[:, :, 0:1].broadcast_to([P, TT, NG]), ALU.subtract), gsub_done)
            link(dve.tensor_copy(gif, ridx[:, 0, :, 0]))
            link(dve.tensor_tensor(oneh, iota[:, 0:NG].unsqueeze(1).broadcast_to([P, TT, NG]),
                                   gif.unsqueeze(2).broadcast_to([P, TT, NG]), ALU.is_equal))
            link(dve.tensor_scalar(pen, oneh, 1.0, -NEG, ALU.subtract, ALU.mult))
            em = emask.rearrange("p t (g e) -> p t g e", e=EPG)
            link(dve.tensor_tensor(em, lg[:, :, NG:NG + NE].rearrange("p t (g e) -> p t g e", e=EPG),
                                   oneh.unsqueeze(3).broadcast_to([P, TT, NG, EPG]), ALU.mult))
            link(dve.tensor_tensor(em, em, pen.unsqueeze(3).broadcast_to([P, TT, NG, EPG]), ALU.add))
            for t in range(TT):
                link(dve.max(eval_[:, t, :], emask[:, t, :]))
                link(dve.max_index(ridx[:, 1, t, :], eval_[:, t, :], emask[:, t, :]))
            link(dve.tensor_tensor(dval, eval_[:, :, 1], eval_[:, :, 0], ALU.subtract), gsub_done)
            link(dve.tensor_copy(eif, ridx[:, 1, :, 0:2]))
            for s in range(2):
                link(dve.tensor_tensor(pick[:, s, :, :], iota[:, 0:NE].unsqueeze(1).broadcast_to([P, TT, NE]),
                                       eif[:, :, s:s + 1].broadcast_to([P, TT, NE]), ALU.is_equal))
            link(dve.tensor_tensor(both, pick[:, 0, :, :], pick[:, 1, :, :], ALU.add), both_done)
            dve.wait_ge(rank_pe, 1)
            link(dve.tensor_copy(rank, bank[1][:, 0:TT * NE].rearrange("p (t e) -> p t e", e=NE)))
            link(dve.tensor_copy(cnt, bank[1][:, TT * NE:TT * NE + NE]))
            link(dve.tensor_scalar(nblk, cnt, float(CAP), None, ALU.is_gt))
            for k in range(2, T // CAP):
                link(dve.scalar_tensor_tensor(out=nblk, in0=cnt, scalar=float(CAP * k), in1=nblk, op0=ALU.is_gt, op1=ALU.add))
            a, b = incl, incl2
            link(dve.tensor_copy(a, nblk))
            for sh in (1, 2, 4, 8, 16):
                link(dve.tensor_copy(b[:, 0:sh], a[:, 0:sh]))
                link(dve.tensor_tensor(b[:, sh:NE], a[:, sh:NE], a[:, 0:NE - sh], ALU.add))
                a, b = b, a
            total = a
            link(dve.tensor_scalar(e64, iota[:, 0:NE], float(CAP), None, ALU.mult))
            link(dve.tensor_tensor(delta, total, nblk, ALU.subtract))
            link(dve.tensor_scalar(delta, delta, float(CAP), float(NE * CAP - CAP), ALU.mult, ALU.add))
            link(dve.tensor_tensor(delta, delta, e64, ALU.subtract))
            link(dve.tensor_scalar(over_at, rank, float(CAP), None, ALU.is_ge))
            link(dve.tensor_tensor(over_at, over_at, delta.unsqueeze(1).broadcast_to([P, TT, NE]), ALU.mult))
            link(dve.tensor_tensor(over_at, over_at, rank, ALU.add))
            link(dve.tensor_tensor(over_at, over_at, e64.unsqueeze(1).broadcast_to([P, TT, NE]), ALU.add))
            for s in range(2):
                link(dve.tensor_tensor(sel, pick[:, s, :, :], over_at, ALU.mult))
                link(dve.tensor_reduce(slot_f[:, s, :], sel, AX, ALU.add))
            link(dve.tensor_copy(slot_i[:, :, :], slot_f), route_done)
            dve.wait_ge(gexp_done, 1)
            link(dve.tensor_reduce(psum_, gexp, AX, ALU.add))
            link(dve.reciprocal(psum_, psum_))
            dve.wait_ge(gexp_done, 2)
            link(dve.tensor_scalar(dden, dexp, 1.0, None, ALU.add))
            link(dve.reciprocal(dden, dden))
            link(dve.tensor_tensor(gw[:, 0, :], dden, psum_, ALU.mult))
            link(dve.tensor_tensor(gw[:, 1, :], gw[:, 0, :], dexp, ALU.mult))
            link(dve.tensor_tensor(tab, total.unsqueeze(1).broadcast_to([P, OVER, NE]),
                                   iota[:, 0:OVER].unsqueeze(2).broadcast_to([P, OVER, NE]), ALU.is_le))
            link(dve.tensor_reduce(tab_e, tab, AX, ALU.add))
            link(dve.tensor_scalar(tab_e, tab_e, float(NE - 1), None, ALU.min))
            link(dve.tensor_copy(over_i[:, 1:1 + OVER], tab_e))
            link(dve.tensor_copy(over_i[:, 0:1], total[:, NE - 1:NE]), route_done)

            def expert(e, b):
                dve.wait_ge(silu_done, e + 1)
                unless_first(dve, hidT_pe, e - 1)
                dve.tensor_tensor(hid[b], silu_g[b], bank[2 + b][:, 256:512], ALU.mult).then_inc(hid_done, 1)
                dve.wait_ge(hidT_pe, e + 1)
                unless_first(dve, dn_done, e - 1)
                dve.tensor_copy(hidT[b], bank[4 + b][:, 0:256].rearrange("p (k r) -> p k r", k=2)).then_inc(hidT_done, 1)

            for b in range(2):
                expert(b, b)
            with dve.Fori(1, NE // 2) as i:
                for b in range(2):
                    expert(i * 2 + b, b)
            n_over = dve.value_load(over_i[0:1, 0:1], min_val=0, max_val=OVER)
            with dve.Fori(0, OVER) as i:
                with dve.If(i < n_over):
                    dve.wait_ge(silu_done, i + (NE + 1))
                    dve.tensor_tensor(hid[0], silu_g[0], bank[2][:, 256:512], ALU.mult).then_inc(hid_done, 1)
                    dve.wait_ge(hidT_pe, i + (NE + 1))
                    dve.tensor_copy(hidT[0], bank[4][:, 0:256].rearrange("p (k r) -> p k r", k=2)).then_inc(hidT_done, 1)
            dve.wait_ge(mcol2_in, 16)
            link(dve.scalar_tensor_tensor(out=acol[:, 2, :], in0=mcol_2[:, 1, :], scalar=1.0, in1=gcol[:, 1, :],
                                          op0=ALU.add, op1=ALU.mult), acol2_done)
            def combine(t):
                dve.wait_ge(yg_in[t], 32)
                y0, y1 = ygat[t % 2]
                link(dve.tensor_scalar(y0, y0, gw[:, 0, t:t + 1], None, ALU.mult))
                link(dve.scalar_tensor_tensor(out=y0, in0=y1, scalar=gw[:, 1, t:t + 1], in1=y0, op0=ALU.mult, op1=ALU.add))
                link(dve.tensor_tensor(y0, y0, g2_b, ALU.mult))
                link(dve.tensor_tensor(xr[:, t, :], xr[:, t, :], y0, ALU.add), comb_done)

            def inv_rms(at, count):
                one = slice(at, at + 1)
                dve.wait_ge(ssq_done, SQ_FINAL + count)
                link(dve.tensor_scalar(rms_t[:, one], ssq[:, one], 1.0 / D, EPS, ALU.mult, ALU.add), ms_done)
                inv_root((rms[:, one], rms_t[:, one], ssq[:, one]), (root_done, MS_FINAL + count))

            for n in range(TT + 2):
                if n < TT:
                    combine(n)
                if 1 <= n <= TT:
                    inv_rms(n - 1, final_at(n - 1))
                    if n == 1:
                        dve.wait_ge(fn_in, 16)
                    link(dve.scalar_tensor_tensor(out=xr[:, n - 1, :], in0=xr[:, n - 1, :], scalar=rms[:, n - 1:n], in1=fn_b,
                                                  op0=ALU.mult, op1=ALU.mult), x2_done)
                if n >= 2:
                    inv_rms(TT + n - 2, first_at(n - 2))
                    link(dve.tensor_scalar(xnb[:, n - 2, :], xr[:, n - 2, :], rms[:, TT + n - 2:TT + n - 1], None, ALU.mult), xnb_done)
            dve.wait_ge(f_pe, 1)
            dve.wait_ge(wr_in, 16 * 10)
            link(dve.tensor_tensor(flog, bank[6][:, 0:TT * H].rearrange("p (t h) -> p t h", h=H),
                                   bf[:, :].unsqueeze(1).broadcast_to([P, TT, H]), ALU.add))
            link(dve.scalar_tensor_tensor(out=fabs, in0=flog, scalar=-1.0, in1=flog, op0=ALU.mult, op1=ALU.min), f_dve)
            dve.wait_ge(f_act, 1)
            link(dve.scalar_tensor_tensor(out=flog, in0=flog, scalar=0.0, in1=fabs, op0=ALU.min, op1=ALU.subtract), f_dve)
            dve.wait_ge(f_pe, 2)
            link(dve.tensor_copy(fcum, bank[7][:, 0:TT * H].rearrange("p (t h) -> p t h", h=H)), f_dve)

            def stick_beta(n):
                h, t, part = unit(n)
                w = (t + 1) * P
                x, y, z = stick_x[part][n % 3], stick_y[part][n % len(stick_y[part])], stick_bank(n)
                dve.wait_ge(sbl_done, n + 1)
                if n >= len(stick_y[part]):
                    dve.wait_ge(sbo_pe, n + 1 - len(stick_y[part]))
                link(dve.scalar_tensor_tensor(out=x[:, 0:w], in0=z[:, 0:w], scalar=0.0, in1=x[:, 0:w], op0=ALU.max, op1=ALU.add))
                link(dve.tensor_tensor(y[:, 0:w], z[:, 0:w], x[:, 0:w], ALU.subtract))
                link(dve.tensor_tensor(x[:, t * P:w], x[:, t * P:w], before[:, :], ALU.mult), sbb_done)

            def stick_rest(n):
                h, t, part = unit(n)
                w = (t + 1) * P
                y = stick_y[part][n % len(stick_y[part])][:, 0:w]
                dve.wait_ge(sbr_pe, n + 1)
                link(dve.tensor_tensor(y, stick_bank(n)[:, 0:w], y, ALU.add), sbc_done)

            def stick_step(k, first):
                part = int(first > 0)
                if of_part(k - REST[part], first):
                    stick_rest(k - REST[part])
                if of_part(k - BETA[part], first):
                    stick_beta(k - BETA[part])

            def fox_max(n):
                w = (unit(n)[1] + 1) * P
                dve.wait_ge(s_done, H * TT + n + 1)
                if n >= 3:
                    dve.wait_ge(p_done, H * TT + n - 2)
                link(dve.tensor_reduce(smx[:, n % 3, 0:1], bank[1 + n % 3][:, 0:w], AX, ALU.max))
                link(dve.tensor_scalar(smx[:, n % 3, 2:3], smx[:, n % 3, 0:1], -1.0, None, ALU.mult), nmax_done)

            def fox_out(n):
                h, t, part = unit(n)
                c = H if part == 0 else 3
                dve.wait_ge(o_done, H * TT + n + 1)
                link(dve.reciprocal(rinv[:, 0:c], ssum[:, 0, n + 1 - c:n + 1]))
                dst = mixed[0][0].rearrange("p t (h d) -> p (t h) d", d=HD) if part == 0 else mixed[1][0][:, :, h * HD:(h + 1) * HD]
                link(dve.tensor_tensor(dst, bank[7][:, 0:c * HD].rearrange("p (t d) -> p t d", d=HD),
                                       rinv[:, 0:c].unsqueeze(2).broadcast_to([P, c, HD]), ALU.mult), att_done)

            def fox_step(k, first):
                part = int(first > 0)
                if of_part(k, first):
                    fox_max(k)
                if of_part(k - FOX_OUT[part], first) and last_of_head(k - FOX_OUT[part]):
                    fox_out(k - FOX_OUT[part])

            def out_norm(part):
                dve.wait_ge(msq_done, 2 * part + 2)
                link(dve.tensor_reduce(mss[part], msq[part], AX, ALU.add), mms_done)
                link(dve.tensor_scalar(mss[part], mss[part], 1.0 / HD, EPS, ALU.mult, ALU.add), mms_done)
                inv_root((mrt[part], mss[part], msc[part]), (mroot_done, part + 1))
                n = NT[part] * H
                for half in range(2):
                    m = mixed_heads[part][:, half * n:(half + 1) * n, :]
                    link(dve.tensor_tensor(m, m, mrt[part][:, half * n:(half + 1) * n].unsqueeze(2).broadcast_to([P, n, HD]), ALU.mult), mixed_done)

            def norm_gain(part):
                gt1, a2, sh2, nf = rows_2[part]
                dve.wait_ge(rows2_in, 16 * 4 * (part + 1))
                link(dve.scalar_tensor_tensor(out=a2, in0=a2, scalar=1.0, in1=nf, op0=ALU.add, op1=ALU.mult))

            def attend(s):
                if s < ST_FOX:
                    stick_step(H + s, H)
                elif s < ST_NORM:
                    fox_step(H + s - ST_FOX, H)
                elif s == ST_NORM:
                    out_norm(1)
                elif 1 <= s - ST_OUT < TT:
                    t = s - ST_OUT
                    if t == 1:
                        norm_gain(1)
                    second_norm(t, 1, *rows_2[1][0:3], h2r_2[t], tmp_2[1], WO_BANKS[t])

            for k in range(H + 3):
                stick_step(k, 0)
            for n in range(H + 3):
                fox_step(n, 0)
                if n == H // 2:
                    norm_gain(0)
            out_norm(0)
            second_norm(0, 1, *rows_2[0][0:3], h2r_2[0], tmp_2[0], WO_BANKS[0])

            TOPK_STEPS = 30

            def topk_step_of(n, k):
                def step(ins, hold=False):
                    nonlocal k
                    k += 1
                    ins.then_inc(topk_step, 1)
                    dve.wait_ge(topk_step, at_head(n, TOPK_STEPS, k))
                    if hold:
                        dve.sem_inc(mark, 1)

                def top16(val, idx, src, rest):
                    step(dve.max(val[:, 0:8], src), True)
                    step(dve.max_index(idx[:, 0:8], val[:, 0:8], src), True)
                    step(dve.match_replace(rest, val[:, 0:8], src, NEG), True)
                    step(dve.max(val[:, 8:16], rest), True)
                    step(dve.max_index(idx[:, 8:16], val[:, 8:16], rest), True)

                return step, top16

            def topk_halves(n):
                step, top16 = topk_step_of(n, 0)
                dve.wait_ge(sc_pe, at_head(n, 1, 1))
                dve.sem_inc(mark, 1)
                for p in range(2):
                    top16(hval[:, p, :], hidx[:, p, :], bank[0][:, p * P:(p + 1) * P], work[:, p, :])
                step(dve.tensor_copy(hidx_f, hidx[:, :, :]))
                step(dve.tensor_tensor(cand.rearrange("p (a b) -> p a b", b=K16), hval[:, 0, :].unsqueeze(2).broadcast_to([P, K16, K16]),
                                       hval[:, 1, :].unsqueeze(1).broadcast_to([P, K16, K16]), ALU.add), True)

            def topk_pairs(n, b):
                step, top16 = topk_step_of(n, 12)
                top16(top, pos, cand, cand2)
                step(dve.tensor_scalar(gsub, top, top[:, 0:1], None, ALU.subtract))
                step(dve.tensor_single_scalar(pos_hl[:, 0, :], pos[:, :], 4, ALU.logical_shift_right))
                step(dve.tensor_single_scalar(pos_hl[:, 1, :], pos[:, :], K16 - 1, ALU.bitwise_and))
                step(dve.tensor_copy(pos_f, pos_hl[:, :, :]))
                dve.sem_inc(gsub2_done, 1)
                for p in range(2):
                    step(dve.tensor_tensor(onehot, iota[:, 0:K16].unsqueeze(1).broadcast_to([P, K16, K16]),
                                           pos_f[:, p, :].unsqueeze(2).broadcast_to([P, K16, K16]), ALU.is_equal))
                    step(dve.tensor_tensor(onehot, onehot, hidx_f[:, p, :].unsqueeze(1).broadcast_to([P, K16, K16]), ALU.mult))
                    step(dve.tensor_reduce(half_i[:, p, :], onehot, AX, ALU.add))
                step(dve.scalar_tensor_tensor(out=id_f, in0=half_i[:, 0, :], scalar=float(P), in1=half_i[:, 1, :], op0=ALU.mult, op1=ALU.add))
                if n[1] >= 2:
                    dve.wait_ge(up_free, up_used(n, -GROUPS - 1))
                dve.tensor_copy(ids[b][:, :], id_f).then_inc(ids_done, 1)
            def gates(n, b):
                dve.wait_ge(gex_done, at_head(n, 1, 1))
                dve.reciprocal(gsum, gsum).then_inc(topk_step, 1)
                dve.wait_ge(topk_step, at_head(n, TOPK_STEPS, TOPK_STEPS - 1))
                dve.tensor_scalar(gate_p[b], gex, gsum, None, ALU.mult).then_inc(topk_step, 1)
                dve.wait_ge(topk_step, at_head(n, TOPK_STEPS, TOPK_STEPS))

            def dot(n, t, g):
                dve.wait_ge(down_in[g % DOWN_SETS], at_head(n, 16 * G4 * (GROUPS // DOWN_SETS), 16 * G4 * (g // DOWN_SETS + 1)))
                for k in range(G4):
                    r = G4 * g + k
                    buf = down[r % (G4 * DOWN_SETS)]
                    d = dve.tensor_tensor_reduce(buf, buf, h2r_2[t], 1.0, 0.0, ALU.mult, ALU.add, dots[:, r:r + 1])
                d.then_inc(down_free, 1)

            def gated(n, b, g):
                at = slice(G4 * g, G4 * g + G4)
                dve.wait_ge(gelu_done, at_head(n, GROUPS, g + 1))
                dve.tensor_tensor(coef[:, at], gel[:, at], gate_p[b][:, at], ALU.mult).then_inc(coef_done, 1)

            def peer_head(n, b, t, more):
                nxt = (n[0], n[1] + 1)
                dot(n, t, 0)
                dot(n, t, 1)
                gated(n, b, 0)
                if more:
                    topk_halves(nxt)
                    topk_pairs(nxt, 1 - b)
                    gates(nxt, 1 - b)
                dot(n, t, 2)
                gated(n, b, 1)
                dot(n, t, 3)
                gated(n, b, 2)
                gated(n, b, 3)

            def peer_part(h, part):
                n, nxt, b = (None, h), (None, h + 1), h % 2
                if part < 4:
                    if part == 3:
                        gated(n, b, 0)
                        gated(n, b, 1)
                    dot(n, 0, part)
                elif part == 4:
                    topk_halves(nxt)
                elif part == 5:
                    topk_pairs(nxt, 1 - b)
                elif part == 6:
                    gated(n, b, 2)
                    gated(n, b, 3)
                elif part == 7:
                    gates(nxt, 1 - b)

            def last_norm(t):
                for j in range(2):
                    at = slice(512 * j, 512 * j + 512)
                    dve.wait_ge(peer_done, t + 1)
                    link(dve.tensor_tensor(tmp_p, bank[4 + 2 * (t % 2) + j][:, :], gt2_2[:, at], ALU.mult))
                    link(dve.tensor_tensor(xr[:, t, at], xr[:, t, at], tmp_p, ALU.add), fin_add if j == 1 else None)
                one = slice(t, t + 1)
                dve.wait_ge(ssq_done, SQ_LAST + t + 1)
                link(dve.tensor_scalar(rms_t[:, one], ssq[:, one], 1.0 / D, EPS, ALU.mult, ALU.add), ms_done)
                inv_root((rms[:, one], rms_t[:, one], ssq[:, one]), (root_done, MS_LAST + t + 1))
                link(dve.scalar_tensor_tensor(out=xr[:, t, :], in0=xr[:, t, :], scalar=rms[:, one], in1=gfin, op0=ALU.mult, op1=ALU.mult), fin_done)

            topk_halves((None, 0))
            topk_pairs((None, 0), 0)
            gates((None, 0), 0)
            for s in range(LEAD):
                attend(s)
            for h in range(H):
                for part in range(PARTS):
                    peer_part(h, part)
                    for s in PLAN[h][part]:
                        attend(s)
            for t in range(1, TT):
                last = t == TT - 1
                with dve.Fori(0, H // 2 - last) as i:
                    for b in range(2):
                        peer_head((i, t * H + b), b, t, True)
                if last:
                    peer_head((None, TT * H - 2), 0, t, True)
                    peer_head((None, TT * H - 1), 1, t, False)
                if t == 1:
                    dve.wait_ge(last_rows_in, 16 * 2)
                last_norm(t - 1)
            last_norm(TT - 1)

        @block.tensor
        def _(pe):
            def project(dst, w, at, rhs, chunks=DC, stationary=None):
                for c in range(chunks):
                    mm = pe.matmul(dst, w[:, c, at], rhs[:, c, :], start=(c == 0), stop=(c == chunks - 1))
                return mm

            def rows_of(dst, xT, t, w, at, chunks=DC):
                for c in range(chunks):
                    mm = pe.matmul(dst, xT[:, c, t * P:(t + 1) * P], w[:, c, at], start=(c == 0), stop=(c == chunks - 1))
                return mm

            def modulation(n, b, vecs):
                for j in range(4):
                    slab_ready(pe, n + j)
                for c in range(DC):
                    for j in range(4):
                        mm = pe.matmul(bank[b][32 * j:32 * j + vecs.stop - vecs.start, :], cvec[:, vecs, c],
                                       slab(n + j)[:, c, :], start=(c == 0), stop=(c == DC - 1))
                mm.then_inc(pe_mod, 1)

            pe.wait_ge(consts, 1)
            pe.wait_ge(cw_in, 16 * 4)
            for cc in range(CC):
                pe.transpose(bank[3][:, 34 * cc:34 * cc + 34], convw_in[0:34, cc * P:(cc + 1) * P], ident[0:34, 0:34])\
                    .then_inc(convw_T, 1)
            pe.wait_ge(silu_c, 1)
            modulation(N_MOD, 0, slice(0, 2))
            for g in range(2 * DC):
                c = g % DC
                if g >= 4:
                    pe.wait_ge(hT_done, g - 3)
                if g == 0:
                    pe.wait_ge(xn_done, CT)
                if g == DC:
                    pe.wait_ge(xn_done, CT + TT)
                for t in range(CT if g < DC else TT):
                    src = cr if g < DC else xr
                    mm = pe.transpose(bank[4 + g % 4][:, t * P:(t + 1) * P], src[:, t, c:D:DC], ident[:, :])
                mm.then_inc(xT_done, 1)
            pe.wait_ge(hT_done, 2 * DC)
            pe.wait_ge(mod_rows, 4)
            pe.wait_ge(convc_done, 1)
            slab_ready(pe, N_GLU)
            slab_ready(pe, N_GLU + 1)
            for cc in range(CC):
                if cc >= 2:
                    pe.wait_ge(u_done, cc - 1)
                at = slice(cc * P, (cc + 1) * P)
                project(bank[2 * (cc % 2)][:, :], slab(N_GLU), at, hT)
                project(bank[2 * (cc % 2) + 1][:, :], slab(N_GLU + 1), at, hT).then_inc(glu_done, 1)

            def conv_mean():
                pe.wait_ge(conv_done, CC)
                for cc in range(CC):
                    mm = pe.matmul(bank[7][:, :], mean_w[:, :], conv[:, cc, :], start=(cc == 0), stop=(cc == CC - 1))
                mm.then_inc(cmean_done, 1)

            def conv_var():
                pe.wait_ge(csq_done, CC)
                for cc in range(CC):
                    mm = pe.matmul(bank[7][:, :], mean_w[:, :], conv_sq[:, cc, :], start=(cc == 0), stop=(cc == CC - 1))
                mm.then_inc(cvar_done, 1)

            for m in range(18):
                if m >= 4:
                    pe.wait_ge(proj_out, m - 3)
                if m in (0, 8, 14):
                    slab_ready(pe, {0: N_K, 8: N_V, 14: N_Q}[m])
                dst = bank[4 + m % 4]
                if m < 4:
                    mm = project(dst[:, :], slab(N_K), slice(m * P, (m + 1) * P), hT)
                elif m < 8:
                    mm = project(dst[:, 0:CTX], slab(N_K), slice((m - 4) * P, (m - 3) * P), hcT)
                elif m < 10:
                    mm = rows_of(dst[:, :], hcT, m - 8, slab(N_V), slice(0, 512))
                elif m < 14:
                    mm = rows_of(dst[:, :], hT, m - 10, slab(N_V), slice(0, 512))
                else:
                    mm = project(dst[:, :], slab(N_Q), slice((m - 14) * P, (m - 13) * P), hT)
                mm.then_inc(proj_done, 1)
                if m == PROJ_JOB:
                    pe.wait_ge(u_done, CC)
                    modulation(N_JOB, 0, slice(0, 1))

            def scores(n):
                h, t = n // TT, n % TT
                if n >= 2:
                    pe.wait_ge(p_done, n - 1)
                at = slice(HD * (h % 2), HD * (h % 2) + HD)
                q = qT[at, h // 2, t * P:(t + 1) * P]
                pe.matmul(bank[n % 2][:, :], q, kT[at, h // 2, :], start=True, stop=True)
                pe.matmul(bank[2 + n % 2][:, 0:CTX], q, kcT[at, h // 2, :], start=True, stop=True).then_inc(s_done, 1)

            def transposes(n):
                pe.wait_ge(pn_done, n + 1)
                if n >= 1:
                    pe.wait_ge(pTa_out, n)
                    pe.wait_ge(pTb_out, n)
                for k in range(KEYS // P):
                    dst = bank[4][:, k * P:(k + 1) * P] if k < 4 else bank[5][:, (k - 4) * P:(k - 3) * P]
                    mm = pe.transpose(dst, prob[n % 3][:, k * P:(k + 1) * P], ident[:, :])
                mm.then_inc(pT_done, 1)

            def weighted(n):
                h, t = n // TT, n % TT
                pe.wait_ge(pTa_out, n + 1)
                pe.wait_ge(pTb_out, n + 1)
                if t == 0 and h >= 2:
                    pe.wait_ge(head_done, h - 1)
                at = slice(h * HD, (h + 1) * HD)
                half = slice(HD * (h % 2), HD * (h % 2) + HD)
                for k in range(KEYS // P):
                    v = vrow[:, k, at] if k < TT else vcrow[:, k - TT, at]
                    mm = pe.matmul(bank[6][half, t * P:(t + 1) * P], v, probT[n % 2][:, k, :], start=(k == 0), stop=(k == KEYS // P - 1))
                mm.then_inc(o_done, 1)

            pe.wait_ge(proj_out, 18)
            pe.wait_ge(mod_rows, 4 + 4)
            for n in range(H * TT + 3):
                if n < H * TT:
                    scores(n)
                if 2 <= n <= H * TT + 1:
                    transposes(n - 2)
                if n >= 3:
                    weighted(n - 3)
                if n == AT_MEAN:
                    conv_mean()
                if n == AT_VAR:
                    conv_var()
                if n in AT_JOB:
                    i = 1 + AT_JOB.index(n)
                    if i == 1:
                        pe.wait_ge(cms_done, 1)
                    else:
                        pe.wait_ge(mod_rows, 4 + 4 * i)
                    modulation(N_JOB + 4 * i, 7, slice(0, 1) if i < 2 else slice(2, 3))
            pe.wait_ge(head_done, H)
            pe.wait_ge(convy_done, CC)
            pe.wait_ge(mod_rows, 24)
            for c in range(DC):
                if c == 0:
                    for i in range(4):
                        slab_ready(pe, N_GA + i)
                if c == 4:
                    slab_ready(pe, N_GA + 4)
                    slab_ready(pe, N_GA + 5)
                if c >= 2:
                    pe.wait_ge(mix_done, c - 1)
                b = 4 * (c % 2)
                n = N_GA if c < 4 else N_GA + 4
                at = slice((c % 4) * P, (c % 4) * P + P)
                project(bank[b][:, :], slab(n), at, hT)
                project(bank[b + 1][:, :], slab(n + 1), at, hT)
                project(bank[b + 2][:, :], slab(N_GA + 2), slice(c * P, (c + 1) * P), attT, AC)
                project(bank[b + 3][:, :], slab(N_GA + 3), slice(c * P, (c + 1) * P), conv, CC).then_inc(merge_pe, 1)
            pe.wait_ge(mix_done, DC)
            slab_ready(pe, N_WO)
            slab_ready(pe, N_WO + 1)
            for g in range(2 * TT):
                rows_of(bank[g][:, :], mixT, g // 2, slab(N_WO + g % 2), slice(0, 512)).then_inc(wo_pe, 1)
            def second_T(t, block, h2, banks):
                pe.wait_ge(h2_done, block * TT + t + 1)
                for c in range(DC):
                    mm = pe.transpose(bank[banks[c // 4]][:, (c % 4) * P:(c % 4) * P + P], h2[:, c:D:DC], ident[:, :])
                mm.then_inc(h2T_pe, 1)

            for t in range(TT):
                second_T(t, 0, h2r[:, t, :], (2 * t, 2 * t + 1))
                if t == 0:
                    pe.wait_ge(wr_in, 16 * 10)
                pe.wait_ge(h2T_done, 2 * t + 2)
                rows_of(bank[2 * t][:, 0:NG + NE], h2T, t, wr, slice(0, NG + NE)).then_inc(logit_pe, 1)
            pe.wait_ge(both_done, 1)
            for t in range(TT + 1):
                dst = bank[1][:, t * NE:(t + 1) * NE]
                for k in range(min(t, TT - 1) + 1):
                    mm = pe.matmul(dst, before[:, :] if k == t else ones[:, :], both[:, k, :], start=(k == 0),
                                   stop=(k == min(t, TT - 1)))
            mm.then_inc(rank_pe, 1)
            pe.wait_ge(sk_dma, 16)
            for m in range(4):
                for k in range(4):
                    mm = pe.transpose(bank[SK_BANKS[m]][:, k * P:(k + 1) * P], sk_in[:, 4 * m + k, :], ident[:, :])
                mm.then_inc(skT_pe, 1)

            def block_T(b):
                for c in range(DC):
                    mm = pe.transpose(bank[b][:, c * CAP:(c + 1) * CAP], xblk[b][:, c:D:DC], ident[0:CAP, 0:CAP])
                return mm

            def block_gu(b, n):
                gu = ring[:, n % RING:n % RING + 2, :].rearrange("p g (c f) -> p g c f", c=DC)
                for c in range(DC):
                    for half in range(2):
                        at = slice(CAP * half, CAP * half + CAP)
                        mm = pe.matmul(bank[2 + b][at, :].rearrange("p (g f) -> p g f", g=2), xbT[b][:, c, :],
                                       gu[:, :, c, 256 * half:256 * half + 256], start=(c == 0), stop=(c == DC - 1))
                return mm

            def hidden_T(b):
                for k in range(2):
                    mm = pe.transpose(bank[4 + b][:, k * P:(k + 1) * P], hid[b][:, k:256:2], ident[:, :])
                return mm

            def block_dn(b, n):
                for i in range(4):
                    half, k = i // 2, i % 2
                    for j in range(2):
                        mm = pe.matmul(bank[6 + b][CAP * j:CAP * j + CAP, :], hidT[b][:, k, CAP * half:CAP * half + CAP],
                                       slab(n)[:, half, k, 512 * j:512 * j + 512], start=(i == 0), stop=(i == 3))
                return mm

            def expert(e, b, i):
                n = N_EXP + 3 * b

                def arrived(k):
                    pe.wait_ge(slab_in[(n + k) % RING], i * 16 + 16 * ((n + k) // RING + 1))

                pe.wait_ge(xb_in[b], i * 16 + 16)
                pe.sem_inc(mark, 1)
                block_T(b).then_inc(xbT_done, 1)
                pe.wait_ge(xbT_out, e + 1)
                arrived(0)
                arrived(1)
                block_gu(b, n).then_inc(gu_done, 1)
                pe.wait_ge(hid_done, e + 1)
                hidden_T(b).then_inc(hidT_pe, 1)
                pe.wait_ge(hidT_done, e + 1)
                arrived(2)
                unless_first(pe, yv_done, e - 1)
                block_dn(b, n + 2).then_inc(dn_done, 1)

            pe.wait_ge(route_done, 2)
            pe.wait_ge(skT_done, 5)
            for b in range(2):
                expert(b, b, 0)
            with pe.Fori(1, NE // 2) as i:
                for b in range(2):
                    expert(i * 2 + b, b, i)
            n_over = pe.value_load(over_i[0:1, 0:1], min_val=0, max_val=OVER)
            with pe.Fori(0, OVER) as i:
                with pe.If(i < n_over):
                    pe.wait_ge(ov_xin, i * 16 + 16)
                    pe.sem_inc(mark, 1)
                    block_T(0).then_inc(xbT_done, 1)
                    pe.wait_ge(xbT_out, i + (NE + 1))
                    pe.wait_ge(ov_slab, i * 48 + 48)
                    block_gu(0, N_EXP).then_inc(gu_done, 1)
                    pe.wait_ge(hid_done, i + (NE + 1))
                    hidden_T(0).then_inc(hidT_pe, 1)
                    pe.wait_ge(hidT_done, i + (NE + 1))
                    block_dn(0, N_EXP + 2).then_inc(dn_done, 1)
            def project2(m):
                k = proj_slab(m)
                if m >= PROJ_STICK + 4:
                    pe.wait_ge(proj_out, 18 + m - 3)
                elif PROJ_V <= m < PROJ_STICK:
                    pe.wait_ge(proj_out, 18 + (m - PROJ_V if m < PROJ_V + 6 else m - 6) + 1)
                if m < 2 or m >= PROJ_V and m % AC == 0:
                    slab2_ready(pe, k)
                dst = bank[proj_bank(m)]
                if m < PROJ_V:
                    mm = rows_of(dst[:, :], hT, m // 2, slab2(k), slice(0, 512))
                else:
                    mm = project(dst[:, :], slab2(k), slice((m % AC) * P, (m % AC + 1) * P), hT)
                mm.then_inc(proj_done, 1)

            for n in range(TT + 1):
                if n < TT:
                    pe.wait_ge(xnb_done, n + 1)
                    for c in range(DC):
                        mm = pe.transpose(bank[2 * n + c // 4][:, (c % 4) * P:(c % 4 + 1) * P], xnb[:, n, c:D:DC], ident[:, :])
                        if c % 4 == 3:
                            mm.then_inc(xT_done, 1)
                if n >= 1:
                    pe.wait_ge(hT_done, 2 * DC + n * DC)
                    project2(2 * n - 2)
                    project2(2 * n - 1)
            for m in range(PROJ_V, PROJ_STICK):
                project2(m)
                if m == PROJ_V:
                    pe.wait_ge(wr_in, 16 * 10)
                    pe.wait_ge(proj_out, 18 + PROJ_V)
                    for t in range(TT):
                        mm = rows_of(bank[6][:, t * H:(t + 1) * H], hT, t, wf, slice(0, H))
                    mm.then_inc(f_pe, 1)
                if m == PROJ_V + 3:
                    pe.wait_ge(f_dve, 2)
                    for t in range(TT):
                        at = slice(t * H, (t + 1) * H)
                        for k in range(t):
                            pe.matmul(bank[7][:, at], ones[:, :], flog[:, k, :], start=(k == 0), stop=False)
                        pe.matmul(bank[7][:, at], before[:, :], flog[:, t, :], start=(t == 0), stop=False)
                        mm = pe.matmul(bank[7][:, at], ident[:, :], flog[:, t, :], start=False, stop=True)
                    mm.then_inc(f_pe, 1)
                if m == PROJ_V + 5:
                    pe.wait_ge(f_dve, 3)
                    for t in range(TT):
                        mm = pe.transpose(bank[6][0:H, t * P:(t + 1) * P], fcum[:, t, :], ident[:, :])
                    mm.then_inc(f_pe, 1)
            pe.wait_ge(proj_out, 18 + PROJ_STICK)
            pe.wait_ge(f_act, 2)

            def fox_scores(n):
                h, t, part = unit(n)
                w = (t + 1) * P
                if n >= 3:
                    pe.wait_ge(p_done, H * TT + n - 2)
                at = slice(HD * (h % 2), HD * (h % 2) + HD)
                dst = bank[1 + n % 3]
                pe.matmul(dst[:, 0:w], fqT[at, h // 2, t * P:(t + 1) * P], fkT[at, h // 2, 0:w], start=True, stop=False)
                pe.matmul(dst[:, 0:w], ident[0:H, h:h + 1].broadcast_to([H, P]), fcumT[:, 0:w], start=False, stop=False)
                pe.matmul(dst[:, t * P:w], ident[:, :], causal[:, :], start=False, stop=True).then_inc(s_done, 1)

            def fox_transposes(n):
                h, t, part = unit(n)
                pe.wait_ge(p_done, H * TT + n + 1)
                if n >= 1:
                    pe.wait_ge(pTa_out, H * TT + n)
                for k in range(t + 1):
                    mm = pe.transpose(bank[6][:, k * P:(k + 1) * P], fprob[part][n % 3][:, k * P:(k + 1) * P], ident[:, :])
                mm.then_inc(pT_done, 1)

            def fox_weighted(n):
                h, t, part = unit(n)
                pe.wait_ge(pTa_out, H * TT + n + 1)
                if part == 1 and t == 1 and h >= 1:
                    pe.wait_ge(att_done, 1 + h)
                o = HD * h if part == 0 else HD * (t - 1)
                for k in range(t + 1):
                    mm = pe.matmul(bank[7][:, o:o + HD], fprobT[part][n % 2][:, k * P:(k + 1) * P],
                                   fvr[:, k, h * HD:(h + 1) * HD], start=(k == 0), stop=(k == t))
                mm.then_inc(o_done, 1)

            def fox_step(k, first):
                part = int(first > 0)
                if k == first:
                    pe.wait_ge(sbc_done, UNITS if part else H)
                    pe.wait_ge(sbo_done, 1 + H if part else 1)
                if of_part(k, first):
                    fox_scores(k)
                if of_part(k - FOX_T[part], first):
                    fox_transposes(k - FOX_T[part])
                if of_part(k - FOX_OUT[part], first):
                    fox_weighted(k - FOX_OUT[part])

            def stick_scores(n):
                h, t, part = unit(n)
                before = n - (4 if part else 3)
                if before >= 0:
                    pe.wait_ge(sbc_done, before + 1)
                at = slice(HD * (h % 2), HD * (h % 2) + HD)
                for j in range(t + 1):
                    mm = pe.matmul(stick_bank(n)[:, j * P:(j + 1) * P], skT_[at, h // 2, j * P:(j + 1) * P],
                                   sqT[at, h // 2, t * P:(t + 1) * P], start=True, stop=True)
                mm.then_inc(sbz_pe, 1)

            def stick_sums(n):
                h, t, part = unit(n)
                x, dst = stick_x[part][n % 3], stick_bank(n)
                pe.wait_ge(sbb_done, n + 1)
                for j in range(t + 1):
                    at = slice(j * P, (j + 1) * P)
                    mm = pe.matmul(dst[:, at], later_neg[:, :], x[:, at], start=True, stop=False)
                    for k in range(j + 1, t + 1):
                        mm = pe.matmul(dst[:, at], ones_neg[:, :], x[:, k * P:(k + 1) * P], start=False, stop=(k == t))
                mm = pe.matmul(dst[:, t * P:(t + 1) * P], ident[:, :], stick_neg, start=False, stop=True)
                mm.then_inc(sbr_pe, 1)

            def stick_out(n):
                h, t, part = unit(n)
                y = stick_y[part][n % len(stick_y[part])]
                pe.wait_ge(sbe_done, n + 1)
                if part == 1 and t == 1:
                    pe.wait_ge(sbo_done, 1 + h)
                o = HD * h if part == 0 else HD * (t - 1)
                dst = bank[6][:, o:o + HD]
                for j in range(t + 1):
                    mm = pe.matmul(dst, y[:, j * P:(j + 1) * P], svr[:, j, h * HD:(h + 1) * HD], start=(j == 0), stop=(j == t))
                mm.then_inc(sbo_pe, 1)

            def stick_step(k, first):
                part = int(first > 0)
                if of_part(k, first):
                    stick_scores(k)
                if of_part(k - SUMS[part], first):
                    stick_sums(k - SUMS[part])
                if of_part(k - OUTS[part], first):
                    stick_out(k - OUTS[part])

            for k in range(H + 3):
                stick_step(k, 0)
                if PROJ_STICK + k < PROJS:
                    project2(PROJ_STICK + k)
            pe.wait_ge(proj_out, 18 + PROJS)
            for n in range(H + 3):
                fox_step(n, 0)
            for half in range(2):
                pe.wait_ge(mixed_done, half + 1)
                for k in range(AC):
                    mm = pe.transpose(bank[1 + half][:, k * P:(k + 1) * P], mixed[0][half][:, 0, k * P:(k + 1) * P], ident[:, :])
                mm.then_inc(attT_pe, 1)
            pe.wait_ge(attT_done, 2)
            slab2_ready(pe, S_WO)
            slab2_ready(pe, S_WO + 1)
            for j in range(2):
                rows_of(bank[WO_BANKS[0][j]][:, :], mixT2[0], 0, slab2(S_WO + j), slice(0, 512)).then_inc(wo_pe, 1)
            second_T(0, 1, h2r_2[0], H2T_BANKS[0])

            def query(q):
                slab2_ready(pe, S_WQ + q)
                for k in range(4):
                    mm = project(bank[(1, 2, 3, 6)[q]][:, k * P:(k + 1) * P], slab2(S_WQ + q), slice(k * P, (k + 1) * P), h2T_2[0])
                mm.then_inc(q_pe, 1)

            def query_b(h, halves=(0, 1)):
                w, there, count = wq_b_of(h)
                pe.wait_ge(there, count)
                for half in halves:
                    m = 2 * h + half
                    if m >= 3:
                        pe.wait_ge(q_done, 4 + m - 2)
                    project(bank[1 + m % 3][:, 0:3 * P], w, slice(half * P, (half + 1) * P), h2T_2[1]).then_inc(q_pe, 1)

            def attend(s):
                if s < ST_FOX:
                    if s == 0:
                        pe.wait_ge(q_done, 4)
                    stick_step(H + s, H)
                elif s < ST_NORM:
                    fox_step(H + s - ST_FOX, H)
                elif ST_NORM < s < ST_OUT:
                    for k in range(DC):
                        pe.wait_ge(mixed_done, 2 + k // AC + 1)
                        if k >= 5:
                            pe.wait_ge(attT_done, 2 + k - 4)
                        for t in range(NT[1]):
                            mm = pe.transpose(bank[(1, 2, 3, 6, 7)[k % 5]][:, t * P:(t + 1) * P],
                                              mixed[1][k // AC][:, t, k % AC * P:(k % AC + 1) * P], ident[:, :])
                        mm.then_inc(attT_pe, 1)
                elif ST_OUT <= s < ST_QUERY:
                    t = s - ST_OUT + 1
                    if t == 1:
                        pe.wait_ge(attT_done, 2 + DC)
                        pe.wait_ge(wo_b_in, 32)
                    if t == 3:
                        pe.wait_ge(res_done, 2 * (TT + 1) + 2)
                    if t < TT:
                        for j in range(2):
                            rows_of(bank[WO_BANKS[t][j]][:, :], mixT2[1], t - 1, wo_b[j], slice(0, 512)).then_inc(wo_pe, 1)
                    if t == TT:
                        pe.wait_ge(res_done, 2 * (TT + 2) + 2)
                        second_T(1, 1, h2r_2[1], H2T_BANKS[1])
                    if t == TT + 1:
                        pe.wait_ge(res_done, 2 * (TT + 3) + 2)
                        second_T(2, 1, h2r_2[2], H2T_BANKS[2])
                    if t == TT + 2:
                        pe.wait_ge(h2T_done, 2 * (TT + 1) + 2)
                        second_T(3, 1, h2r_2[3], H2T_BANKS[3])
                elif s >= ST_QUERY:
                    if s == ST_QUERY:
                        pe.wait_ge(h2T_done, 4 * TT)
                    query_b(s - ST_QUERY)

            def peer_scores(n, head):
                pe.wait_ge(qh_done, at_head(n, 1, 1))
                if n[1] > 0:
                    pe.wait_ge(ids_done, at_head(n, 1, 0))
                pe.sem_inc(mark, 1)
                for p in range(2):
                    keys = skT[:, head, p * P:(p + 1) * P] if isinstance(head, int) else \
                        skT[:, bass.ds(head, 1), p * P:(p + 1) * P].rearrange("p a b -> p (a b)")
                    mm = pe.matmul(bank[0][:, p * P:(p + 1) * P], qh[:, p, :], keys, start=True, stop=True)
                mm.then_inc(sc_pe, 1)

            def up_sums(n, t, g):
                at, (per, first) = up_set(n, g)
                pe.wait_ge(diag_done, at_head(n, GROUPS, g + 1))
                pe.wait_ge(up_in[at], at_head(n, per, first))
                for k in range(G4):
                    for j in range(2):
                        mm = pe.matmul(bank[4 + 2 * (t % 2) + j][:, :], diag[:, G4 * g + k, :], up[G4 * at + k][:, 512 * j:512 * j + 512],
                                       start=False, stop=False)
                mm.then_inc(up_free, 1)

            def peer_head(n, t, nxt, query=None):
                if nxt is not None:
                    peer_scores((n[0], n[1] + 1), nxt)
                for g in range(GROUPS):
                    up_sums(n, t, g)
                    if query is not None and g % 2 == 0:
                        query_b(query, (g // 2,))

            def peer_part(h, part):
                if part == 3:
                    peer_scores((None, h + 1), (h + 1) % H)
                elif part in (5, 6):
                    up_sums((None, h), 0, part - 5)
                elif part in (0, 1) and h > 0:
                    up_sums((None, h - 1), 0, 2 + part)

            def edge(t, first):
                for j in range(2):
                    mm = pe.matmul(bank[4 + 2 * (t % 2) + j][:, :], zeros[:, :], zeros[:, :].unsqueeze(1).broadcast_to([P, 4, P]),
                                   start=first, stop=not first)
                return mm

            pe.wait_ge(h2T_done, 2 * (TT + 0) + 2)
            query(0)
            query(1)
            peer_scores((None, 0), 0)
            query(2)
            query(3)
            pe.wait_ge(q_pe, 2)
            pe.sem_inc(up_free, UP_FIRST)
            edge(0, True)
            for s in range(LEAD):
                attend(s)
            for h in range(H):
                for part in range(PARTS):
                    peer_part(h, part)
                    for s in PLAN[h][part]:
                        attend(s)
            for g in (2, 3):
                up_sums((None, H - 1), 0, g)
            edge(0, False).then_inc(peer_done, 1)
            edge(1, True)
            for h in range(H):
                peer_head((None, H + h), 1, (h + 1) % H, h + AHEAD if h + AHEAD < H else None)
            edge(1, False).then_inc(peer_done, 1)
            for t in range(2, TT):
                last = t == TT - 1
                pe.wait_ge(fin_add, t - 1)
                edge(t, True)
                with pe.Fori(0, H // 2 - last) as i:
                    for b in range(2):
                        peer_head((i, t * H + b), t, i * 2 + (b + 1))
                if last:
                    peer_head((None, TT * H - 2), t, H - 1)
                    peer_head((None, TT * H - 1), t, None)
                edge(t, False).then_inc(peer_done, 1)


_INS = ["x", "c", "ctx", "c_ctx", "w_mod", "b_mod", "norm_mix", "w_in", "rpb", "w_att_out", "conv_w", "conv_b",
        "conv_ln_g", "conv_ln_b", "w_conv_out", "w_o", "norm_ffn", "w_router_group", "b_router_group",
        "w_router_expert", "b_router_expert", "w_exp_gate", "w_exp_up", "w_exp_down", "final_norm", "c_2", "w_ada_2",
        "b_ada_2", "g_norm_mix_2", "w_in_2", "b_forget_2", "g_out_fox_2", "g_out_sb_2", "w_out_2", "g_norm_ffn_2",
        "w_query_2", "sub_keys_2", "expert_down_2", "expert_up_2", "g_final_2"]
_FLAT = {"c_ctx", "final_norm", "g_final_2"}


def kernel(**inputs):
    import concourse.bacc as _bacc
    from concourse.bass_utils import run_bass_kernel_spmd as _run

    nc = _bacc.Bacc("TRN2", target_bir_lowering=False, num_devices=1)
    arrays, A = {}, {}
    for name in _INS:
        a = np.ascontiguousarray(inputs[name])
        arrays[f"in_{name}"] = a
        ap = nc.dram_tensor(f"in_{name}", a.shape, F32, kind="ExternalInput").ap()
        A[name] = ap if name in _FLAT else ap[0]
    out = nc.dram_tensor("out_0", (T, D), F32, kind="ExternalOutput").ap()
    build(nc, A, out)
    r = _run(nc, [arrays], core_ids=[0])
    return r.results[0]["out_0"].reshape(1, T, D)
```
